# Optimizing a Trainium2 kernel written in Bass

```python
import jax
import jax.numpy as jnp
from jax import lax
import numpy as np
import math
import jax, jax.numpy as jnp

D_MODEL = 1024
BATCH = 1
SEQ = 512
DEPTH = 1

GRID_W = 64
CTX_LEN = 256
HEAD_DIM = 64
N_Q_HEADS = 8
N_KV_HEADS = 2
Q_PER_KV = N_Q_HEADS // N_KV_HEADS
ATTN_WIDTH = N_Q_HEADS * HEAD_DIM
KV_WIDTH = N_KV_HEADS * HEAD_DIM
WINDOW = 128
BLOCK = 128
ROPE_BASE = 10000.0
ROPE_PAIRS = HEAD_DIM // 4
CONV_WIDTH = D_MODEL // 2
CONV_K = 3
PEER_HEADS = 8
PEER_KEY_DIM = 256
PEER_N_KEYS = 128
PEER_N_EXPERTS = PEER_N_KEYS * PEER_N_KEYS
PEER_TOPK = 16
PEER_CHUNK = 128
N_MOD = 6
EPS = 1e-6
NEG_INF = -1e30

PROJ_SIZES = (ATTN_WIDTH, KV_WIDTH, KV_WIDTH, CONV_WIDTH, CONV_WIDTH, CONV_WIDTH, D_MODEL, D_MODEL)
PROJ_WIDTH = sum(PROJ_SIZES)
PROJ_SPLITS = tuple(int(s) for s in np.cumsum(PROJ_SIZES)[:-1])
KV_START = ATTN_WIDTH
KV_END = ATTN_WIDTH + 2 * KV_WIDTH


def rmsnorm(x, g):
    xf = x.astype(jnp.float32)
    y = xf * lax.rsqrt(jnp.mean(xf * xf, axis=-1, keepdims=True) + EPS)
    return (y * g.astype(jnp.float32)).astype(x.dtype)

def adaln_params(cond, w_mod, b_mod):
    m = jax.nn.silu(cond) @ w_mod + b_mod
    return jnp.split(m, N_MOD, axis=-1)

def axial_rope_tables(length):
    rows = length // GRID_W
    row = jnp.repeat(jnp.arange(rows, dtype=jnp.float32), GRID_W)
    col = jnp.tile(jnp.arange(GRID_W, dtype=jnp.float32), rows)
    inv_freq = ROPE_BASE ** (-jnp.arange(ROPE_PAIRS, dtype=jnp.float32) / ROPE_PAIRS)
    ang_r = row[:, None] * inv_freq
    ang_c = col[:, None] * inv_freq
    return (jnp.cos(ang_r), jnp.sin(ang_r), jnp.cos(ang_c), jnp.sin(ang_c))

def _rotate(xp, cos, sin):
    x1, x2 = jnp.split(xp, 2, axis=-1)
    c = cos[:, None, :]
    s = sin[:, None, :]
    return jnp.concatenate([x1 * c - x2 * s, x1 * s + x2 * c], axis=-1)

def apply_axial_rope(x, tables):
    cos_r, sin_r, cos_c, sin_c = tables
    xr, xc = jnp.split(x.astype(jnp.float32), 2, axis=-1)
    out = jnp.concatenate([_rotate(xr, cos_r, sin_r), _rotate(xc, cos_c, sin_c)], axis=-1)
    return out.astype(x.dtype)

def split_proj(z):
    return jnp.split(z, PROJ_SPLITS, axis=-1)

def windowed_attention(q, k, v, k_ctx, v_ctx, sink):
    B, L = q.shape[0], q.shape[1]
    nb = L // BLOCK
    scale = HEAD_DIM ** -0.5
    qb = q.reshape(B, nb, BLOCK, N_KV_HEADS, Q_PER_KV, HEAD_DIM)
    pad = ((0, 0), (BLOCK, BLOCK), (0, 0), (0, 0))
    kp = jnp.pad(k, pad).reshape(B, nb + 2, BLOCK, N_KV_HEADS, HEAD_DIM)
    vp = jnp.pad(v, pad).reshape(B, nb + 2, BLOCK, N_KV_HEADS, HEAD_DIM)
    kb = jnp.concatenate([kp[:, :-2], kp[:, 1:-1], kp[:, 2:]], axis=2)
    vb = jnp.concatenate([vp[:, :-2], vp[:, 1:-1], vp[:, 2:]], axis=2)
    s_loc = jnp.einsum('bnqhgd,bnkhd->bhgnqk', qb, kb, preferred_element_type=jnp.float32) * scale
    s_ctx = jnp.einsum('bnqhgd,bchd->bhgnqc', qb, k_ctx, preferred_element_type=jnp.float32) * scale
    blk = jnp.arange(nb)[:, None]
    qpos = blk * BLOCK + jnp.arange(BLOCK)[None, :]
    kpos = (blk - 1) * BLOCK + jnp.arange(3 * BLOCK)[None, :]
    valid = ((kpos[:, None, :] >= 0) & (kpos[:, None, :] < L)
             & (jnp.abs(qpos[:, :, None] - kpos[:, None, :]) <= WINDOW))
    s_loc = jnp.where(valid, s_loc, NEG_INF)
    sink_l = jnp.broadcast_to(
        sink.astype(jnp.float32).reshape(N_KV_HEADS, Q_PER_KV)[None, :, :, None, None, None],
        s_loc.shape[:-1] + (1,))
    p = jax.nn.softmax(jnp.concatenate([s_loc, s_ctx, sink_l], axis=-1), axis=-1)
    n_loc = 3 * BLOCK
    n_ctx = k_ctx.shape[1]
    p_loc = p[..., :n_loc].astype(v.dtype)
    p_ctx = p[..., n_loc:n_loc + n_ctx].astype(v.dtype)
    out = (jnp.einsum('bhgnqk,bnkhd->bnqhgd', p_loc, vb)
           + jnp.einsum('bhgnqc,bchd->bnqhgd', p_ctx, v_ctx))
    return out.reshape(B, L, ATTN_WIDTH)

def context_attention(q, k, v, sink):
    B, C = q.shape[0], q.shape[1]
    qg = q.reshape(B, C, N_KV_HEADS, Q_PER_KV, HEAD_DIM)
    s = jnp.einsum('bqhgd,bkhd->bhgqk', qg, k, preferred_element_type=jnp.float32) * HEAD_DIM ** -0.5
    sink_l = jnp.broadcast_to(
        sink.astype(jnp.float32).reshape(N_KV_HEADS, Q_PER_KV)[None, :, :, None, None],
        s.shape[:-1] + (1,))
    p = jax.nn.softmax(jnp.concatenate([s, sink_l], axis=-1), axis=-1)[..., :C].astype(v.dtype)
    out = jnp.einsum('bhgqk,bkhd->bqhgd', p, v)
    return out.reshape(B, C, ATTN_WIDTH)

def short_conv(z, w):
    L = z.shape[1]
    zp = jnp.pad(z, ((0, 0), (1, 1), (0, 0)))
    return zp[:, :L] * w[0] + zp[:, 1:L + 1] * w[1] + zp[:, 2:] * w[2]

def conv_branch(gate_b, gate_c, u, conv_w, w_conv_out):
    return (gate_b * short_conv(gate_c * u, conv_w)) @ w_conv_out

def merge_branches(y_attn, y_conv, ga, gc, w_mix_out):
    return (jax.nn.sigmoid(ga) * y_attn + jax.nn.sigmoid(gc) * y_conv) @ w_mix_out

def peer(h, w_q, sub_keys, u_tab, v_tab):
    B, L, D = h.shape
    tok = h.reshape(-1, PEER_CHUNK, D)

    def chunk(t):
        T = t.shape[0]
        qh = (t @ w_q).reshape(T, PEER_HEADS, 2, PEER_KEY_DIM // 2)
        s = jnp.einsum('thpd,hpnd->thpn', qh, sub_keys, preferred_element_type=jnp.float32)
        s_top, i_top = lax.top_k(s, PEER_TOPK)
        cand = s_top[:, :, 0, :, None] + s_top[:, :, 1, None, :]
        cand_idx = i_top[:, :, 0, :, None] * PEER_N_KEYS + i_top[:, :, 1, None, :]
        best, pos = lax.top_k(cand.reshape(T, PEER_HEADS, PEER_TOPK * PEER_TOPK), PEER_TOPK)
        idx = jnp.take_along_axis(cand_idx.reshape(T, PEER_HEADS, PEER_TOPK * PEER_TOPK), pos, axis=-1)
        g = jax.nn.softmax(best, axis=-1)
        ue = jnp.take(u_tab, idx, axis=0)
        ve = jnp.take(v_tab, idx, axis=0)
        act = jax.nn.gelu(jnp.einsum('thkd,td->thk', ue, t, preferred_element_type=jnp.float32),
                          approximate=False)
        return jnp.einsum('thk,thkd->td', (g * act).astype(t.dtype), ve)

    return lax.map(chunk, tok).reshape(B, L, D)

def trunk_layer(x, xc, c, c_ctx, w_mod, b_mod, n1, n2, w_in, sink, conv_w,
                w_attn_out, w_conv_out, w_mix_out, pw_q, p_keys, p_u, p_v, rope, update_ctx):
    B, L, _ = x.shape
    C = xc.shape[1]
    sh1, sc1, g1, sh2, sc2, g2 = [m[:, None, :] for m in adaln_params(c, w_mod, b_mod)]
    csh1, csc1, cg1, csh2, csc2, cg2 = adaln_params(c_ctx, w_mod, b_mod)

    hc = rmsnorm(xc, n1) * (1 + csc1) + csh1
    if update_ctx:
        qc, kc, vc, gbc, gcc, uc, gac, gvc = split_proj(hc @ w_in)
    else:
        kc, vc = jnp.split(hc @ w_in[:, KV_START:KV_END], 2, axis=-1)
    kc = kc.reshape(B, C, N_KV_HEADS, HEAD_DIM)
    vc = vc.reshape(B, C, N_KV_HEADS, HEAD_DIM)

    h = rmsnorm(x, n1) * (1 + sc1) + sh1
    q, k, v, gb, gcv, u, ga, gv = split_proj(h @ w_in)
    q = apply_axial_rope(q.reshape(B, L, N_Q_HEADS, HEAD_DIM), rope)
    k = apply_axial_rope(k.reshape(B, L, N_KV_HEADS, HEAD_DIM), rope)
    v = v.reshape(B, L, N_KV_HEADS, HEAD_DIM)
    y_attn = windowed_attention(q, k, v, kc, vc, sink) @ w_attn_out
    y_conv = conv_branch(gb, gcv, u, conv_w, w_conv_out)
    x = x + g1 * merge_branches(y_attn, y_conv, ga, gv, w_mix_out)
    h2 = rmsnorm(x, n2) * (1 + sc2) + sh2
    x = x + g2 * peer(h2, pw_q, p_keys, p_u, p_v)

    if update_ctx:
        yc_attn = context_attention(qc.reshape(B, C, N_Q_HEADS, HEAD_DIM), kc, vc, sink) @ w_attn_out
        yc_conv = conv_branch(gbc, gcc, uc, conv_w, w_conv_out)
        xc = xc + cg1 * merge_branches(yc_attn, yc_conv, gac, gvc, w_mix_out)
        hc2 = rmsnorm(xc, n2) * (1 + csc2) + csh2
        xc = xc + cg2 * peer(hc2, pw_q, p_keys, p_u, p_v)
    return x, xc

def first_inputs(seed: int = 0) -> dict:
    key = jax.random.key(seed)
    ks = jax.random.split(key, 19)

    def nrm(k, shape, s):
        return jax.random.normal(k, shape, jnp.float32) * s

    return {
        "x": nrm(ks[0], (BATCH, SEQ, D_MODEL), 1.0),
        "c": nrm(ks[1], (BATCH, D_MODEL), 1.0),
        "ctx": nrm(ks[2], (BATCH, CTX_LEN, D_MODEL), 1.0),
        "c_ctx": nrm(ks[3], (D_MODEL,), 1.0),
        "w_mod": nrm(ks[4], (DEPTH, D_MODEL, N_MOD * D_MODEL), D_MODEL ** -0.5),
        "b_mod": nrm(ks[5], (DEPTH, N_MOD * D_MODEL), 0.02),
        "norm1_g": 1.0 + nrm(ks[6], (DEPTH, D_MODEL), 0.02),
        "norm2_g": 1.0 + nrm(ks[7], (DEPTH, D_MODEL), 0.02),
        "w_in": nrm(ks[8], (DEPTH, D_MODEL, PROJ_WIDTH), D_MODEL ** -0.5),
        "attn_sink": nrm(ks[9], (DEPTH, N_Q_HEADS), 1.0),
        "conv_w": nrm(ks[10], (DEPTH, CONV_K, CONV_WIDTH), CONV_K ** -0.5),
        "w_attn_out": nrm(ks[11], (DEPTH, ATTN_WIDTH, D_MODEL), ATTN_WIDTH ** -0.5),
        "w_conv_out": nrm(ks[12], (DEPTH, CONV_WIDTH, D_MODEL), CONV_WIDTH ** -0.5),
        "w_mix_out": nrm(ks[13], (DEPTH, D_MODEL, D_MODEL), D_MODEL ** -0.5),
        "peer_w_q": nrm(ks[14], (DEPTH, D_MODEL, PEER_HEADS * PEER_KEY_DIM), D_MODEL ** -0.5),
        "peer_sub_keys": nrm(ks[15], (DEPTH, PEER_HEADS, 2, PEER_N_KEYS, PEER_KEY_DIM // 2),
                             (PEER_KEY_DIM // 2) ** -0.5),
        "peer_u": nrm(ks[16], (DEPTH, PEER_N_EXPERTS, D_MODEL), D_MODEL ** -0.5),
        "peer_v": nrm(ks[17], (DEPTH, PEER_N_EXPERTS, D_MODEL), 0.5),
        "final_g": 1.0 + nrm(ks[18], (D_MODEL,), 0.02),
    }

def first_block(x, c, ctx, c_ctx, w_mod, b_mod, norm1_g, norm2_g, w_in, attn_sink, conv_w,
              w_attn_out, w_conv_out, w_mix_out, peer_w_q, peer_sub_keys, peer_u, peer_v, final_g):
    rope = axial_rope_tables(x.shape[1])
    xc = ctx
    for l in range(DEPTH):
        x, xc = trunk_layer(x, xc, c, c_ctx, w_mod[l], b_mod[l], norm1_g[l], norm2_g[l], w_in[l],
                            attn_sink[l], conv_w[l], w_attn_out[l], w_conv_out[l], w_mix_out[l],
                            peer_w_q[l], peer_sub_keys[l], peer_u[l], peer_v[l], rope,
                            l < DEPTH - 1)
    return rmsnorm(x, final_g)


DEPTH_2 = 2

CHUNK = 64
N_MIXERS = 2
MLSTM_HEADS = 4
MLSTM_DK = 128
MLSTM_DV = 256
CONV_W = 4
POOL_WINDOWS = (2, 4, 8, 16)
POOL_GROUPS = 4
POOL_GW = D_MODEL // POOL_GROUPS
MEM_LEN = 256
XATTN_HEADS = 4
XATTN_HD = D_MODEL // XATTN_HEADS
D_FF = 4 * D_MODEL
N_A = (DEPTH_2 + 1) // 2
N_B = DEPTH_2 // 2
ALPHA = (2 * DEPTH_2) ** 0.25
BETA = (8 * DEPTH_2) ** -0.25
LN_EPS = 1e-5


def layer_norm(x, g, b):
    xf = x.astype(jnp.float32)
    mu = jnp.mean(xf, axis=-1, keepdims=True)
    var = jnp.mean(jnp.square(xf - mu), axis=-1, keepdims=True)
    y = (xf - mu) * lax.rsqrt(var + LN_EPS) * g.astype(jnp.float32) + b.astype(jnp.float32)
    return y.astype(x.dtype)

def causal_dwconv(u, w):
    S = u.shape[1]
    up = jnp.pad(u, ((0, 0), (CONV_W - 1, 0), (0, 0)))
    acc = up[:, 0:S] * w[0]
    for j in range(1, CONV_W):
        acc = acc + up[:, j:j + S] * w[j]
    return acc

def mlstm_chunk_step(carry, inp):
    C, n, m = carry
    q, k, v, ig, lf = inp
    L = q.shape[2]
    b = jnp.cumsum(lf, axis=-1)
    tril = jnp.tril(jnp.ones((L, L), dtype=bool))
    dmat = jnp.where(tril, b[..., :, None] - b[..., None, :] + ig[..., None, :], -jnp.inf)
    inter = b + m[..., None]
    m_t = jnp.maximum(inter, jnp.max(dmat, axis=-1))
    wts = jnp.exp(dmat - m_t[..., None])
    sc = jnp.einsum('bhtd,bhsd->bhts', q, k) * wts
    a_t = jnp.exp(inter - m_t)
    num = jnp.einsum('bhts,bhsv->bhtv', sc, v) + a_t[..., None] * jnp.einsum('bhtd,bhdv->bhtv', q, C)
    den = jnp.sum(sc, axis=-1) + a_t * jnp.einsum('bhtd,bhd->bht', q, n)
    h = num / jnp.maximum(jnp.abs(den), jnp.exp(-m_t))[..., None]
    b_last = b[..., -1]
    g = b_last[..., None] - b + ig
    m_new = jnp.maximum(b_last + m, jnp.max(g, axis=-1))
    decay = jnp.exp(b_last + m - m_new)
    wk = jnp.exp(g - m_new[..., None])
    C_new = decay[..., None, None] * C + jnp.einsum('bhs,bhsd,bhsv->bhdv', wk, k, v)
    n_new = decay[..., None] * n + jnp.einsum('bhs,bhsd->bhd', wk, k)
    return (C_new, n_new, m_new), h

def mlstm_mixer(x, w_in, gate_b, conv_w, norm_g, w_out):
    B, S, _ = x.shape
    H, DK, DV, L = MLSTM_HEADS, MLSTM_DK, MLSTM_DV, CHUNK
    NC = S // L
    nqk, nv = 2 * H * DK, H * DV
    proj = x @ w_in
    qk = jax.nn.silu(causal_dwconv(proj[..., :nqk], conv_w))
    v = proj[..., nqk:nqk + nv]
    o = proj[..., nqk + nv:nqk + nv + D_MODEL]
    gates = proj[..., nqk + nv + D_MODEL:].astype(jnp.float32) + gate_b.astype(jnp.float32)
    i_pre = gates[..., :H]
    log_f = jax.nn.log_sigmoid(gates[..., H:])

    def to_chunks(t, d):
        return t.astype(jnp.float32).reshape(B, NC, L, H, d).transpose(1, 0, 3, 2, 4)

    q = to_chunks(qk[..., :H * DK], DK) * (DK ** -0.5)
    k = to_chunks(qk[..., H * DK:], DK)
    vc = to_chunks(v, DV)
    ic = i_pre.reshape(B, NC, L, H).transpose(1, 0, 3, 2)
    fc = log_f.reshape(B, NC, L, H).transpose(1, 0, 3, 2)
    init = (jnp.zeros((B, H, DK, DV), jnp.float32),
            jnp.zeros((B, H, DK), jnp.float32),
            jnp.zeros((B, H), jnp.float32))
    _, h = lax.scan(mlstm_chunk_step, init, (q, k, vc, ic, fc))
    h = h.transpose(1, 0, 3, 2, 4).reshape(B, S, H, DV)
    h = h * lax.rsqrt(jnp.mean(jnp.square(h), axis=-1, keepdims=True) + LN_EPS)
    h = h.reshape(B, S, H * DV) * norm_g.astype(jnp.float32)
    y = (jax.nn.sigmoid(o.astype(jnp.float32)) * h).astype(x.dtype)
    return y @ w_out

def pool_mixer(x, w_grp, scale):
    B, S, D = x.shape
    xg = x.astype(jnp.float32).reshape(B, S, POOL_GROUPS, POOL_GW)
    cs = jnp.cumsum(xg, axis=1)
    t1 = (jnp.arange(S) + 1).astype(jnp.float32)
    pooled = []
    for j, w in enumerate(POOL_WINDOWS):
        c = cs[:, :, j]
        lo = jnp.concatenate([jnp.zeros((B, w, POOL_GW), jnp.float32), c[:, :S - w]], axis=1)
        cnt = jnp.minimum(t1, float(w))[None, :, None]
        pooled.append((c - lo) / cnt)
    pooled = jnp.stack(pooled, axis=2)
    diff = pooled - xg
    y = jnp.einsum('bsgc,gcd->bsgd', diff, w_grp.astype(jnp.float32)).reshape(B, S, D)
    return (y * scale.astype(jnp.float32)).astype(x.dtype)

def memory_cross_attn(x, mem_k, mem_v, wq, wo):
    B, S, _ = x.shape
    q = (x @ wq).reshape(B, S, XATTN_HEADS, XATTN_HD).astype(jnp.float32)
    s = jnp.einsum('bshd,bmhd->bhsm', q, mem_k) * (XATTN_HD ** -0.5)
    p = jax.nn.softmax(s, axis=-1)
    o = jnp.einsum('bhsm,bmhd->bshd', p, mem_v).reshape(B, S, D_MODEL).astype(x.dtype)
    return o @ wo

def sq_relu_mlp(x, w1, b1, w2, b2):
    return jnp.square(jax.nn.relu(x @ w1 + b1)) @ w2 + b2

def second_inputs(seed: int = 0) -> dict:
    key = jax.random.key(seed)
    ks = jax.random.split(key, 20)
    H = MLSTM_HEADS
    nqk, nv = 2 * H * MLSTM_DK, H * MLSTM_DV
    p_in = nqk + nv + D_MODEL + 2 * H
    nrm = jax.random.normal
    f_bias = jnp.linspace(3.0, 6.0, H, dtype=jnp.float32)
    gate_b = jnp.concatenate([0.1 * nrm(ks[3], (N_A, H)),
                              f_bias[None, :] + 0.1 * nrm(ks[4], (N_A, H))], axis=-1)
    return {
        "x": nrm(ks[0], (BATCH, SEQ, D_MODEL), jnp.float32),
        "mem": nrm(ks[1], (BATCH, MEM_LEN, D_MODEL), jnp.float32),
        "mlstm_w_in": nrm(ks[2], (N_A, D_MODEL, p_in), jnp.float32) * D_MODEL ** -0.5,
        "mlstm_gate_b": gate_b,
        "mlstm_conv_w": nrm(ks[5], (N_A, CONV_W, nqk), jnp.float32) * CONV_W ** -0.5,
        "mlstm_norm_g": 1.0 + 0.02 * nrm(ks[6], (N_A, nv), jnp.float32),
        "mlstm_w_out": nrm(ks[7], (N_A, nv, D_MODEL), jnp.float32) * (nv ** -0.5) * BETA,
        "pool_w": nrm(ks[8], (N_B, POOL_GROUPS, POOL_GW, POOL_GW), jnp.float32) * (POOL_GW ** -0.5) * BETA,
        "pool_scale": 1.0 + 0.02 * nrm(ks[9], (N_B, D_MODEL), jnp.float32),
        "mem_w_kv": nrm(ks[10], (D_MODEL, 2 * D_MODEL), jnp.float32) * D_MODEL ** -0.5,
        "xattn_wq": nrm(ks[11], (DEPTH_2, D_MODEL, D_MODEL), jnp.float32) * D_MODEL ** -0.5,
        "xattn_wo": nrm(ks[12], (DEPTH_2, D_MODEL, D_MODEL), jnp.float32) * (D_MODEL ** -0.5) * BETA,
        "mlp_w1": nrm(ks[13], (DEPTH_2, D_MODEL, D_FF), jnp.float32) * D_MODEL ** -0.5,
        "mlp_b1": 0.01 * nrm(ks[14], (DEPTH_2, D_FF), jnp.float32),
        "mlp_w2": nrm(ks[15], (DEPTH_2, D_FF, D_MODEL), jnp.float32) * (D_FF ** -0.5) * BETA,
        "mlp_b2": 0.01 * nrm(ks[16], (DEPTH_2, D_MODEL), jnp.float32),
        "ln_g": 1.0 + 0.02 * nrm(ks[17], (DEPTH_2, 3, D_MODEL), jnp.float32),
        "ln_b": 0.02 * nrm(ks[18], (DEPTH_2, 3, D_MODEL), jnp.float32),
    }

def second_block(x, mem, mlstm_w_in, mlstm_gate_b, mlstm_conv_w, mlstm_norm_g, mlstm_w_out,
              pool_w, pool_scale, mem_w_kv, xattn_wq, xattn_wo,
              mlp_w1, mlp_b1, mlp_w2, mlp_b2, ln_g, ln_b):
    B = mem.shape[0]
    kv = (mem @ mem_w_kv).astype(jnp.float32)
    mem_k = kv[..., :D_MODEL].reshape(B, MEM_LEN, XATTN_HEADS, XATTN_HD)
    mem_v = kv[..., D_MODEL:].reshape(B, MEM_LEN, XATTN_HEADS, XATTN_HD)
    for i in range(DEPTH_2):
        j = i // N_MIXERS
        if i % N_MIXERS == 0:
            y = mlstm_mixer(x, mlstm_w_in[j], mlstm_gate_b[j], mlstm_conv_w[j],
                            mlstm_norm_g[j], mlstm_w_out[j])
        else:
            y = pool_mixer(x, pool_w[j], pool_scale[j])
        x = layer_norm(ALPHA * x + y, ln_g[i, 0], ln_b[i, 0])
        x = layer_norm(ALPHA * x + memory_cross_attn(x, mem_k, mem_v, xattn_wq[i], xattn_wo[i]),
                       ln_g[i, 1], ln_b[i, 1])
        x = layer_norm(ALPHA * x + sq_relu_mlp(x, mlp_w1[i], mlp_b1[i], mlp_w2[i], mlp_b2[i]),
                       ln_g[i, 2], ln_b[i, 2])
    return x


def setup_inputs(seed=0):
    out = dict(first_inputs(seed))
    for name, value in second_inputs(seed + 1).items():
        if name != "x":
            out[name + "_2"] = value
    return out


def reference(
    x, c, ctx, c_ctx, w_mod, b_mod, norm1_g, norm2_g, w_in, attn_sink, conv_w, w_attn_out,
    w_conv_out, w_mix_out, peer_w_q, peer_sub_keys, peer_u, peer_v, final_g, mem_2,
    mlstm_w_in_2, mlstm_gate_b_2, mlstm_conv_w_2, mlstm_norm_g_2, mlstm_w_out_2, pool_w_2,
    pool_scale_2, mem_w_kv_2, xattn_wq_2, xattn_wo_2, mlp_w1_2, mlp_b1_2, mlp_w2_2, mlp_b2_2,
    ln_g_2, ln_b_2,
):
    x = first_block(
        x, c, ctx, c_ctx, w_mod, b_mod, norm1_g, norm2_g, w_in, attn_sink, conv_w, w_attn_out,
        w_conv_out, w_mix_out, peer_w_q, peer_sub_keys, peer_u, peer_v, final_g,
    )
    return second_block(
        x, mem_2, mlstm_w_in_2, mlstm_gate_b_2, mlstm_conv_w_2, mlstm_norm_g_2, mlstm_w_out_2,
        pool_w_2, pool_scale_2, mem_w_kv_2, xattn_wq_2, xattn_wo_2, mlp_w1_2, mlp_b1_2,
        mlp_w2_2, mlp_b2_2, ln_g_2, ln_b_2,
    )


_drawn_inputs = setup_inputs


def setup_inputs(seed=0):
    import zlib

    import numpy as np

    out = dict(_drawn_inputs(seed))
    spreads = {}
    factors = {'attn_sink': 8.0,
     'final_g': 2.722,
     'mlstm_norm_g_2': 137.648,
     'pool_scale_2': 62.54,
     'mlp_b1_2': 8.0,
     'mlp_b2_2': 6.344}
    for name, (base, spread) in spreads.items():
        noise = np.random.default_rng([zlib.crc32(name.encode()), seed]).standard_normal(out[name].shape)
        drawn = base * np.exp(spread * noise) if base else spread * noise
        out[name] = jnp.asarray(drawn.astype(out[name].dtype))
    for name, factor in factors.items():
        out[name] = (out[name] * factor).astype(out[name].dtype)
    return out
```

```python
from contextlib import ExitStack

import concourse.bass as bass
from concourse import mybir
import numpy as np

ALU = mybir.AluOpType
ACT = mybir.ActivationFunctionType
AX = mybir.AxisListType
F32 = mybir.dt.float32
F32R = mybir.dt.float32r
U32 = mybir.dt.uint32

P = 128
D = 1024
KB = D // P
T = 512
TT = T // P
CT = 256
EPS = 1e-6
LN_EPS = 1e-5
ALPHA = (2 * 2) ** 0.25
RING = 4
ROPE_BASE = 10000.0
GRID_W = 64
PAIRS = 16
TOPK = 16
HP = 16
KEYS = 128
TB = 32
TBS = T // TB
FF = 4096
WINDOWS = (2, 4, 8, 16)
NEG = -1e30
ARENA = 13320
LOWEST = -3e38

_VEC = {}
_at = 0
for _name, _n in (("b_mod", 48), ("n1", 8), ("n2", 8), ("final", 8), ("conv", 12), ("mconv", 32), ("mnorm", 8),
                  ("gate_b", 1), ("pscale", 8), ("b1", 64), ("b2", 16), ("ln_g", 48), ("ln_b", 48), ("sink", 8),
                  ("c", 16)):
    _VEC[_name] = (_at, _n)
    _at += _n
NVEC = _at
_CONST = {}
_at = 0
for _name, _n in (("ident", P), ("ones", P), ("perm", P), ("iota", P), ("utri", P), ("band", 3 * P), ("cos", T),
                  ("sin", T), ("cnt", 4 * 16)):
    _CONST[_name] = (_at, _n)
    _at += _n
NCONST = _at


def plan():
    sections = {}
    n = 0
    done = []
    early = 0

    def tile(outs):
        nonlocal n, early
        for j in range(outs):
            if j + 1 < outs:
                early += 1
                done.append(("early", early))
            else:
                n += 1
                done.append(("tile", n))

    def section(name, tiles):
        nonlocal early
        sections[name] = (n, len(done))
        for outs in tiles:
            if outs < 0:
                for _ in range(-outs):
                    early += 1
                    done.append(("early", early))
            else:
                tile(outs)

    section("in", [2] + [1] * 4 + [2])
    for i in range(12):
        section(f"conv{i}", [1] + [-1] * (i >= 2) + [-1] * (i < 11))
    section("gates", [1, -1] * 16)
    section("tail", [-1] * 6)
    section("branch", [2] * 8)
    section("mix", [1] * 8)
    section("pq", [1] * 16)
    section("pu", [1] * 128)
    section("memk", [1] * 8)
    section("pv", [2] * 128)
    section("memv", [1] * 8)
    section("lstm", [1] * 17)
    section("core", [1, 1, -2] * 4)
    section("lout", [1] * 8)
    for layer in range(2):
        if layer:
            section("pool", [4] * 2)
        section(f"xq{layer}", [1] * 4 + ([-2] + [1] * 2) * 2 + [-2, -2])
        section(f"xo{layer}", [1] * 8)
        section(f"mlp{layer}", [1] * 4 + ([1] * 4 + [2] * 4) * 7 + [2] * 4)
    return sections, done, n


SECTIONS, DONE, NTILES = plan()

SEMAPHORES = (
    "tile_done", "early_done", "bank_free0", "bank_free1", "bank_free2", "bank_free3", "w_loaded0", "w_loaded1",
    "w_loaded2", "w_loaded3", "w_split", "consts_in", "vecs_in", "ctx_in", "mod_in0", "mod_in1", "mod_in2",
    "mod_in3", "x_in", "mod_used", "norm_out", "stored", "gates_stored0", "gates_stored1", "act_stored0",
    "act_stored1", "zeros_set", "w_upper", "values_turned", "values_copied", "summed", "stats_read", "sums_ready", "cond_ready", "split1", "split0",
    "rotated", "swapped", "scores_read", "scores_ready", "probs_ready", "turned_copied", "turned",     "conv_split", "merge_split", "keys_in", "key_scores_copied", "key_scores", "split2", "picks_ready",
    "picks_copied", "picks_turned", "hot_ready", "quad_copied", "quad_done", "gated_split", "mem_split", "split3",
    "rows_ready", "decay_turned", "floor_read", "max_spread", "lstm_weighted", "qk_ready", "lstm_scores",
    "head_rms_read", "decay_copied", "lstm_den", "decay_arg", "floor_spread", "head_squares", "head_rms",
    "lstm_split", "pool_split", "x_scores_read", "x_scores", "x_probs", "x_turned_copied", "x_turned", "split4",
    "split5", "split6", "split7", "split8", "hidden_split", "squared", "inverse_ready", "root_ready", "scaled",
    "affine_done", "mod_ready", "shift_ready", "attn_exp", "conv_in", "best_ready", "best_exp", "act_back0",
    "act_back1", "gate_back0", "gate_back1", "mem_in", "peer_added", "lconv_done", "lraw_zero", "gate_rows",
    "floor_arg", "decay", "head_inverse", "head_root", "pool_added", "x_shift", "x_exp", "mlp_start", "ppad_zero",
    "act_step", "dve_step",
)


def build(nc, a, out):
    ctx = ExitStack()
    with ctx:
        def sb(name, shape, dt=F32):
            return ctx.enter_context(nc.sbuf_tensor(name, shape, dt))

        sems = {name: ctx.enter_context(nc.semaphore(name)) for name in SEMAPHORES}

        def sem(name):
            return sems[name]

        w32 = sb("w32", [P, RING, 1024])
        whi = sb("whi", [P, RING, KB, P], F32R)
        wlo = sb("wlo", [P, RING, KB, P], F32R)
        zeros = sb("zeros", [P, 1])
        xres = sb("xres", [P, KB, T])
        xhi = sb("xhi", [P, KB, T], F32R)
        xlo = sb("xlo", [P, KB, T], F32R)
        yhi = sb("yhi", [P, KB, T], F32R)
        ylo = sb("ylo", [P, KB, T], F32R)
        acc = sb("acc", [P, KB, T])
        work = sb("work", [P, 8, T])
        consts = sb("consts", [P, NCONST])
        vecs = sb("vecs", [P, NVEC])
        mod = sb("mod", [P, 48, 2])
        gain = sb("gain", [P, 3, KB])
        arena = sb("arena", [P, ARENA])
        small = sb("small", [P, 72])
        psum = ctx.enter_context(nc.psum_tensor("psum", [P, 8, 512], F32))
        gates_dram = nc.dram_tensor("gates_scratch", (TBS, P, KEYS, TB), F32, kind="Internal").ap()
        act_dram = nc.dram_tensor("act_scratch", (KEYS, P, T), F32, kind="Internal").ap()

        def const(name, rows=P):
            at, n = _CONST[name]
            return consts[0:rows, at:at + n]

        def vec(name, j, rows=P):
            return vecs[0:rows, _VEC[name][0] + j:_VEC[name][0] + j + 1]

        def vecr(name):
            at, n = _VEC[name]
            return vecs[:, at:at + n]

        ident, ones = const("ident"), const("ones")

        def ar(at, n):
            return arena[:, at:at + n]

        def tiles_of(at, *shape):
            n = int(np.prod(shape))
            names = "abc"[:len(shape)]
            sizes = dict(zip(names, shape))
            return ar(at, n).rearrange("p (" + " ".join(names) + ") -> p " + " ".join(names), **sizes)

        mod_w = tiles_of(0, 12, 1024)
        mod_pairs = [ar(0, 2048), ar(2048, 2048)] + [acc[:, 4 * j:4 * j + 4, :].rearrange("p k t -> p (k t)")
                                                     for j in range(2)]
        gv = tiles_of(0, KB, T)
        q_rope = tiles_of(4096, 4, T)
        k_rope = ar(6144, T)
        k_ctx = ar(6656, CT)
        v_tok = tiles_of(6912, TT, P)
        v_ctx = tiles_of(7424, 2, P)
        zpad = tiles_of(7680, 2, T + 2)
        cgate = tiles_of(7680 + 1028, 2, T)
        probs = tiles_of(9732, 2, 640)
        probsT = ar(11012, 640)
        sink8 = small[:, 60:68]
        scores_all = tiles_of(0, TT, HP, KEYS)
        sub_keys = tiles_of(8192, HP, KEYS)
        picks = tiles_of(8192, TT, 3, P)
        picksT = tiles_of(10240, 3, T)
        flat_acc = acc[:, :, :].rearrange("p k t -> p (k t)")
        cand = flat_acc[:, 0:2048]
        look = flat_acc[:, 2048:4096]
        hot = flat_acc[:, 0:2048].rearrange("p (s two n) -> p s two n", s=8, two=2)
        stage = tiles_of(0, 2, KEYS, TB)
        ga_act = tiles_of(0, 2, 4, T)
        ga_gate = tiles_of(4096, 2, 4 * T)
        flat_work = work[:, 2:8, :].rearrange("p k t -> p (k t)")
        top_v = flat_work[:, 0:256]
        top_i = flat_work[:, 256:512]
        top_f = flat_work[:, 512:768]
        best = flat_work[:, 768:896]
        best_pos = flat_work[:, 896:1024]
        best_row = flat_work[:, 1024:1152]
        best_e = flat_work[:, 1536:2048]
        best_sum = flat_work[:, 2048:2056]
        memT = look.rearrange("p (k t) -> p k t", k=KB)
        mem_raw = tiles_of(12288, 2, CT)
        mv = tiles_of(8192, 2, D)
        mk = tiles_of(10240, KB, CT)
        lq, lk = tiles_of(0, 4, T), tiles_of(2048, 4, T)
        lv = tiles_of(4096, TT, D)
        lraw = tiles_of(12288, 2, T + 3)
        lsig = tiles_of(12288, 2, T)
        lp = work[:, 4:8, :]
        arow, irow = work[0:4, 6, :], work[0:4, 7, :]
        frow, mrow = const("cos", 4), const("sin", 4)
        acol = small[:, 44:60]
        xq = tiles_of(0, KB, T)
        xp = tiles_of(4096, TT, CT)
        xpT = tiles_of(5120, 2, T)
        ppad = tiles_of(6144, 2, T + 16)
        pool_y = tiles_of(0, 2, T)

        def unit(u):
            m, g, qt = u // 8, u // 4 % 2, u % 4
            return m, g, qt, max(0, qt - 1), min(TT - 1, qt + 1)

        def bank(b):
            return psum[:, b, :]

        def conv_out(i):
            return SECTIONS[f"conv{i}"][1]

        def mod_product(i):
            return SECTIONS[f"conv{i}"][1] + (1 if i < 2 else 2)

        def mod_tiles(i):
            return range(3 * i, min(3 * i + 3, 32))

        def attn_product(u):
            if u < 10:
                return SECTIONS[f"conv{u + 2}"][1] + 1
            return SECTIONS["gates"][1] + 2 * (u - 10) + 1 if u < 26 else SECTIONS["tail"][1] + u - 26

        def x_value_out(i):
            return SECTIONS[f"xq{i // 4}"][1] + (4, 8, 12, 14)[i % 4] + 1

        def wide(b, n):
            return psum[:, b:b + (n + 511) // 512, :].rearrange("p b n -> p (b n)")[:, 0:n]

        tile_done, early_done = sem("tile_done"), sem("early_done")
        bank_free = [sem(f"bank_free{b}") for b in range(RING)]
        w_loaded = [sem(f"w_loaded{s}") for s in range(RING)]
        w_split = sem("w_split")

        def first_tile(section):
            return SECTIONS[section][0]

        def first_out(section):
            return SECTIONS[section][1]

        def wait_product(eng, o, shift=0):
            kind, count = DONE[o]
            eng.wait_ge(tile_done if kind == "tile" else early_done, count + shift)

        def wait_bank(eng, o, shift=0):
            if o >= RING:
                eng.wait_ge(bank_free[o % RING], o // RING + shift)

        def free(ins, o):
            ins.then_inc(bank_free[o % RING], 1)

        def wait_read(eng, o, shift=0):
            eng.wait_ge(bank_free[o % RING], o // RING + 1 + shift)

        class Steps:

            def __init__(self, eng, name):
                self.eng, self.sem, self.n, self.turn = eng, sem(name), 0, 0

            def __call__(self, ins):
                ins.then_inc(self.sem, 1)
                self.n += 1

            def settle(self):
                self.eng.wait_ge(self.sem, self.turn + self.n)

        block = ctx.enter_context(nc.Block())

        @block.sync
        def _(sp):
            sp.dma_start(consts[:, :], a["consts"]).then_inc(sem("consts_in"), 16)
            sp.dma_start(vecs[:, :], a["vecs"]).then_inc(sem("vecs_in"), 16)
            sp.dma_start(acc[:, :, 0:CT], a["ctxT"].rearrange("(k p) t -> p k t", p=P)).then_inc(sem("ctx_in"), 16)
            sp.dma_start(xres[:, :, :], a["xT"].rearrange("(k p) t -> p k t", p=P)).then_inc(sem("x_in"), 16)
            for g in range(4):
                if g == 3:
                    sp.wait_ge(sem("mod_used"), 4)
                sp.dma_start(mod_w[:, 4 * (g % 3):4 * (g % 3) + 4, :], a["wmod"][4 * g:4 * g + 4]
                             .rearrange("a p n -> p a n")).then_inc(sem(f"mod_in{g}"), 16)
                if g == 0:
                    for s in range(RING):
                        sp.dma_start(w32[:, s, :], a["stream"][s]).then_inc(w_loaded[s], 16)
            whole = NTILES // RING
            with sp.Fori(1, whole) as g:
                for s in range(RING):
                    sp.wait_ge(w_split, g * RING + (s + 1 - RING))
                    sp.dma_start(w32[:, s, :], a["stream"][bass.ds(g * RING + s, 1)].rearrange("a p n -> (a p) n"))\
                        .then_inc(w_loaded[s], 16)
            for n in range(whole * RING, NTILES):
                sp.wait_ge(w_split, n + 1 - RING)
                sp.dma_start(w32[:, n % RING, :], a["stream"][n]).then_inc(w_loaded[n % RING], 16)
            for k in range(KB):
                sp.wait_ge(sem("norm_out"), k + 1)
                sp.dma_start(out[k * P:(k + 1) * P, :], xres[:, k, :]).then_inc(sem("stored"), 16)
            sp.wait_ge(sem("stored"), 16 * KB)
            sp.wait_ge(sem("gates_stored0"), 8 * TBS)
            sp.wait_ge(sem("gates_stored1"), 8 * TBS)
            sp.wait_ge(sem("act_stored0"), 16 * KEYS // 2)
            sp.wait_ge(sem("act_stored1"), 16 * KEYS // 2)

        @block.gpsimd
        def _(pool):
            pool.memset(zeros[:, :], 0.0).then_inc(sem("zeros_set"), 1)
            pool.wait_ge(sem("zeros_set"), 1)

            def split_tile(s, n, nth, reused):
                pool.wait_ge(w_loaded[s], nth * 16)
                if reused:
                    pool.wait_ge(tile_done, n + 1 - RING)
                hi = whi[:, s, :, :].rearrange("p k n -> p (k n)")
                lo = wlo[:, s, :, :].rearrange("p k n -> p (k n)")
                pool.tensor_tensor(hi, w32[:, s, :], zeros[:, :].broadcast_to((P, 1024)), ALU.add).then_inc(sem("w_upper"), 1)
                pool.wait_ge(sem("w_upper"), n + 1)
                pool.tensor_tensor(lo, w32[:, s, :], hi.bitcast(F32), ALU.subtract).then_inc(w_split, 1)

            for s in range(RING):
                split_tile(s, s, 1, False)
            whole = NTILES // RING
            with pool.Fori(1, whole) as g:
                for s in range(RING):
                    split_tile(s, g * RING + s, g + 1, True)
            for n in range(whole * RING, NTILES):
                split_tile(n % RING, n, n // RING + 1, True)

        @block.tensor
        def _(pe):
            def feature_product(dst, s, xh, xl, ks, w0=0, ready=None, last_sem=None):
                for j, k in enumerate(ks):
                    if ready is not None:
                        pe.wait_ge(ready[0], ready[1] + k + 1)
                    hi, lo = whi[:, s, w0 + j, :], wlo[:, s, w0 + j, :]
                    pe.matmul(dst, hi, xh(k), start=(j == 0), stop=False)
                    pe.matmul(dst, hi, xl(k), start=False, stop=False)
                    mm = pe.matmul(dst, lo, xh(k), start=False, stop=(j == len(ks) - 1))
                mm.then_inc(last_sem, 1)

            XH, XL = (lambda k: xhi[:, k, :]), (lambda k: xlo[:, k, :])
            YH, YL = (lambda k: yhi[:, k, :]), (lambda k: ylo[:, k, :])
            CH, CL = (lambda k: yhi[:, k, 0:CT]), (lambda k: ylo[:, k, 0:CT])

            def linear(n, o, XH=XH, XL=XL, cols=T, ready=None):
                pe.wait_ge(w_split, n + 1)
                wait_bank(pe, o)
                feature_product(bank(o % RING)[:, 0:cols], n % RING, XH, XL, range(KB), ready=ready,
                                last_sem=tile_done)

            def linear_group(n, outs, ready):
                pe.wait_ge(w_split, n + len(outs))
                for oo in outs:
                    wait_bank(pe, oo)
                for k in range(KB):
                    pe.wait_ge(ready[0], ready[1] + k + 1)
                    for m, oo in enumerate(outs):
                        dst, s = bank(oo % RING), (n + m) % RING
                        pe.matmul(dst, whi[:, s, k, :], XH(k), start=(k == 0), stop=False)
                        pe.matmul(dst, whi[:, s, k, :], XL(k), start=False, stop=False)
                        mm = pe.matmul(dst, wlo[:, s, k, :], XH(k), start=False, stop=(k == KB - 1))
                        if k == KB - 1:
                            mm.then_inc(tile_done, 1)

            def norm_sums(ni, cols=T, mean=False):
                pe.wait_ge(sem("summed"), 8 * (ni + 1))
                if ni:
                    pe.wait_ge(sem("stats_read"), ni)
                if mean:
                    pe.matmul(bank(4)[:, 0:cols], ones, work[:, 4, 0:cols], start=True, stop=True)
                pe.matmul(bank(5)[:, 0:cols], ones, work[:, 5, 0:cols], start=True, stop=True)\
                    .then_inc(sem("sums_ready"), 1)

            cond = small[:, 0:16].rearrange("p (k two) -> p k two", two=2)
            pe.wait_ge(sem("consts_in"), 16)
            norm_sums(0, CT)
            pe.wait_ge(sem("cond_ready"), 1)

            def mod_product_of(dst, w, signal):
                w = w.rearrange("p (k n) -> p k n", k=KB)
                for k in range(KB):
                    mm = pe.matmul(dst, w[:, k, :], cond[:, k, :], start=(k == 0), stop=(k == KB - 1))
                mm.then_inc(signal, 1)

            for t in range(16):
                if t % 4 == 0:
                    pe.wait_ge(sem(f"mod_in{t // 4}"), 16)
                mod_product_of(bank(6)[:, 2 * t:2 * t + 2], mod_w[:, t % 12, :], sem("mod_used"))
            norm_sums(1)

            n, o = SECTIONS["in"]
            NX, NC = (sem("split1"), 0), (sem("split0"), 0)

            def both(n, o, product_x, product_c):
                pe.wait_ge(w_split, n + 1)
                wait_bank(pe, o)
                product_c(bank(o % RING)[:, 0:CT], early_done)
                wait_bank(pe, o + 1)
                product_x(bank((o + 1) % RING), tile_done)

            pe.wait_ge(w_split, n + 1)
            feature_product(bank(o % RING)[:, 0:CT], n % RING, CH, CL, range(KB), ready=NC, last_sem=early_done)
            linear_group(n, [o + 1, o + 2, o + 3], NX)

            def rotate(i):
                wait_read(pe, SECTIONS["in"][1] + 1 + i)
                if i:
                    pe.wait_ge(sem("rotated"), i)
                pe.matmul(bank(6), const("perm"), work[:, i % 2, :], start=True, stop=True)\
                    .then_inc(sem("swapped"), 1)

            rotate(0)
            linear(n + 3, o + 4)
            rotate(1)
            linear(n + 4, o + 5)
            rotate(2)
            both(n + 5, o + 6, lambda d, m: feature_product(d, (n + 5) % RING, XH, XL, range(KB), last_sem=m),
                 lambda d, m: feature_product(d, (n + 5) % RING, CH, CL, range(KB), last_sem=m))
            rotate(3)
            rotate(4)

            def turn_values(src, tiles, dst):
                for t in range(tiles):
                    mm = pe.transpose(dst[:, t * P:(t + 1) * P], src[:, t * P:(t + 1) * P], ident)
                mm.then_inc(sem("values_turned"), 1)

            wait_read(pe, o + 6)
            turn_values(work[:, 1, :], CT // P, bank(7))
            wait_read(pe, o + 7)
            pe.wait_ge(sem("values_copied"), 1)
            turn_values(work[:, 0, :], TT, bank(7))

            def attn_scores(u):
                m, g, qt, lo, hi = unit(u)
                rows = slice(64 * g, 64 * g + 64)
                if u:
                    pe.wait_ge(sem("scores_read"), u)
                qs = q_rope[rows, m, qt * P:(qt + 1) * P]
                for j, kt in enumerate(range(lo, hi + 1)):
                    pe.matmul(wide(4, 640)[:, j * P:(j + 1) * P], qs, k_rope[rows, kt * P:(kt + 1) * P],
                              start=True, stop=True)
                nl = hi - lo + 1
                for j in range(2):
                    c = (nl + j) * P
                    mm = pe.matmul(wide(4, 640)[:, c:c + P], qs, k_ctx[rows, j * P:(j + 1) * P], start=True, stop=True)
                mm.then_inc(sem("scores_ready"), 1)

            def attn_turn(u):
                m, g, qt, lo, hi = unit(u)
                nk = hi - lo + 3
                pe.wait_ge(sem("probs_ready"), u + 1)
                if u:
                    pe.wait_ge(sem("turned_copied"), u)
                for j in range(nk):
                    mm = pe.transpose(wide(6, 640)[:, j * P:(j + 1) * P], probs[:, u % 2, j * P:(j + 1) * P], ident)
                mm.then_inc(sem("turned"), 1)

            def attn_values(u):
                m, g, qt, lo, hi = unit(u)
                rows = slice(64 * g, 64 * g + 64)
                pe.wait_ge(sem("turned_copied"), u + 1)
                o = attn_product(u)
                wait_bank(pe, o)
                for j, kt in enumerate(list(range(lo, hi + 1)) + [0, 1]):
                    vs = (v_tok[:, kt, 64 * g:64 * g + 64] if j < hi - lo + 1 else v_ctx[:, kt, 64 * g:64 * g + 64])
                    mm = pe.matmul(psum[rows, o % RING, 0:P], vs, probsT[:, j * P:(j + 1) * P],
                                   start=(j == 0), stop=(j == hi - lo + 2))
                mm.then_inc(early_done, 1)

            def attn_slot(i):
                if i < 32:
                    if i == 0:
                        pe.wait_ge(sem("rotated"), 5)
                        wait_read(pe, SECTIONS["in"][1])
                        pe.wait_ge(sem("values_copied"), 2)
                    attn_scores(i)
                if 1 <= i <= 32:
                    attn_turn(i - 1)
                if 2 <= i <= 33:
                    attn_values(i - 2)

            for i in range(12):
                linear(SECTIONS[f"conv{i}"][0], conv_out(i))
                attn_slot(i)
                if i < 11:
                    wait_bank(pe, mod_product(i))
                    for j, t in enumerate(mod_tiles(i)):
                        pe.wait_ge(sem(f"mod_in{t // 2 % 4}"), 32 + 16 * (t // 8))
                        mod_product_of(bank(mod_product(i) % RING)[:, 2 * j:2 * j + 2],
                                       mod_pairs[t // 2 % 4][:, 1024 * (t % 2):1024 * (t % 2) + 1024],
                                       sem("mod_used") if t != mod_tiles(i)[-1] else early_done)
            n, o = SECTIONS["gates"]
            for i in range(16):
                linear(n + i, o + 2 * i)
                attn_slot(12 + i)
            for i in range(28, 34):
                attn_slot(i)
            n, o = SECTIONS["branch"]
            for u in range(28, 32):
                wait_read(pe, attn_product(u))
            pe.wait_ge(sem("conv_split"), 4)
            for m in range(KB):
                pe.wait_ge(w_split, n + m + 1)
                for j, done in ((0, early_done), (1, tile_done)):
                    wait_bank(pe, o + 2 * m + j)
                    feature_product(bank((o + 2 * m + j) % RING), (n + m) % RING, YH, YL, range(4 * j, 4 * j + 4),
                                    w0=4 * j, last_sem=done)
            n, o = SECTIONS["mix"]
            for m in range(KB):
                linear(n + m, o + m, ready=(sem("merge_split"), 0) if m == 0 else None)
            norm_sums(2)

            n, o = SECTIONS["pq"]

            def key_scores(m):
                wait_read(pe, SECTIONS["pq"][1] + m)
                if m == 0:
                    pe.wait_ge(sem("keys_in"), 16)
                if m:
                    pe.wait_ge(sem("key_scores_copied"), m)
                for t in range(TT):
                    mm = pe.matmul(bank(6)[:, t * P:(t + 1) * P], acc[:, m % 2, t * P:(t + 1) * P], sub_keys[:, m, :],
                                   start=True, stop=True)
                mm.then_inc(sem("key_scores"), 1)

            linear_group(n, range(o, o + 4), (sem("split2"), 0))
            for m in range(3):
                key_scores(m)
            for m in range(4, HP):
                linear(n + m, o + m)
                key_scores(m - 1)
            key_scores(HP - 1)

            n, o = SECTIONS["pu"]

            def expert_inputs(g, k, n0, o0):
                pe.wait_ge(w_split, g * RING + (n0 + k + 1))
                wait_bank(pe, o0 + k, g)
                feature_product(bank((o0 + k) % RING), (n0 + k) % RING, XH, XL, range(KB), last_sem=tile_done)

            with pe.Fori(0, 16) as g:
                for k in range(RING):
                    expert_inputs(g, k, n, o)
            for tt in range(TT):
                for j in range(3):
                    pe.wait_ge(sem("picks_ready"), tt + 1)
                    i = 3 * tt + j
                    if i >= 2:
                        pe.wait_ge(sem("picks_copied"), i - 1)
                    pe.transpose(bank(6 + i % 2)[:, 0:P], picks[:, tt, j, :], ident).then_inc(sem("picks_turned"), 1)

            def gate_turn(g, half, first):
                for k in range(RING):
                    t0 = 64 + 4 * half
                    nn, oo = n + t0 + k, o + t0 + k
                    pe.wait_ge(w_split, g * 8 + (nn + 1))
                    wait_bank(pe, oo, g * 2)
                    feature_product(bank(oo % RING), nn % RING, XH, XL, range(KB), last_sem=tile_done)
                    for q in range(2 * k, 2 * k + 2):
                        pe.wait_ge(sem("hot_ready"), g * 16 + (8 * half + q + 1))
                        if not (first and q < 2):
                            pe.wait_ge(sem("quad_copied"), g * 16 + (8 * half + q - 1))
                        for r in range(4):
                            slot = (4 * q + r) % 8
                            mm = pe.matmul(bank(6 + q % 2)[:, r * P:(r + 1) * P], hot[:, slot, 0, :],
                                           hot[:, slot, 1, :], start=True, stop=True)
                        mm.then_inc(sem("quad_done"), 1)

            gate_turn(0, 0, True)
            gate_turn(0, 1, False)
            with pe.Fori(1, 8) as g:
                gate_turn(g, 0, False)
                gate_turn(g, 1, False)

            n, o = SECTIONS["memk"]
            MH, ML = (lambda k: xhi[:, k, 0:CT]), (lambda k: xlo[:, k, 0:CT])
            for m in range(KB):
                linear(n + m, o + m, MH, ML, CT, ready=(sem("mem_split"), 0) if m == 0 else None)

            n, o = SECTIONS["pv"]

            def half_group_out(turn_tiles, turn_outs, n0, o0, half, ready, ready_count):
                for k in range(4):
                    if k == 0:
                        pe.wait_ge(ready, ready_count)
                    pe.wait_ge(w_split, turn_tiles + (n0 + k + 1))
                    for j, done in ((0, early_done), (1, tile_done)):
                        oo = o0 + 2 * k + j
                        wait_bank(pe, oo, turn_outs)
                        feature_product(bank(oo % RING), (n0 + k) % RING, YH, YL, range(4 * half, 4 * half + 4),
                                        w0=4 * j, last_sem=done)

            with pe.Fori(0, 16) as g:
                for half in range(2):
                    half_group_out(g * 8, g * 4, n + 4 * half, o + 8 * half, half, sem("gated_split"),
                                   g * 8 + 4 * (half + 1))

            n, o = SECTIONS["memv"]

            def turn_copied(m, o, src, tiles, turned):
                wait_read(pe, o + m)
                if m >= 2:
                    pe.wait_ge(sem("values_copied"), turned + m - 1)
                turn_values(src[:, m % 2, :], tiles, bank(6 + m % 2))

            for m in range(KB):
                linear(n + m, o + m, MH, ML, CT)
                if m:
                    turn_copied(m - 1, o, mem_raw, CT // P, 2)
                if m == 4:
                    norm_sums(3)
            turn_copied(7, o, mem_raw, CT // P, 2)

            n, o = SECTIONS["lstm"]
            linear_group(n, range(o, o + 4), (sem("split3"), 0))
            pe.wait_ge(sem("values_copied"), 10)
            for m in range(4, 17):
                linear(n + m, o + m)
                if m > 9:
                    turn_copied(m - 10, o + 9, work, TT, 10)
            turn_copied(7, o + 9, work, TT, 10)
            pe.wait_ge(sem("values_copied"), 18)
            pe.wait_ge(sem("rows_ready"), 1)
            for t in range(TT):
                mm = pe.transpose(bank(7)[:, 4 * t:4 * t + 4], arow[:, t * P:(t + 1) * P], const("ident", 4)[:, 0:4])
            mm.then_inc(sem("decay_turned"), 1)
            n, o = SECTIONS["core"]
            for h in range(4):
                pick = const("ident", 4)[:, h:h + 1].broadcast_to((4, P))
                if h:
                    pe.wait_ge(sem("floor_read"), h)
                pe.matmul(bank(4), pick, mrow, start=True, stop=True).then_inc(sem("max_spread"), 1)
                for st in range(TT):
                    i = 4 * h + st
                    if i >= 2:
                        pe.wait_ge(sem("lstm_weighted"), i - 1)
                    if i == 0:
                        pe.wait_ge(sem("qk_ready"), 8)
                    c = slice(st * P, T)
                    pe.matmul(bank(5 + i % 2)[:, c], lk[:, h, st * P:(st + 1) * P], lq[:, h, c],
                              start=True, stop=True).then_inc(sem("lstm_scores"), 1)
                for j in range(2):
                    linear(n + 2 * h + j, o + 4 * h + j)
                pe.wait_ge(sem("lstm_weighted"), 4 * h + 4)
                if h:
                    pe.wait_ge(sem("head_rms_read"), h)
                else:
                    pe.wait_ge(sem("decay_copied"), 1)
                for st in range(TT):
                    c = slice(st * P, T)
                    mm = pe.matmul(bank(7)[:, c], ones, lp[:, st, c], start=(st == 0), stop=(st == TT - 1))
                mm.then_inc(sem("lstm_den"), 1)
                pe.wait_ge(sem("decay_arg"), 4 * h + 4)
                pe.matmul(bank(4), pick, frow, start=True, stop=True).then_inc(sem("floor_spread"), 1)
                for j in range(2):
                    oo = o + 4 * h + 2 + j
                    wait_bank(pe, oo)
                    for st in range(TT):
                        c = slice(st * P, T)
                        f = (2 * h + j) * P
                        mm = pe.matmul(bank(oo % RING)[:, c], lv[:, st, f:f + P], lp[:, st, c],
                                       start=(st == 0), stop=(st == TT - 1))
                    mm.then_inc(early_done, 1)
                pe.wait_ge(sem("head_squares"), 2 * h + 2)
                for j in range(2):
                    mm = pe.matmul(bank(7), ones, work[:, j, :], start=(j == 0), stop=(j == 1))
                mm.then_inc(sem("head_rms"), 1)
            n, o = SECTIONS["lout"]
            for m in range(KB):
                linear(n + m, o + m, YH, YL, ready=(sem("lstm_split"), 0) if m == 0 else None)
            norm_sums(4, mean=True)

            ni = 4
            for layer in range(2):
                if layer:
                    n, o = SECTIONS["pool"]
                    for m in range(KB):
                        if m % 4 == 0:
                            pe.wait_ge(w_split, n + m // 4 + 1)
                        wait_bank(pe, o + m)
                        feature_product(bank((o + m) % RING), (n + m // 4) % RING, YH, YL,
                                        range(2 * (m // 2), 2 * (m // 2) + 2), w0=2 * (m % 4),
                                        ready=(sem("pool_split"), 0),
                                        last_sem=tile_done if m % 4 == 3 else early_done)
                    norm_sums(7, mean=True)
                    ni = 7
                n, o = SECTIONS[f"xq{layer}"]

                def x_scores(h):
                    i = 4 * layer + h
                    wait_read(pe, o + 2 * h + 1 + (0, 0, 2, 4)[h])
                    wait_read(pe, o + 2 * h + (0, 0, 2, 4)[h])
                    if i:
                        pe.wait_ge(sem("x_scores_read"), 4 * i)
                    for t in range(TT):
                        for j in range(2):
                            mm = pe.matmul(wide(4, 1024)[:, t * CT:(t + 1) * CT], xq[:, 2 * h + j, t * P:(t + 1) * P],
                                           mk[:, 2 * h + j, :], start=(j == 0), stop=(j == 1))
                        mm.then_inc(sem("x_scores"), 1)

                def x_turn(h):
                    i = 4 * layer + h
                    for t in range(TT):
                        pe.wait_ge(sem("x_probs"), 4 * i + t + 1)
                        if t == 0 and i:
                            pe.wait_ge(sem("x_turned_copied"), 2 * i)
                        for j in range(2):
                            mm = pe.transpose(bank(6 + j)[:, t * P:(t + 1) * P], xp[:, t % 4, j * P:(j + 1) * P],
                                              ident)
                        mm.then_inc(sem("x_turned"), 1)

                def x_values(h, o):
                    i = 4 * layer + h
                    pe.wait_ge(sem("x_turned_copied"), 2 * i + 2)
                    for j in range(2):
                        wait_bank(pe, o + j)
                        for mt in range(2):
                            f = (2 * h + j) * P
                            mm = pe.matmul(bank((o + j) % RING), mv[:, mt, f:f + P], xpT[:, mt, :],
                                           start=(mt == 0), stop=(mt == 1))
                        mm.then_inc(early_done, 1)

                linear_group(n, range(o, o + 4), (sem(f"split{ni}"), 0))
                for m in range(KB):
                    oo = o + m + (0 if m < 4 else 2 if m < 6 else 4)
                    if m >= 4:
                        linear(n + m, oo)
                    if m % 2:
                        h = m // 2
                        if h:
                            x_turn(h - 1)
                        x_scores(h)
                        if h:
                            x_values(h - 1, o + (4, 8, 12)[h - 1])
                x_turn(3)
                x_values(3, o + 14)
                n, o = SECTIONS[f"xo{layer}"]
                for m in range(KB):
                    if m == 0:
                        for j in range(4):
                            wait_read(pe, x_value_out(4 * layer + 3) - j)
                    linear(n + m, o + m, YH, YL)
                norm_sums(ni + 1, mean=True)
                n, o = SECTIONS[f"mlp{layer}"]
                hidden = sem("hidden_split")

                linear_group(n, range(o, o + 4), (sem(f"split{ni + 1}"), 0))
                def turn(g, half, last):
                    if not last:
                        for k in range(4):
                            nn, oo = n + 4 + 8 * half + k, o + 4 + 12 * half + k
                            pe.wait_ge(w_split, g * 16 + (nn + 1))
                            wait_bank(pe, oo, g * 6)
                            feature_product(bank(oo % RING), nn % RING, XH, XL, range(KB), last_sem=tile_done)
                    if last:
                        half_group_out(0, 0, n + 60, o + 88, half, hidden, 32 * layer + 32)
                    else:
                        half_group_out(g * 16, g * 6, n + 8 + 8 * half, o + 8 + 12 * half, half, hidden,
                                       g * 8 + (32 * layer + 4 * half + 4))

                with pe.Fori(0, 3) as g:
                    turn(g, 0, False)
                    turn(g, 1, False)
                turn(3, 0, False)
                turn(3, 1, True)
                norm_sums(ni + 2, mean=True)

        @block.scalar
        def _(act):
            step = Steps(act, "act_step")

            def squares(ni, src, cols=T, ready=None):
                for k in range(KB):
                    if ready is not None:
                        ready(k)
                    if k >= 2:
                        act.wait_ge(sem("summed"), 8 * ni + k - 1)
                    act.activation(work[:, k % 2, 0:cols], src(k), ACT.Square).then_inc(sem("squared"), 1)

            def root(ni, cols=T):
                act.wait_ge(sem("inverse_ready"), ni + 1)
                act.activation(work[:, 7, 0:cols], work[:, 7, 0:cols], ACT.Sqrt).then_inc(sem("root_ready"), 1)

            def affine(ni, scale, bias, dst, cols=T, last=None, between=None):
                for k in range(KB):
                    act.wait_ge(sem("scaled"), 8 * ni + k + 1)
                    if k >= 2 and dst is None:
                        act.wait_ge(sem(f"split{ni}"), k - 1)
                    to = work[:, k % 2, 0:cols] if dst is None else dst(k)
                    src = work[:, 2 + k % 2, 0:cols]
                    b = 0.0 if bias is None else bias(k)
                    act.activation(to, src, ACT.Identity, scale=scale(k), bias=b)\
                        .then_inc(sem("affine_done") if last is None else last, 1)
                    if between is not None:
                        between(k)

            act.wait_ge(sem("vecs_in"), 16)
            act.activation(small[:, 0:16], vecr("c"), ACT.Silu).then_inc(sem("cond_ready"), 1)
            act.wait_ge(sem("ctx_in"), 16)
            squares(0, lambda k: acc[:, k, 0:CT], CT)
            act.wait_ge(sem("x_in"), 16)
            act.wait_ge(sem("summed"), 8)
            squares(1, lambda k: xres[:, k, :])
            root(0, CT)
            act.wait_ge(sem("mod_ready"), 3)
            affine(0, lambda k: gain[:, 1, k:k + 1], lambda k: mod[:, k, 1:2], None, CT)
            root(1)
            affine(1, lambda k: gain[:, 0, k:k + 1], lambda k: mod[:, k, 0:1], None)

            n, o = SECTIONS["in"]

            def copy_product(dst, o, cols=T, func=ACT.Copy, **more):
                wait_product(act, o)
                free(act.activation(dst, bank(o % RING)[:, 0:cols], func, **more), o)

            def raw(i, o):
                if i == 0:
                    act.wait_ge(sem("split1"), 8)
                if i >= 2:
                    act.wait_ge(sem("rotated"), i - 1)
                copy_product(work[:, i % 2, :], o)

            def load_mod_pair(p):
                act.dma_start(mod_pairs[p % 4].rearrange("p (a n) -> p a n", a=2),
                              a["wmod"][16 + 2 * p:18 + 2 * p].rearrange("a p n -> p a n"))\
                    .then_inc(sem(f"mod_in{p % 4}"), 16)

            act.wait_ge(sem("mod_used"), 16)
            act.wait_ge(sem("scaled"), 8)
            for p in range(4):
                load_mod_pair(p)
            copy_product(k_ctx, o, CT)
            for i in range(5):
                raw(i, o + 1 + i)
            act.wait_ge(sem("rotated"), 4)
            copy_product(work[:, 1, 0:CT], o + 6, CT)
            act.wait_ge(sem("rotated"), 5)
            copy_product(work[:, 0, :], o + 7)
            act.wait_ge(sem("values_turned"), 1)
            act.activation(v_ctx.rearrange("p t n -> p (t n)"), bank(7)[:, 0:CT], ACT.Copy)\
                .then_inc(sem("values_copied"), 1)
            act.wait_ge(sem("values_turned"), 2)
            act.activation(v_tok.rearrange("p t n -> p (t n)"), bank(7), ACT.Copy).then_inc(sem("values_copied"), 1)

            def attn_exp(u):
                m, g, qt, lo, hi = unit(u)
                w = (hi - lo + 3) * P
                act.wait_ge(sem("shift_ready"), u + 1)
                act.activation(probs[:, u % 2, 0:w], probs[:, u % 2, 0:w], ACT.Exp, scale=0.125,
                               bias=small[:, 20 + u % 2:21 + u % 2],
                               accum_out=small[:, 24 + u % 2:25 + u % 2]).then_inc(sem("attn_exp"), 1)
                head = m + 4 * g
                act.activation(small[:, 26 + u % 2:27 + u % 2], vec("sink", head), ACT.Exp,
                               bias=small[:, 20 + u % 2:21 + u % 2]).then_inc(sem("attn_exp"), 1)

            def attn_copy(u):
                m, g, qt, lo, hi = unit(u)
                act.wait_ge(sem("turned"), u + 1)
                if u:
                    wait_product(act, attn_product(u - 1))
                w = (hi - lo + 3) * P
                act.activation(probsT[:, 0:w], wide(6, 640)[:, 0:w], ACT.Copy).then_inc(sem("turned_copied"), 1)

            def attn_slot(i):
                if 1 <= i <= 32:
                    attn_copy(i - 1)
                if i < 32:
                    attn_exp(i)

            pair = 4
            for i in range(12):
                if i % 3 == 0:
                    c = i // 3
                    if c >= 2:
                        act.wait_ge(sem("conv_in"), c - 1)
                    copy_product(cgate[:, c % 2, :], conv_out(i))
                attn_slot(i)
                while pair < 16 and 2 * pair - 6 <= 3 * i:
                    wait_product(act, mod_product((2 * pair - 7) // 3))
                    load_mod_pair(pair)
                    pair += 1
            n, o = SECTIONS["gates"]
            for i in range(16):
                dst = acc[:, i // 2, :] if i % 2 == 0 else gv[:, i // 2, :]
                copy_product(dst, o + 2 * i, func=ACT.Sigmoid)
                attn_slot(12 + i)
            for i in range(28, 34):
                attn_slot(i)

            squares(2, lambda k: xres[:, k, :], ready=lambda k: wait_read(act, SECTIONS["mix"][1] + k))
            root(2)
            act.wait_ge(sem("mod_ready"), 4)
            affine(2, lambda k: gain[:, 2, k:k + 1], lambda k: mod[:, 24 + k, 0:1], None)

            act.dma_start(sub_keys, a["keysT"]).then_inc(sem("keys_in"), 16)
            n, o = SECTIONS["pq"]
            for m in range(HP):
                if m >= 2:
                    act.wait_ge(sem("key_scores"), m - 1)
                copy_product(acc[:, m % 2, :], o + m)

            n, o = SECTIONS["pu"]
            act.wait_ge(sem("split2"), 8)

            def gelu_out(g, k, n0, o0, tile0, first, per_turn=RING):
                s = k % 2
                wait_product(act, o0 + k, g * per_turn)
                if not (first and k < 2):
                    act.wait_ge(sem(f"act_stored{s}"), g * (8 * per_turn) + 16 * ((tile0 + k) // 2))
                free(act.activation(work[:, s, :], bank((o0 + k) % RING), ACT.Gelu), o0 + k)
                wait_read(act, o0 + k, g * per_turn // RING)
                act.dma_start(act_dram[bass.ds(g * per_turn + (tile0 + k), 1)].rearrange("a p n -> (a p) n"),
                              work[:, s, :]).then_inc(sem(f"act_stored{s}"), 16)

            for k in range(RING):
                gelu_out(0, k, n, o, 0, True)
            with act.Fori(0, 12) as g:
                for k in range(RING):
                    gelu_out(g, k, n + 4, o + 4, 4, False)
            act.wait_ge(sem("best_ready"), TT)
            act.activation(best_e, best_e, ACT.Exp).then_inc(sem("best_exp"), 1)
            with act.Fori(0, 3) as g:
                for k in range(RING):
                    gelu_out(g, k, n + 52, o + 52, 52, False)

            act.wait_ge(sem("picks_ready"), TT)
            act.dma_start(memT, a["memT"].rearrange("(k p) t -> p k t", p=P)).then_inc(sem("mem_in"), 16)

            def gate_turn(g, half, first):
                for k in range(RING):
                    t0 = 64 + 4 * half
                    gelu_out(g, k, n + t0, o + t0, t0, False, 8)
                    for q in range(2 * k, 2 * k + 2):
                        act.wait_ge(sem("quad_done"), g * 16 + (8 * half + q + 1))
                        if q == 0 and not first:
                            act.wait_ge(sem(f"gates_stored{half}"), g * 16)
                        act.activation(stage[:, half, :, 4 * q:4 * q + 4],
                                       bank(6 + q % 2).rearrange("p (t j) -> p j t", t=4),
                                       ACT.Copy).then_inc(sem("quad_copied"), 1)
                act.wait_ge(sem("quad_copied"), g * 16 + (8 * half + 8))
                act.dma_start(gates_dram[bass.ds(g * 2 + half, 1)].rearrange("a i j t -> (a i) (j t)"),
                              stage[:, half, :, :].rearrange("p j t -> p (j t)"))\
                    .then_inc(sem(f"gates_stored{half}"), 16)

            gate_turn(0, 0, True)
            gate_turn(0, 1, True)
            with act.Fori(1, 8) as g:
                gate_turn(g, 0, False)
                gate_turn(g, 1, False)

            act.wait_ge(sem("gates_stored0"), 8 * TBS)
            act.wait_ge(sem("gates_stored1"), 8 * TBS)
            act.wait_ge(sem("act_stored0"), 16 * KEYS // 2)
            act.wait_ge(sem("act_stored1"), 16 * KEYS // 2)

            def load_half(j0, b):
                js = bass.ds(j0, 4)
                act.dma_start(ga_act[:, b, :, :], act_dram[js].rearrange("j p t -> p j t")).then_inc(
                    sem(f"act_back{b}"), 16)
                act.dma_start(ga_gate[:, b, :].rearrange("p (b n) -> p b n", b=TBS),
                              gates_dram[:, :, js, :].rearrange("b i j t -> i b (j t)")).then_inc(
                    sem(f"gate_back{b}"), 16)

            load_half(0, 0)
            load_half(4, 1)
            n, o = SECTIONS["memk"]
            for m in range(KB):
                copy_product(mk[:, m, :], o + m, CT)
            with act.Fori(1, 16) as g:
                for b in range(2):
                    act.wait_ge(sem("gated_split"), g * 8 + (4 * b - 4))
                    load_half(g * 8 + 4 * b, b)

            n, o = SECTIONS["memv"]

            def turn_back(m, dst, tiles, turned):
                act.wait_ge(sem("values_turned"), turned + m + 1)
                act.activation(dst[:, :, m * P:(m + 1) * P],
                               bank(6 + m % 2)[:, 0:tiles * P].rearrange("p (t n) -> p t n", t=tiles), ACT.Copy)\
                    .then_inc(sem("values_copied"), 1)

            def mem_copy(m):
                if m < KB:
                    if m >= 2:
                        act.wait_ge(sem("values_turned"), 2 + m - 1)
                    copy_product(mem_raw[:, m % 2, :], o + m, CT)
                if m:
                    turn_back(m - 1, mv, CT // P, 2)

            squares(3, lambda k: xres[:, k, :], ready=lambda k: act.wait_ge(sem("peer_added"), k + 1))
            for m in range(5):
                mem_copy(m)
            root(3)
            for m in range(5, 9):
                mem_copy(m)
            affine(3, lambda k: vec("final", k), None, lambda k: xres[:, k, :])

            n, o = SECTIONS["lstm"]

            def silu(m):
                act.wait_ge(sem("lconv_done"), m + 1)
                dst = lq[:, m, :] if m < 4 else lk[:, m - 4, :]
                act.activation(dst, work[:, 2 + m % 2, :], ACT.Silu).then_inc(sem("qk_ready"), 1)

            act.wait_ge(sem("lraw_zero"), 1)
            for m in range(8):
                if m >= 2:
                    act.wait_ge(sem("lconv_done"), m - 1)
                copy_product(lraw[:, m % 2, 3:3 + T], o + m)
                if m:
                    silu(m - 1)
            silu(7)
            wait_product(act, o + 8)
            act.wait_ge(sem("split3"), 8)
            gb = _VEC["gate_b"][0]
            step(act.activation(irow, psum[0:4, (o + 8) % RING, :], ACT.Identity, bias=vecs[0:4, gb:gb + 1]))
            free(act.activation(frow, psum[32:36, (o + 8) % RING, :], ACT.Identity, bias=vecs[32:36, gb:gb + 1]),
                 o + 8)
            wait_read(act, o + 8)
            step(act.activation(mrow, frow, ACT.Abs))
            step.settle()
            step(act.activation(mrow, mrow, ACT.Exp, scale=-1.0))
            step.settle()
            act.activation(mrow, mrow, ACT.Ln, bias=1.0).then_inc(sem("gate_rows"), 1)
            for m in range(9):
                if m < 8:
                    if m >= 2:
                        act.wait_ge(sem("values_turned"), 10 + m - 1)
                    copy_product(work[:, m % 2, :], o + 9 + m)
                if m:
                    turn_back(m - 1, lv, TT, 10)
            act.wait_ge(sem("floor_arg"), 1)
            act.activation(frow, frow, ACT.Exp, scale=-1.0).then_inc(sem("rows_ready"), 1)
            n, o = SECTIONS["core"]
            for h in range(4):
                for st in range(TT):
                    i = 4 * h + st
                    act.wait_ge(sem("decay_arg"), i + 1)
                    c = slice(st * P, T)
                    act.activation(work[:, 2 + i % 2, c], work[:, 2 + i % 2, c], ACT.Exp).then_inc(sem("decay"), 1)
                for j in range(2):
                    oo = o + 4 * h + j
                    wait_product(act, oo)
                    if h:
                        act.wait_ge(sem("lstm_split"), 2 * h + j - 1)
                    free(act.activation(lsig[:, j, :], bank(oo % RING), ACT.Sigmoid), oo)
                for j in range(2):
                    wait_read(act, o + 4 * h + 2 + j)
                    if h:
                        act.wait_ge(sem("head_rms"), h)
                    act.activation(work[:, j, :], acc[:, 2 * h + j, :], ACT.Square).then_inc(sem("head_squares"), 1)
                act.wait_ge(sem("head_inverse"), h + 1)
                act.activation(work[:, 3, :], work[:, 3, :], ACT.Sqrt).then_inc(sem("head_root"), 1)

            def post_norm(ni, j, ready, last=False):
                squares(ni, lambda k: acc[:, k, :], ready=ready)
                root(ni)
                affine(ni, lambda k: vec("ln_g", 8 * j + k), lambda k: vec("ln_b", 8 * j + k),
                       lambda k: xres[:, k, :], last=sem("norm_out") if last else None)

            def read_of(o):
                return lambda k: wait_read(act, o + k)

            post_norm(4, 0, read_of(SECTIONS["lout"][1]))
            ni = 4
            for layer in range(2):
                if layer:
                    post_norm(7, 3, lambda k: act.wait_ge(sem("pool_added"), k + 1))
                    ni = 7
                n, o = SECTIONS[f"xq{layer}"]

                def x_exp(h):
                    for t in range(TT):
                        i = 4 * (4 * layer + h) + t
                        act.wait_ge(sem("x_shift"), i + 1)
                        act.activation(xp[:, t, :], xp[:, t, :], ACT.Exp, scale=0.0625,
                                       bias=small[:, 32 + t:33 + t],
                                       accum_out=small[:, 36 + t:37 + t]).then_inc(sem("x_exp"), 1)

                def x_copy(h):
                    i = 4 * layer + h
                    for j in range(2):
                        if j == 0:
                            act.wait_ge(sem("x_turned"), 4 * i + 4)
                            if i:
                                wait_product(act, x_value_out(i - 1))
                        act.activation(xpT[:, j, :], bank(6 + j), ACT.Copy).then_inc(sem("x_turned_copied"), 1)

                for m in range(KB):
                    oo = o + m + (0 if m < 4 else 2 if m < 6 else 4)
                    copy_product(xq[:, m, :], oo)
                    if m % 2:
                        h = m // 2
                        if h:
                            x_copy(h - 1)
                        x_exp(h)
                x_copy(3)
                post_norm(ni + 1, 3 * layer + 1, read_of(SECTIONS[f"xo{layer}"][1]))
                act.wait_ge(sem("affine_done"), 8 * (ni + 2))
                act.wait_ge(sem("scaled"), 8 * (ni + 2))
                for k in range(KB):
                    act.activation(acc[:, k, :], xres[:, k, :], ACT.Identity, scale=ALPHA,
                                   bias=vec("b2", 8 * layer + k)).then_inc(sem("mlp_start"), 1)
                n, o = SECTIONS[f"mlp{layer}"]
                b1at = _VEC["b1"][0] + 32 * layer

                def relu(oo, first, f, turn=0):
                    wait_product(act, oo, turn * 16)
                    if not first:
                        act.wait_ge(sem("hidden_split"), turn * 8 + (32 * layer + f - 1))
                    free(act.activation(work[:, f % 2, :], bank(oo % RING), ACT.Relu,
                                        bias=vecs[:, bass.ds(turn * 8 + (b1at + f), 1)]), oo)

                for k in range(4):
                    relu(o + k, layer == 0 and k < 2, k)
                with act.Fori(0, 3) as g:
                    for half in range(2):
                        for k in range(4):
                            relu(o + 4 + 12 * half + k, False, 4 + 4 * half + k, g)
                for k in range(4):
                    relu(o + 76 + k, False, 28 + k)
                post_norm(ni + 2, 3 * layer + 2, read_of(o + 88), last=(layer == 1))

        @block.vector
        def _(dve):
            step = Steps(dve, "dve_step")

            def split(src, hi, lo, signal):
                step(dve.tensor_copy(hi, src))
                step.settle()
                dve.tensor_tensor(lo, src, hi.bitcast(F32), ALU.subtract).then_inc(signal, 1)

            def add_square(ni, k, cols=T):
                dve.wait_ge(sem("squared"), 8 * ni + k + 1)
                if k:
                    dve.wait_ge(sem("summed"), 8 * ni + k)
                    ins = dve.tensor_tensor(work[:, 5, 0:cols], work[:, 5, 0:cols], work[:, k % 2, 0:cols], ALU.add)
                else:
                    if ni:
                        dve.wait_ge(sem("inverse_ready"), ni)
                    ins = dve.tensor_copy(work[:, 5, 0:cols], work[:, k % 2, 0:cols])
                ins.then_inc(sem("summed"), 1)

            def add_value(ni, k, src):
                step.settle()
                if k:
                    step(dve.tensor_tensor(work[:, 4, :], work[:, 4, :], src, ALU.add))
                else:
                    step(dve.tensor_copy(work[:, 4, :], src))

            def statistics(ni, eps, cols=T, mean=False, width=D):
                dve.wait_ge(sem("sums_ready"), ni + 1)
                mu, v, r = work[:, 6, 0:cols], work[:, 5, 0:cols], work[:, 7, 0:cols]
                if mean:
                    step(dve.tensor_scalar(mu, bank(4)[:, 0:cols], 1.0 / width, None, ALU.mult))
                    step.settle()
                    step(dve.tensor_tensor(work[:, 4, 0:cols], mu, mu, ALU.mult))
                    step.settle()
                    dve.scalar_tensor_tensor(v, bank(5)[:, 0:cols], 1.0 / width, work[:, 4, 0:cols], ALU.mult,
                                             ALU.subtract).then_inc(sem("stats_read"), 1)
                    dve.wait_ge(sem("stats_read"), ni + 1)
                    step(dve.tensor_scalar(v, v, 0.0, eps, ALU.max, ALU.add))
                else:
                    dve.tensor_scalar(v, bank(5)[:, 0:cols], 1.0 / width, eps, ALU.mult, ALU.add)\
                        .then_inc(sem("stats_read"), 1)
                    dve.wait_ge(sem("stats_read"), ni + 1)
                step.settle()
                dve.reciprocal(r, v).then_inc(sem("inverse_ready"), 1)

            def normalise(ni, src, cols=T, mean=False):
                def centre(k):
                    step(dve.tensor_tensor(src(k), src(k), work[:, 6, :], ALU.subtract))

                if mean:
                    for k in range(3):
                        centre(k)
                dve.wait_ge(sem("root_ready"), ni + 1)
                step.settle()

                def scale(k):
                    if mean and k >= 3:
                        centre(k)
                        step.settle()
                    if k >= 2:
                        dve.wait_ge(sem("norm_out") if ni == 9 else sem("affine_done"),
                                    (k - 1) if ni == 9 else 8 * ni + k - 1)
                    dve.tensor_tensor(work[:, 2 + k % 2, 0:cols], src(k), work[:, 7, 0:cols], ALU.mult)\
                        .then_inc(sem("scaled"), 1)
                return scale

            def norm_out(ni, scale, out_tile, hi, lo):
                scale(0)
                for k in range(KB):
                    if k + 1 < KB:
                        scale(k + 1)
                    dve.wait_ge(sem("affine_done"), 8 * ni + k + 1)
                    split(out_tile(k), hi(k), lo(k), sem(f"split{ni}"))

            dve.wait_ge(sem("vecs_in"), 16)
            dve.wait_ge(sem("consts_in"), 16)
            step(dve.tensor_scalar(sink8, vecr("sink"), 8.0, None, ALU.mult))
            for k in range(KB):
                add_square(0, k, CT)
            statistics(0, EPS, CT)
            for k in range(KB):
                add_square(1, k)
            dve.wait_ge(sem("mod_used"), 16)
            step(dve.memset(zpad[:, :, 0:1], 0.0))
            step(dve.memset(zpad[:, :, T + 1:T + 2], 0.0))

            def bias_mod(t0, nt, src):
                return dve.tensor_tensor(mod[:, t0:t0 + nt, :], src.rearrange("p (t two) -> p t two", two=2),
                                         vecr("b_mod")[:, t0:t0 + nt].unsqueeze(2).broadcast_to((P, nt, 2)), ALU.add)

            def gain_of(j, t0, col, nv):
                dve.scalar_tensor_tensor(gain[:, j, :], mod[:, t0:t0 + 8, col], 1.0, vecr(nv), ALU.add, ALU.mult)\
                    .then_inc(sem("mod_ready"), 1)

            bias_mod(0, 16, bank(6)[:, 0:32]).then_inc(sem("mod_ready"), 1)
            dve.wait_ge(sem("mod_ready"), 1)
            gain_of(0, 8, 0, "n1")
            gain_of(1, 8, 1, "n1")
            norm_out(0, normalise(0, lambda k: acc[:, k, 0:CT], CT), lambda k: work[:, k % 2, 0:CT],
                     lambda k: yhi[:, k, 0:CT], lambda k: ylo[:, k, 0:CT])
            statistics(1, EPS)
            norm_out(1, normalise(1, lambda k: xres[:, k, :]), lambda k: work[:, k % 2, :],
                     lambda k: xhi[:, k, :], lambda k: xlo[:, k, :])

            n, o = SECTIONS["in"]
            for i in range(5):
                dst = k_rope if i == 0 else q_rope[:, i - 1, :]
                wait_read(dve, o + 1 + i)
                step(dve.tensor_tensor(work[:, 2, :], work[:, i % 2, :], const("cos"), ALU.mult))
                dve.wait_ge(sem("swapped"), i + 1)
                step(dve.tensor_tensor(work[:, 3, :], bank(6), const("sin"), ALU.mult))
                step.settle()
                dve.tensor_tensor(dst, work[:, 2, :], work[:, 3, :], ALU.add).then_inc(sem("rotated"), 1)
                dve.wait_ge(sem("rotated"), i + 1)

            def attn_softmax_in(u):
                m, g, qt, lo, hi = unit(u)
                wl = (hi - lo + 1) * P
                w = wl + CT
                s = probs[:, u % 2, :]
                dve.wait_ge(sem("scores_ready"), u + 1)
                if u >= 2:
                    dve.wait_ge(sem("turned"), u - 1)
                b0 = _CONST["band"][0] + (lo - qt + 1) * P
                step(dve.tensor_tensor(s[:, 0:wl], wide(4, 640)[:, 0:wl], consts[:, b0:b0 + wl], ALU.add))
                dve.tensor_copy(s[:, wl:w], wide(4, 640)[:, wl:w]).then_inc(sem("scores_read"), 1)
                step.settle()
                dve.wait_ge(sem("scores_read"), u + 1)
                mx = small[:, 22 + u % 2:23 + u % 2]
                step(dve.tensor_reduce(mx, s[:, 0:w], AX.X, ALU.max))
                step.settle()
                head = m + 4 * g
                dve.tensor_scalar(small[:, 20 + u % 2:21 + u % 2], mx, sink8[:, head:head + 1], -0.125, ALU.max,
                                  ALU.mult).then_inc(sem("shift_ready"), 1)

            def attn_softmax_out(u):
                m, g, qt, lo, hi = unit(u)
                w = (hi - lo + 3) * P
                dve.wait_ge(sem("attn_exp"), 2 * u + 2)
                den = small[:, 28 + u % 2:29 + u % 2]
                step(dve.tensor_tensor(den, small[:, 24 + u % 2:25 + u % 2], small[:, 26 + u % 2:27 + u % 2], ALU.add))
                step.settle()
                step(dve.reciprocal(den, den))
                step.settle()
                dve.tensor_scalar(probs[:, u % 2, 0:w], probs[:, u % 2, 0:w], den, None, ALU.mult)\
                    .then_inc(sem("probs_ready"), 1)

            def attn_split(u):
                m, g, qt, lo, hi = unit(u)
                rows = slice(64 * g, 64 * g + 64)
                c = slice(qt * P, (qt + 1) * P)
                o = attn_product(u)
                wait_product(dve, o)
                split(psum[rows, o % RING, 0:P], yhi[rows, m, c], ylo[rows, m, c], bank_free[o % RING])

            def attn_slot(i):
                if i < 32:
                    attn_softmax_in(i)
                    attn_softmax_out(i)
                if 2 <= i <= 33:
                    attn_split(i - 2)

            for i in range(12):
                c = i // 3
                if i % 3 == 1:
                    wait_read(dve, conv_out(i - 1))
                    o = conv_out(i)
                    wait_product(dve, o)
                    free(dve.tensor_tensor(zpad[:, c % 2, 1:T + 1], bank(o % RING), cgate[:, c % 2, :],
                                           ALU.mult), o)
                    wait_read(dve, o)
                    y = work[:, 2 + c % 2, :]
                    z = zpad[:, c % 2, :]
                    dve.tensor_scalar(y, z[:, 0:T], vec("conv", c), None, ALU.mult).then_inc(sem("conv_in"), 1)
                    dve.wait_ge(sem("conv_in"), c + 1)
                    for tap in (1, 2):
                        step(dve.scalar_tensor_tensor(y, z[:, tap:tap + T], vec("conv", 4 * tap + c), y, ALU.mult,
                                                      ALU.add))
                        step.settle()
                if i % 3 == 2:
                    o = conv_out(i)
                    wait_product(dve, o)
                    y = work[:, 2 + c % 2, :]
                    free(dve.tensor_tensor(y, bank(o % RING), y, ALU.mult), o)
                    wait_read(dve, o)
                    split(y, yhi[:, 4 + c, :], ylo[:, 4 + c, :], sem("conv_split"))
                attn_slot(i)
                if i < 11:
                    o = mod_product(i)
                    t = mod_tiles(i)
                    wait_product(dve, o)
                    free(bias_mod(16 + t[0], len(t), bank(o % RING)[:, 0:2 * len(t)]), o)
            wait_read(dve, mod_product(10))
            gain_of(2, 32, 0, "n2")
            for i in range(12, 34):
                attn_slot(i)

            n, o = SECTIONS["branch"]
            for m in range(KB):
                for j, t in ((0, acc[:, m, :]), (1, gv[:, m, :])):
                    wait_read(dve, SECTIONS["gates"][1] + 4 * m + 2 * j)
                    wait_product(dve, o + 2 * m + j)
                    free(dve.tensor_tensor(t, bank((o + 2 * m + j) % RING), t, ALU.mult), o + 2 * m + j)
                    wait_read(dve, o + 2 * m + j)
                step(dve.tensor_tensor(acc[:, m, :], acc[:, m, :], gv[:, m, :], ALU.add))
                step.settle()
                split(acc[:, m, :], xhi[:, m, :], xlo[:, m, :], sem("merge_split"))

            n, o = SECTIONS["mix"]
            for k in range(KB):
                wait_product(dve, o + k)
                free(dve.scalar_tensor_tensor(xres[:, k, :], bank((o + k) % RING), mod[:, 16 + k, 0:1], xres[:, k, :],
                                              ALU.mult, ALU.add), o + k)
                if k:
                    add_square(2, k - 1)
            add_square(2, KB - 1)
            statistics(2, EPS)
            norm_out(2, normalise(2, lambda k: xres[:, k, :]), lambda k: work[:, k % 2, :],
                     lambda k: xhi[:, k, :], lambda k: xlo[:, k, :])

            for m in range(HP):
                dve.wait_ge(sem("key_scores"), m + 1)
                dve.tensor_copy(scores_all[:, :, m, :], bank(6).rearrange("p (t n) -> p t n", t=TT))\
                    .then_inc(sem("key_scores_copied"), 1)
            dve.wait_ge(sem("key_scores_copied"), HP)

            def top16(values, indices, rows, src):
                for half in range(2):
                    c = slice(8 * half, 8 * half + 8)
                    for r in range(rows):
                        step(dve.max(values[:, r, c], src[:, r, :]))
                    step.settle()
                    for r in range(rows):
                        step(dve.max_index(indices[:, r, c], values[:, r, c], src[:, r, :]))
                    step.settle()
                    if half == 0:
                        for r in range(rows):
                            step(dve.match_replace(src[:, r, :], values[:, r, c], src[:, r, :], LOWEST))
                        step.settle()

            heads = HP // 2
            v = top_v.rearrange("p (h s r) -> p h s r", h=heads, s=2)
            f = top_f.rearrange("p (h s r) -> p h s r", h=heads, s=2)
            b = best.rearrange("p (h k) -> p h k", h=heads)
            e_all = best_e.rearrange("p (t h k) -> p t h k", t=TT, h=heads)
            look3 = look.rearrange("p (n r) -> p n r", r=TOPK)
            look4 = look.rearrange("p (h k r) -> p h k r", h=heads, k=TOPK)
            for tt in range(TT):
                top16(top_v.rearrange("p (h r) -> p h r", h=HP), top_i.bitcast(U32).rearrange("p (h r) -> p h r", h=HP),
                      HP, scores_all[:, tt, :, :])
                step(dve.tensor_copy(top_f, top_i.bitcast(U32)))
                step(dve.tensor_tensor(cand.rearrange("p (h a b) -> p h a b", h=heads, a=TOPK),
                                       v[:, :, 0, :].unsqueeze(3).broadcast_to((P, heads, TOPK, TOPK)),
                                       v[:, :, 1, :].unsqueeze(2).broadcast_to((P, heads, TOPK, TOPK)), ALU.add))
                step.settle()
                top16(b, best_pos.bitcast(U32).rearrange("p (h k) -> p h k", h=heads), heads,
                      cand.rearrange("p (h n) -> p h n", h=heads))
                step(dve.tensor_scalar(best_row.bitcast(U32), best_pos.bitcast(U32), 4, None,
                                       ALU.logical_shift_right))
                step.settle()
                step(dve.tensor_scalar(best_pos.bitcast(U32), best_pos.bitcast(U32), 15, None, ALU.bitwise_and))
                step(dve.tensor_copy(top_i[:, 0:P], best_row.bitcast(U32)))
                step.settle()
                step(dve.tensor_copy(top_i[:, P:2 * P], best_pos.bitcast(U32)))
                step.settle()
                for s in range(2):
                    step(dve.tensor_tensor(look3, top_i[:, s * P:(s + 1) * P].unsqueeze(2).broadcast_to((P, P, TOPK)),
                                           const("iota")[:, 0:TOPK].unsqueeze(1).broadcast_to((P, P, TOPK)),
                                           ALU.is_equal))
                    step.settle()
                    step(dve.tensor_tensor(look4, look4,
                                           f[:, :, s, :].unsqueeze(2).broadcast_to((P, heads, TOPK, TOPK)),
                                           ALU.mult))
                    step.settle()
                    step(dve.tensor_reduce(picks[:, tt, s, :], look3, AX.X, ALU.add))
                    step.settle()
                dve.tensor_tensor(e_all[:, tt, :, :], b, b[:, :, 0:1].broadcast_to((P, heads, TOPK)),
                                  ALU.subtract).then_inc(sem("best_ready"), 1)
                dve.wait_ge(sem("best_ready"), tt + 1)
            dve.wait_ge(sem("best_exp"), 1)
            for tt in range(TT):
                step(dve.tensor_reduce(best_sum, e_all[:, tt, :, :], AX.X, ALU.add))
                step.settle()
                step(dve.reciprocal(best_sum, best_sum))
                step.settle()
                dve.tensor_tensor(picks[:, tt, 2, :].rearrange("p (h k) -> p h k", h=heads), e_all[:, tt, :, :],
                                  best_sum.unsqueeze(2).broadcast_to((P, heads, TOPK)), ALU.mult)\
                    .then_inc(sem("picks_ready"), 1)
                dve.wait_ge(sem("picks_ready"), tt + 1)

            for i in range(3 * TT):
                dve.wait_ge(sem("picks_turned"), i + 1)
                dve.tensor_copy(picksT[:, i % 3, (i // 3) * P:(i // 3 + 1) * P], bank(6 + i % 2)[:, 0:P])\
                    .then_inc(sem("picks_copied"), 1)
            dve.wait_ge(sem("picks_copied"), 3 * TT)

            def hot_rows(g, half, first):
                for q in range(8):
                    if not (first and q < 2):
                        dve.wait_ge(sem("quad_done"), g * 16 + (8 * half + q - 1))
                    for r in range(4):
                        slot = (4 * q + r) % 8
                        tok = bass.ds(g * (2 * TB) + (TB * half + 4 * q + r), 1)
                        step(dve.tensor_scalar(hot[:, slot, 0, :], const("iota"), picksT[:, 0, tok], None,
                                               ALU.is_equal))
                        ins = dve.tensor_scalar(hot[:, slot, 1, :], const("iota"), picksT[:, 1, tok],
                                                picksT[:, 2, tok], ALU.is_equal, ALU.mult)
                        if r < 3:
                            step(ins)
                        else:
                            ins.then_inc(sem("hot_ready"), 1)

            hot_rows(0, 0, True)
            hot_rows(0, 1, False)
            per = 7 * 16
            with dve.Fori(1, 8) as g:
                hot_rows(g, 0, False)
                hot_rows(g, 1, False)
            step.n += 6 * per
            dve.wait_ge(sem("quad_done"), 128)
            dve.wait_ge(sem("mem_in"), 16)
            wait_product(dve, SECTIONS["pu"][1] + 127)
            for k in range(KB):
                split(memT[:, k, :], xhi[:, k, 0:CT], xlo[:, k, 0:CT], sem("mem_split"))
            dve.wait_ge(sem("mem_split"), KB)

            def gated(g, b, j):
                if j == 0:
                    dve.wait_ge(sem(f"act_back{b}"), g * 16 + 16)
                    dve.wait_ge(sem(f"gate_back{b}"), g * 16 + 16)
                t = ga_act[:, b, j, :]
                gt = ga_gate[:, b, :].rearrange("p (b j t) -> p b j t", b=TBS, j=4)[:, :, j, :]
                step(dve.tensor_tensor(t.rearrange("p (b t) -> p b t", b=TBS), t.rearrange("p (b t) -> p b t", b=TBS),
                                       gt, ALU.mult))
                step.settle()
                split(t, yhi[:, 4 * b + j, :], ylo[:, 4 * b + j, :], sem("gated_split"))

            def collect(oo, shift, k, first=False):
                wait_product(dve, oo, shift)
                if first:
                    ins = dve.tensor_copy(acc[:, k, :], bank(oo % RING))
                else:
                    ins = dve.tensor_tensor(acc[:, k, :], acc[:, k, :], bank(oo % RING), ALU.add)
                free(ins, oo)

            n, o = SECTIONS["pv"]
            for b in range(2):
                for j in range(4):
                    gated(0, b, j)
            for half in range(2):
                for k in range(KB):
                    collect(o + 8 * half + k, 0, k, first=(half == 0))
                for j in range(4):
                    gated(1, half, j)
            per = 2 * 4 * 2
            base = step.n
            with dve.Fori(1, 15) as g:
                step.turn = g * per - per
                for half in range(2):
                    for k in range(KB):
                        collect(o + 8 * half + k, g * 8, k)
                    for j in range(4):
                        gated(g + 1, half, j)
            assert step.n == base + per
            step.turn = 0
            step.n = base + 14 * per
            dve.wait_ge(sem("gated_split"), 128)
            for k in range(2 * KB):
                if k >= KB:
                    wait_read(dve, o + 240 + k - KB)
                collect(o + 240 + k, 0, k % KB)
            for k in range(KB):
                wait_read(dve, o + 248 + k)
                dve.scalar_tensor_tensor(xres[:, k, :], acc[:, k, :], mod[:, 40 + k, 0:1], xres[:, k, :], ALU.mult,
                                         ALU.add).then_inc(sem("peer_added"), 1)
                if k:
                    add_square(3, k - 1)
            add_square(3, KB - 1)
            statistics(3, EPS)
            wait_product(dve, SECTIONS["memv"][1] + 7)
            norm_out(3, normalise(3, lambda k: xres[:, k, :]), lambda k: xres[:, k, :],
                     lambda k: xhi[:, k, :], lambda k: xlo[:, k, :])

            dve.memset(lraw[:, :, 0:3], 0.0).then_inc(sem("lraw_zero"), 1)
            dve.wait_ge(sem("lraw_zero"), 1)
            for m in range(8):
                wait_read(dve, SECTIONS["lstm"][1] + m)
                if m >= 2:
                    dve.wait_ge(sem("qk_ready"), m - 1)
                y = work[:, 2 + m % 2, :]
                step(dve.tensor_scalar(y, lraw[:, m % 2, 0:T], vec("mconv", m), None, ALU.mult))
                step.settle()
                for tap in (1, 2, 3):
                    ins = dve.scalar_tensor_tensor(y, lraw[:, m % 2, tap:tap + T], vec("mconv", 8 * tap + m), y,
                                                   ALU.mult, ALU.add)
                    if tap < 3:
                        step(ins)
                        step.settle()
                    else:
                        ins.then_inc(sem("lconv_done"), 1)
            dve.wait_ge(sem("gate_rows"), 1)
            step(dve.tensor_scalar(arow, frow, 0.0, None, ALU.min))
            step.settle()
            step(dve.tensor_tensor(arow, arow, mrow, ALU.subtract))
            step.settle()
            step(dve.tensor_tensor_scan(frow, const("ones", 4)[:, 0:1].broadcast_to((4, T)), arow, 0.0, ALU.mult,
                                        ALU.add))
            step.settle()
            step(dve.tensor_tensor(arow, irow, frow, ALU.subtract))
            step.settle()
            step(dve.tensor_tensor_scan(mrow, arow, arow, 0.0, ALU.max, ALU.max))
            step.settle()
            step(dve.tensor_tensor(frow, frow, mrow, ALU.add))
            step.settle()
            dve.tensor_scalar(mrow, mrow, -1.0, None, ALU.mult).then_inc(sem("floor_arg"), 1)
            dve.wait_ge(sem("decay_turned"), 1)
            dve.tensor_copy(acol, bank(7)[:, 0:16]).then_inc(sem("decay_copied"), 1)
            dve.wait_ge(sem("decay_copied"), 1)
            n, o = SECTIONS["core"]
            for h in range(4):
                dve.wait_ge(sem("max_spread"), h + 1)
                dve.wait_ge(sem("qk_ready"), 8)

                def decay_arg(st):
                    i = 4 * h + st
                    c = slice(st * P, T)
                    step.settle()
                    dve.tensor_scalar(work[:, 2 + i % 2, c], bank(4)[:, c], acol[:, 4 * st + h:4 * st + h + 1], 0.0,
                                      ALU.add, ALU.min).then_inc(sem("decay_arg"), 1)
                decay_arg(0)
                for st in range(TT):
                    i = 4 * h + st
                    if st + 1 < TT:
                        if i >= 1:
                            dve.wait_ge(sem("lstm_weighted"), i)
                        decay_arg(st + 1)
                    c = slice(st * P, T)
                    dve.wait_ge(sem("decay"), i + 1)
                    dve.wait_ge(sem("lstm_scores"), i + 1)
                    step(dve.scalar_tensor_tensor(lp[:, st, c], bank(5 + i % 2)[:, c], 128 ** -0.5,
                                                  work[:, 2 + i % 2, c], ALU.mult, ALU.mult))
                    step.settle()
                    d = slice(st * P, (st + 1) * P)
                    dve.tensor_tensor(lp[:, st, d], lp[:, st, d], const("utri"), ALU.mult)\
                        .then_inc(sem("lstm_weighted"), 1)
                dve.wait_ge(sem("lstm_weighted"), 4 * h + 4)
                dve.wait_ge(sem("lstm_den"), h + 1)
                den = work[:, 2, :]
                step(dve.tensor_copy(den, bank(7)))
                step.settle()
                step(dve.scalar_tensor_tensor(den, den, -1.0, den, ALU.mult, ALU.max))
                dve.wait_ge(sem("floor_spread"), h + 1)
                step.settle()
                dve.tensor_tensor(den, den, bank(4), ALU.max).then_inc(sem("floor_read"), 1)
                dve.wait_ge(sem("floor_read"), h + 1)
                step(dve.reciprocal(den, den))
                step.settle()
                for j in range(2):
                    oo = o + 4 * h + 2 + j
                    wait_product(dve, oo)
                    free(dve.tensor_tensor(acc[:, 2 * h + j, :], bank(oo % RING), den, ALU.mult), oo)
                    wait_read(dve, oo)
                dve.wait_ge(sem("head_rms"), h + 1)
                v = work[:, 3, :]
                dve.tensor_scalar(v, bank(7), 1.0 / 256, LN_EPS, ALU.mult, ALU.add).then_inc(sem("head_rms_read"), 1)
                dve.wait_ge(sem("head_rms_read"), h + 1)
                dve.reciprocal(v, v).then_inc(sem("head_inverse"), 1)
                dve.wait_ge(sem("head_root"), h + 1)
                for j in range(2):
                    t = acc[:, 2 * h + j, :]
                    step(dve.tensor_tensor(t, t, v, ALU.mult))
                    step.settle()
                    wait_read(dve, o + 4 * h + j)
                    step(dve.scalar_tensor_tensor(t, t, vec("mnorm", 2 * h + j), lsig[:, j, :], ALU.mult, ALU.mult))
                    step.settle()
                    split(t, yhi[:, 2 * h + j, :], ylo[:, 2 * h + j, :], sem("lstm_split"))

            def residual_products(ni, o):
                for k in range(KB):
                    wait_product(dve, o + k)
                    free(dve.scalar_tensor_tensor(acc[:, k, :], xres[:, k, :], ALPHA, bank((o + k) % RING), ALU.mult,
                                                  ALU.add), o + k)
                    wait_read(dve, o + k)
                    add_value(ni, k, acc[:, k, :])
                    if k:
                        add_square(ni, k - 1)
                add_square(ni, KB - 1)
                step.settle()

            def pool_mixer(scale):
                dve.memset(ppad[:, :, 0:16], 0.0).then_inc(sem("ppad_zero"), 1)
                dve.wait_ge(sem("ppad_zero"), 1)
                scale(0)
                for k in range(KB):
                    if k + 1 < KB:
                        scale(k + 1)
                    w = WINDOWS[k // 2]
                    x = xres[:, k, :]
                    dve.wait_ge(sem("affine_done"), 8 * 6 + k + 1)
                    step(dve.tensor_tensor(ppad[:, 0, 17:], x[:, 1:T], x[:, 0:T - 1], ALU.add))
                    step(dve.tensor_copy(ppad[:, 0, 16:17], x[:, 0:1]))
                    step.settle()
                    at, shift = 0, 2
                    while shift < w:
                        step(dve.tensor_tensor(ppad[:, 1 - at, 16:], ppad[:, at, 16:],
                                               ppad[:, at, 16 - shift:16 - shift + T], ALU.add))
                        step.settle()
                        at, shift = 1 - at, 2 * shift
                    y = pool_y[:, k % 2, :]
                    step(dve.scalar_tensor_tensor(y[:, 16:T], ppad[:, at, 32:], 1.0 / w, x[:, 16:T], ALU.mult,
                                                  ALU.subtract))
                    c0 = _CONST["cnt"][0] + 16 * (k // 2)
                    step(dve.tensor_tensor(y[:, 0:16], ppad[:, at, 16:32], consts[:, c0:c0 + 16], ALU.mult))
                    step.settle()
                    step(dve.tensor_tensor(y[:, 0:16], y[:, 0:16], x[:, 0:16], ALU.subtract))
                    step.settle()
                    split(y, yhi[:, k, :], ylo[:, k, :], sem("pool_split"))
                    dve.wait_ge(sem("pool_split"), k + 1)

            def post_norm(ni, last=False):
                statistics(ni, LN_EPS, mean=True)
                scale = normalise(ni, lambda k: acc[:, k, :], mean=True)
                if ni == 6:
                    pool_mixer(scale)
                elif last:
                    for k in range(KB):
                        scale(k)
                else:
                    norm_out(ni, scale, lambda k: xres[:, k, :], lambda k: xhi[:, k, :], lambda k: xlo[:, k, :])

            dve.wait_ge(sem("lstm_split"), 8)
            residual_products(4, SECTIONS["lout"][1])
            post_norm(4)
            ni = 4
            for layer in range(2):
                if layer:
                    o = SECTIONS["pool"][1]
                    for k in range(KB):
                        wait_product(dve, o + k)
                        free(dve.tensor_scalar(acc[:, k, :], bank((o + k) % RING), vec("pscale", k), None, ALU.mult),
                             o + k)
                        wait_read(dve, o + k)
                        dve.scalar_tensor_tensor(acc[:, k, :], xres[:, k, :], ALPHA, acc[:, k, :], ALU.mult,
                                                 ALU.add).then_inc(sem("pool_added"), 1)
                        dve.wait_ge(sem("pool_added"), k + 1)
                        add_value(7, k, acc[:, k, :])
                        if k:
                            add_square(7, k - 1)
                    add_square(7, KB - 1)
                    step.settle()
                    post_norm(7)
                    ni = 7
                n, o = SECTIONS[f"xq{layer}"]

                def x_softmax_in(h):
                    for t in range(TT):
                        i = 4 * (4 * layer + h) + t
                        dve.wait_ge(sem("x_scores"), i + 2 - t % 2)
                        if i >= 4:
                            dve.wait_ge(sem("x_turned"), i - 3)
                        s = wide(4, 1024)[:, t * CT:(t + 1) * CT]
                        mx = small[:, 40 + t:41 + t]
                        step(dve.tensor_reduce(mx, s, AX.X, ALU.max))
                        dve.tensor_copy(xp[:, t, :], s).then_inc(sem("x_scores_read"), 1)
                        dve.wait_ge(sem("x_scores_read"), i + 1)
                        step.settle()
                        dve.tensor_scalar(small[:, 32 + t:33 + t], mx, -0.0625, None, ALU.mult)\
                            .then_inc(sem("x_shift"), 1)

                def x_softmax_out(h):
                    for t in range(TT):
                        i = 4 * (4 * layer + h) + t
                        dve.wait_ge(sem("x_exp"), i + 1)
                        r = small[:, 36 + t:37 + t]
                        step(dve.reciprocal(r, r))
                        step.settle()
                        dve.tensor_scalar(xp[:, t, :], xp[:, t, :], r, None, ALU.mult).then_inc(sem("x_probs"), 1)

                def x_split(h):
                    for j in range(2):
                        oo = x_value_out(4 * layer + h) - 1 + j
                        wait_product(dve, oo)
                        step(dve.tensor_copy(yhi[:, 2 * h + j, :], bank(oo % RING)))
                        step.settle()
                        free(dve.tensor_tensor(ylo[:, 2 * h + j, :], bank(oo % RING), yhi[:, 2 * h + j, :].bitcast(F32),
                                               ALU.subtract), oo)

                for h in range(4):
                    x_softmax_in(h)
                    x_softmax_out(h)
                    if h:
                        x_split(h - 1)
                x_split(3)
                residual_products(ni + 1, SECTIONS[f"xo{layer}"][1])
                post_norm(ni + 1)
                n, o = SECTIONS[f"mlp{layer}"]

                def hidden(oo, j, f, first=False, turn=0):
                    wait_read(dve, oo, turn * 6)
                    if not first:
                        dve.wait_ge(sem("hidden_split"), turn * 8 + (32 * layer + f - 1))
                    t, q = work[:, j % 2, :], work[:, 2 + j % 2, :]
                    step(dve.tensor_tensor(q, t, t, ALU.mult))
                    step.settle()
                    split(q, yhi[:, j, :], ylo[:, j, :], sem("hidden_split"))

                dve.wait_ge(sem("mlp_start"), 8 * layer + 8)
                for j in range(4):
                    hidden(o + j, j, j, layer == 0 and j < 2)

                def turn(g, half):
                    for j in range(4):
                        hidden(o + 4 + 12 * half + j, 4 * (1 - half) + j, 4 + 4 * half + j, turn=g)
                    for k in range(KB):
                        oo = o + 8 + 12 * half + k
                        wait_product(dve, oo, g * 16 if DONE[oo][0] == "tile" else g * 8)
                        free(dve.tensor_tensor(acc[:, k, :], acc[:, k, :], bank(oo % RING), ALU.add), oo)

                per = 2 * (4 * 2)
                base = step.n
                with dve.Fori(0, 3) as g:
                    step.turn = g * per
                    turn(g, 0)
                    turn(g, 1)
                assert step.n == base + per
                step.turn = 0
                step.n = base + 3 * per
                turn(3, 0)
                for k in range(8):
                    oo = o + 88 + k
                    wait_product(dve, oo)
                    wait_read(dve, oo - 8)
                    free(dve.tensor_tensor(acc[:, k, :], acc[:, k, :], bank(oo % RING), ALU.add), oo)
                    wait_read(dve, oo)
                    add_value(ni + 2, k, acc[:, k, :])
                    if k:
                        add_square(ni + 2, k - 1)
                add_square(ni + 2, KB - 1)
                step.settle()
                post_norm(ni + 2, last=(layer == 1))


def shape_constants():
    parts = {"ident": np.eye(P), "ones": np.ones((P, P)), "iota": np.tile(np.arange(P), (P, 1))}
    perm = np.zeros((P, P))
    for f in range(P):
        if f % 32 < 16:
            perm[f + 16, f] = -1.0
        else:
            perm[f - 16, f] = 1.0
    parts["perm"] = perm
    r = np.arange(P)
    parts["utri"] = (r[:, None] <= r[None, :]).astype(np.float32)
    before = np.where(r[None, :] >= r[:, None], 0.0, NEG)
    after = np.where(r[None, :] <= r[:, None], 0.0, NEG)
    parts["band"] = np.concatenate([before, np.zeros((P, P)), after], axis=1)
    t = np.arange(T)
    freq = (np.float32(ROPE_BASE) ** (-np.arange(PAIRS, dtype=np.float32) / np.float32(PAIRS))).astype(np.float32)
    angle = np.zeros((P, T), np.float32)
    for f in range(P):
        place = (t // GRID_W if f % 64 < 32 else t % GRID_W).astype(np.float32)
        angle[f] = place * freq[f % 16]
    parts["cos"], parts["sin"] = np.cos(angle), np.sin(angle)
    parts["cnt"] = np.tile(np.concatenate([1.0 / np.minimum(np.arange(16) + 1, w) for w in WINDOWS]), (P, 1))
    return np.concatenate([np.asarray(parts[name], np.float32) for name in _CONST], axis=1)


def columns(v):
    return np.ascontiguousarray(np.asarray(v).reshape(-1, P).T)


def row_tiles(w):
    k, m = w.shape
    return w.reshape(k // P, P, m // P, P).transpose(2, 1, 0, 3).reshape(m // P, P, k)


def half_groups(w):
    k = w.shape[0]
    return w.reshape(k // 512, 4, P, 4, 2, P).transpose(0, 3, 2, 4, 1, 5).reshape(k // 128, P, 1024)


def layout(x):
    a = {}
    z = np.zeros
    f32 = np.float32
    w_in = x["w_in"][0]
    heads = w_in[:, 0:512].reshape(D, 2, 4, 64).transpose(0, 2, 1, 3).reshape(D, 512)
    q, rest = row_tiles(heads), row_tiles(w_in[:, 512:])
    k, v, gb, gc, u, ga, gv = rest[0:1], rest[1:2], rest[2:6], rest[6:10], rest[10:14], rest[14:22], rest[22:30]
    conv = np.stack([gc, u, gb], axis=1).reshape(12, P, 1024)
    gates = np.stack([ga, gv], axis=1).reshape(16, P, 1024)
    attn_out = x["w_attn_out"][0].reshape(2, 4, 64, D).transpose(1, 0, 2, 3).reshape(512, D)
    branch = np.concatenate([row_tiles(attn_out), row_tiles(x["w_conv_out"][0])], axis=2)
    peer_u = x["peer_u"][0].reshape(P, KEYS, KB, P).transpose(1, 3, 2, 0).reshape(KEYS, P, 1024)
    peer_v = half_groups(x["peer_v"][0].reshape(P, KEYS, D).transpose(1, 0, 2).reshape(P * KEYS, D))
    w_l = x["mlstm_w_in_2"][0]
    pad = z((D, 28), f32)
    gate_cols = np.concatenate([w_l[:, 3072:3076], pad, w_l[:, 3076:3080], z((D, 92), f32)], axis=1)
    l_tiles = row_tiles(w_l[:, 0:3072])

    def mlp(layer):
        w1, w2 = row_tiles(x["mlp_w1_2"][layer]), half_groups(x["mlp_w2_2"][layer])
        parts = [w1[0:4]]
        for g in range(7):
            parts += [w1[4 * g + 4:4 * g + 8], w2[4 * g:4 * g + 4]]
        return parts + [w2[28:32]]

    pool = x["pool_w_2"][0].reshape(4, 2, P, 2, P).transpose(0, 3, 2, 1, 4)
    pool = pool.reshape(2, 4, P, 256).transpose(0, 2, 1, 3).reshape(2, P, 1024)
    mem = row_tiles(x["mem_w_kv_2"])
    stream = [k, q, v, conv, gates, branch, row_tiles(x["w_mix_out"][0]), row_tiles(x["peer_w_q"][0]), peer_u,
              mem[0:8], peer_v, mem[8:16], l_tiles[0:8], row_tiles(gate_cols), l_tiles[8:16], l_tiles[16:24],
              row_tiles(x["mlstm_w_out_2"][0])]
    for layer in range(2):
        if layer:
            stream.append(pool)
        stream += [row_tiles(x["xattn_wq_2"][layer]), row_tiles(x["xattn_wo_2"][layer])] + mlp(layer)
    a["stream"] = np.concatenate(stream, axis=0)
    assert a["stream"].shape[0] == NTILES
    a["wmod"] = row_tiles(x["w_mod"][0])
    a["xT"] = x["x"][0].T
    a["ctxT"] = x["ctx"][0].T
    a["memT"] = x["mem_2"][0].T
    a["keysT"] = x["peer_sub_keys"][0].reshape(HP, KEYS, P).transpose(2, 0, 1)
    gate_b = z((P, 1), f32)
    gate_b[0:4, 0] = x["mlstm_gate_b_2"][0, 0:4]
    gate_b[32:36, 0] = x["mlstm_gate_b_2"][0, 4:8]
    vec = {
        "b_mod": columns(x["b_mod"][0]), "n1": columns(x["norm1_g"][0]), "n2": columns(x["norm2_g"][0]),
        "final": columns(x["final_g"]), "conv": columns(x["conv_w"][0]), "mconv": columns(x["mlstm_conv_w_2"][0]),
        "mnorm": columns(x["mlstm_norm_g_2"][0]), "gate_b": gate_b, "pscale": columns(x["pool_scale_2"][0]),
        "b1": columns(x["mlp_b1_2"]), "b2": columns(x["mlp_b2_2"]), "ln_g": columns(x["ln_g_2"]),
        "ln_b": columns(x["ln_b_2"]), "sink": np.broadcast_to(x["attn_sink"], (P, 8)),
        "c": np.stack([columns(x["c"][0]), columns(x["c_ctx"])], axis=2).reshape(P, 16),
    }
    a["vecs"] = np.concatenate([vec[name] for name in _VEC], axis=1)
    a["consts"] = shape_constants()
    return {name: np.ascontiguousarray(v) for name, v in a.items()}


def kernel(**inputs):
    import concourse.bacc as bacc
    from concourse.bass_utils import run_bass_kernel_spmd

    arrays = layout({name: np.asarray(v) for name, v in inputs.items()})
    nc = bacc.Bacc("TRN2", target_bir_lowering=False, num_devices=1, dynamic_dma_scratch_size=1024)
    aps = {name: nc.dram_tensor(f"in_{name}", v.shape, mybir.dt.from_np(v.dtype), kind="ExternalInput").ap()
           for name, v in arrays.items()}
    out = nc.dram_tensor("outT", (D, T), F32, kind="ExternalOutput").ap()
    build(nc, aps, out)
    r = run_bass_kernel_spmd(nc, [{f"in_{name}": v for name, v in arrays.items()}], core_ids=[0])
    return np.ascontiguousarray(r.results[0]["outT"].T)[None]
```

```python
from contextlib import ExitStack

import concourse.bass as bass
from concourse import mybir
import numpy as np

ALU = mybir.AluOpType
ACT = mybir.ActivationFunctionType
AX = mybir.AxisListType
F32 = mybir.dt.float32
F32R = mybir.dt.float32r
U32 = mybir.dt.uint32

P = 128
D = 1024
KB = D // P
T = 512
TT = T // P
CT = 256
EPS = 1e-6
LN_EPS = 1e-5
ALPHA = (2 * 2) ** 0.25
RING = 4
ROPE_BASE = 10000.0
GRID_W = 64
PAIRS = 16
TOPK = 16
HP = 16
KEYS = 128
TB = 32
TBS = T // TB
FF = 4096
WINDOWS = (2, 4, 8, 16)
MIX_ORDER = (1, 0, 3, 2, 5, 4, 7, 6)
NEG = -1e30
ARENA = 13320
LOWEST = -3e38

_VEC = {}
_at = 0
for _name, _n in (("b_mod", 48), ("n1", 8), ("n2", 8), ("final", 8), ("conv", 12), ("mconv", 32), ("mnorm", 8),
                  ("gate_b", 1), ("pscale", 8), ("b1", 64), ("b2", 16), ("ln_g", 48), ("ln_b", 48), ("sink", 8),
                  ("c", 16)):
    _VEC[_name] = (_at, _n)
    _at += _n
NVEC = _at
_CONST = {}
_at = 0
for _name, _n in (("ident", P), ("ones", P), ("perm", P), ("iota", P), ("utri", P), ("band", 3 * P), ("cos", T),
                  ("sin", T), ("cnt", 4 * 16)):
    _CONST[_name] = (_at, _n)
    _at += _n
NCONST = _at


def plan():
    sections = {}
    n = 0
    done = []
    early = 0

    def tile(outs):
        nonlocal n, early
        for j in range(outs):
            if j + 1 < outs:
                early += 1
                done.append(("early", early))
            else:
                n += 1
                done.append(("tile", n))

    def section(name, tiles):
        nonlocal early
        sections[name] = (n, len(done))
        for outs in tiles:
            if outs < 0:
                for _ in range(-outs):
                    early += 1
                    done.append(("early", early))
            else:
                tile(outs)

    section("in", [2] + [1] * 4 + [2])
    for i in range(12):
        section(f"conv{i}", [1] + [-1] * (i >= 2))
    section("gates", [1, -1] * 16)
    section("tail", [-1] * 6)
    section("branch", [2] * 8)
    section("mix", [1] * 8)
    section("pq", [1] * 16)
    section("pu", [1] * 128)
    section("memk", [1] * 8)
    section("pv", [2] * 128)
    section("memv", [1] * 8)
    section("lstm", [1] * 17)
    section("core", [1, 1, -2] * 4)
    section("lout", [1] * 8)
    for layer in range(2):
        if layer:
            section("pool", [4] * 2)
        section(f"xq{layer}", [1] * 4 + ([-2] + [1] * 2) * 2 + [-2, -2])
        section(f"xo{layer}", [1] * 8)
        section(f"mlp{layer}", [1] * 4 + ([1] * 4 + [2] * 4) * 7 + [2] * 4)
    return sections, done, n


SECTIONS, DONE, NTILES = plan()

SEMAPHORES = (
    "tile_done", "early_done", "bank_free0", "bank_free1", "bank_free2", "bank_free3", "w_loaded0", "w_loaded1",
    "w_loaded2", "w_loaded3", "w_split", "consts_in", "vecs_in", "ctx_in", "conds_in", "mod_dot", "mod_in0",
    "mod_in1", "mod_in2", "mod_in3", "x_in", "mod_used", "norm_out", "stored", "gates_stored0", "gates_stored1",
    "act_stored0", "act_stored1", "zeros_set", "w_upper", "values_turned", "values_copied", "summed", "stats_read",
    "sums_ready", "cond_ready", "split1", "split0", "rotated", "swapped", "scores_read", "scores_ready",
    "probs_ready", "turned_copied", "turned", "conv_split", "merge_split", "keys_in", "key_scores_copied",
    "key_scores", "split2", "picks_ready", "picks_copied", "picks_turned", "hot_ready", "quad_copied", "quad_done",
    "gated_split", "mem_split", "split3", "rows_ready", "decay_turned", "floor_read", "max_spread", "lstm_weighted",
    "qk_ready", "lstm_scores", "head_rms_read", "decay_copied", "lstm_den", "decay_arg", "floor_spread",
    "head_squares", "head_rms", "lstm_split", "pool_split", "x_scores_read", "x_scores", "x_probs", "x_turned_copied",
    "x_turned", "split4", "split5", "split6", "split7", "split8", "hidden_split", "squared", "inverse_ready",
    "root_ready", "mean_spread", "inverse_spread", "scaled", "affine_done", "mod_ready", "shift_ready", "attn_exp",
    "conv_in", "best_ready", "best_exp", "act_back0", "act_back1", "gate_back0", "gate_back1", "mem_in", "peer_added",
    "lconv_done", "lraw_zero", "gate_rows", "floor_arg", "decay", "head_inverse", "head_root", "head_inverse_spread",
    "pool_added", "x_shift", "x_exp", "mlp_start", "ppad_zero", "pool_step", "odd_split", "act_step", "dve_step",
)


def build(nc, a, out):
    ctx = ExitStack()
    with ctx:
        def sb(name, shape, dt=F32):
            return ctx.enter_context(nc.sbuf_tensor(name, shape, dt))

        sems = {name: ctx.enter_context(nc.semaphore(name)) for name in SEMAPHORES}

        def sem(name):
            return sems[name]

        w32 = sb("w32", [P, RING, 1024])
        whi = sb("whi", [P, RING, KB, P], F32R)
        wlo = sb("wlo", [P, RING, KB, P], F32R)
        zeros = sb("zeros", [P, 1])
        xres = sb("xres", [P, KB, T])
        xhi = sb("xhi", [P, KB, T], F32R)
        xlo = sb("xlo", [P, KB, T], F32R)
        yhi = sb("yhi", [P, KB, T], F32R)
        ylo = sb("ylo", [P, KB, T], F32R)
        acc = sb("acc", [P, KB, T])
        work = sb("work", [P, 8, T])
        consts = sb("consts", [P, NCONST])
        vecs = sb("vecs", [P, NVEC])
        mod = sb("mod", [P, 48, 2])
        gain = sb("gain", [P, 3, KB])
        arena = sb("arena", [P, ARENA])
        small = sb("small", [P, 92])
        stats = [small[:, 68 + 12 * j:80 + 12 * j] for j in range(2)]
        psum = ctx.enter_context(nc.psum_tensor("psum", [P, 8, 512], F32))
        gates_dram = nc.dram_tensor("gates_scratch", (TBS, P, KEYS, TB), F32, kind="Internal").ap()
        act_dram = nc.dram_tensor("act_scratch", (KEYS, P, T), F32, kind="Internal").ap()

        def const(name, rows=P):
            at, n = _CONST[name]
            return consts[0:rows, at:at + n]

        def vec(name, j, rows=P):
            return vecs[0:rows, _VEC[name][0] + j:_VEC[name][0] + j + 1]

        def vecr(name):
            at, n = _VEC[name]
            return vecs[:, at:at + n]

        ident, ones = const("ident"), const("ones")

        def ar(at, n):
            return arena[:, at:at + n]

        def tiles_of(at, *shape):
            n = int(np.prod(shape))
            names = "abc"[:len(shape)]
            sizes = dict(zip(names, shape))
            return ar(at, n).rearrange("p (" + " ".join(names) + ") -> p " + " ".join(names), **sizes)

        mod_w = tiles_of(0, 12, 1024)
        mod_pairs = [ar(0, 2048), ar(2048, 2048)] + [acc[:, 4 * j:4 * j + 4, :].rearrange("p k t -> p (k t)")
                                                     for j in range(2)]
        cond_rows = [acc[:, 4 * j:4 * j + 4, CT:2 * CT] for j in range(2)]
        cond_row = work[:, 4:6, :].rearrange("p a n -> p (a n)").rearrange("p (k n) -> p k n", n=CT)
        gv = tiles_of(0, KB, T)
        q_rope = tiles_of(4096, 4, T)
        k_rope = ar(6144, T)
        k_ctx = ar(6656, CT)
        v_tok = tiles_of(6912, TT, P)
        v_ctx = tiles_of(7424, 2, P)
        zpad = tiles_of(7680, 2, T + 2)
        cgate = tiles_of(7680 + 1028, 2, T)
        probs = tiles_of(9732, 2, 640)
        probsT = ar(11012, 640)
        sink8 = small[:, 60:68]
        scores_all = tiles_of(0, TT, HP, KEYS)
        sub_keys = tiles_of(8192, HP, KEYS)
        picks = tiles_of(8192, TT, 3, P)
        picksT = tiles_of(10240, 3, T)
        flat_acc = acc[:, :, :].rearrange("p k t -> p (k t)")
        cand = flat_acc[:, 0:2048]
        look = flat_acc[:, 2048:4096]
        hot = flat_acc[:, 0:2048].rearrange("p (s two n) -> p s two n", s=8, two=2)
        stage = tiles_of(0, 2, KEYS, TB)
        ga_act = tiles_of(0, 2, 4, T)
        ga_gate = tiles_of(4096, 2, 4 * T)
        flat_work = work[:, 2:8, :].rearrange("p k t -> p (k t)")
        top_v = flat_work[:, 0:256]
        top_i = flat_work[:, 256:512]
        top_f = flat_work[:, 512:768]
        best = flat_work[:, 768:896]
        best_pos = flat_work[:, 896:1024]
        best_row = flat_work[:, 1024:1152]
        best_e = flat_work[:, 1536:2048]
        best_sum = flat_work[:, 2048:2056]
        memT = look.rearrange("p (k t) -> p k t", k=KB)
        mem_raw = tiles_of(12288, 2, CT)
        mv = tiles_of(8192, 2, D)
        mk = tiles_of(10240, KB, CT)
        lq, lk = tiles_of(0, 4, T), tiles_of(2048, 4, T)
        lv = tiles_of(4096, TT, D)
        lraw = tiles_of(12288, 2, T + 3)
        lsig = tiles_of(12288, 2, T)
        lp = work[:, 4:8, :]
        arow, irow = work[0:4, 6, :], work[0:4, 7, :]
        frow, mrow = const("cos", 4), const("sin", 4)
        acol = small[:, 44:60]
        xq = tiles_of(0, KB, T)
        xp = tiles_of(4096, TT, CT)
        xpT = tiles_of(5120, 2, T)
        ppad = tiles_of(6144, 2, T + 16)
        pool_y = tiles_of(0, 2, T)
        ppad_odd = tiles_of(1024, 2, T + 16)
        pool_y_odd = ar(1024 + 2 * (T + 16), T)

        def unit(u):
            m, g, qt = u // 8, u // 4 % 2, u % 4
            return m, g, qt, max(0, qt - 1), min(TT - 1, qt + 1)

        def bank(b):
            return psum[:, b, :]

        def conv_out(i):
            return SECTIONS[f"conv{i}"][1]

        def attn_product(u):
            if u < 10:
                return SECTIONS[f"conv{u + 2}"][1] + 1
            return SECTIONS["gates"][1] + 2 * (u - 10) + 1 if u < 26 else SECTIONS["tail"][1] + u - 26

        def x_value_out(i):
            return SECTIONS[f"xq{i // 4}"][1] + (4, 8, 12, 14)[i % 4] + 1

        def wide(b, n):
            return psum[:, b:b + (n + 511) // 512, :].rearrange("p b n -> p (b n)")[:, 0:n]

        tile_done, early_done = sem("tile_done"), sem("early_done")
        bank_free = [sem(f"bank_free{b}") for b in range(RING)]
        w_loaded = [sem(f"w_loaded{s}") for s in range(RING)]
        w_split = sem("w_split")

        def first_tile(section):
            return SECTIONS[section][0]

        def wait_product(eng, o, shift=0):
            kind, count = DONE[o]
            eng.wait_ge(tile_done if kind == "tile" else early_done, count + shift)

        def wait_bank(eng, o, shift=0):
            if o >= RING:
                eng.wait_ge(bank_free[o % RING], o // RING + shift)

        def free(ins, o):
            ins.then_inc(bank_free[o % RING], 1)

        def wait_read(eng, o, shift=0):
            eng.wait_ge(bank_free[o % RING], o // RING + 1 + shift)

        class Steps:

            def __init__(self, eng, name):
                self.eng, self.sem, self.n, self.turn = eng, sem(name), 0, 0

            def __call__(self, ins):
                ins.then_inc(self.sem, 1)
                self.n += 1

            def settle(self):
                self.eng.wait_ge(self.sem, self.turn + self.n)

        def mix_window(eng, step, k, pad, y, fused):
            w = WINDOWS[k // 2]
            x = xres[:, k, :]
            step(eng.tensor_tensor(pad[:, 0, 17:], x[:, 1:T], x[:, 0:T - 1], ALU.add))
            step(eng.tensor_copy(pad[:, 0, 16:17], x[:, 0:1]))
            step.settle()
            at, shift = 0, 2
            while shift < w:
                step(eng.tensor_tensor(pad[:, 1 - at, 16:], pad[:, at, 16:], pad[:, at, 16 - shift:16 - shift + T],
                                       ALU.add))
                step.settle()
                at, shift = 1 - at, 2 * shift
            if fused:
                step(eng.scalar_tensor_tensor(y[:, 16:T], pad[:, at, 32:], 1.0 / w, x[:, 16:T], ALU.mult,
                                              ALU.subtract))
            else:
                step(eng.tensor_scalar(y[:, 16:T], pad[:, at, 32:], 1.0 / w, None, ALU.mult))
                step.settle()
                step(eng.tensor_tensor(y[:, 16:T], y[:, 16:T], x[:, 16:T], ALU.subtract))
            c0 = _CONST["cnt"][0] + 16 * (k // 2)
            step(eng.tensor_tensor(y[:, 0:16], pad[:, at, 16:32], consts[:, c0:c0 + 16], ALU.mult))
            step.settle()
            step(eng.tensor_tensor(y[:, 0:16], y[:, 0:16], x[:, 0:16], ALU.subtract))
            step.settle()

        block = ctx.enter_context(nc.Block())

        @block.sync
        def _(sp):
            sp.dma_start(consts[:, :], a["consts"]).then_inc(sem("consts_in"), 16)
            sp.dma_start(vecs[:, :], a["vecs"]).then_inc(sem("vecs_in"), 16)
            conds = a["conds"].rearrange("a (k n) -> a k n", n=CT)
            sp.dma_start(acc[:, :, CT:2 * CT], conds.broadcast_to((P, 8, CT))).then_inc(sem("conds_in"), 16)
            sp.dma_start(acc[:, :, 0:CT], a["ctxT"].rearrange("(k p) t -> p k t", p=P)).then_inc(sem("ctx_in"), 16)
            sp.dma_start(xres[:, :, :], a["xT"].rearrange("(k p) t -> p k t", p=P)).then_inc(sem("x_in"), 16)
            for g in range(4):
                if g == 3:
                    sp.wait_ge(sem("mod_used"), 2)
                    sp.wait_ge(sem("mod_dot"), 4)
                sp.dma_start(mod_w[:, 4 * (g % 3):4 * (g % 3) + 4, :], a["wmod"][4 * g:4 * g + 4]
                             .rearrange("a p n -> p a n")).then_inc(sem(f"mod_in{g}"), 16)
                if g == 0:
                    for s in range(RING):
                        sp.dma_start(w32[:, s, :], a["stream"][s]).then_inc(w_loaded[s], 16)
            whole = NTILES // RING
            with sp.Fori(1, whole) as g:
                for s in range(RING):
                    sp.wait_ge(w_split, g * RING + (s + 1 - RING))
                    sp.dma_start(w32[:, s, :], a["stream"][bass.ds(g * RING + s, 1)].rearrange("a p n -> (a p) n"))\
                        .then_inc(w_loaded[s], 16)
            for n in range(whole * RING, NTILES):
                sp.wait_ge(w_split, n + 1 - RING)
                sp.dma_start(w32[:, n % RING, :], a["stream"][n]).then_inc(w_loaded[n % RING], 16)
            for k in range(KB):
                sp.wait_ge(sem("norm_out"), k + 1)
                sp.dma_start(out[k * P:(k + 1) * P, :], xres[:, k, :]).then_inc(sem("stored"), 16)
            sp.wait_ge(sem("stored"), 16 * KB)
            sp.wait_ge(sem("gates_stored0"), 8 * TBS)
            sp.wait_ge(sem("gates_stored1"), 8 * TBS)
            sp.wait_ge(sem("act_stored0"), 16 * KEYS // 2)
            sp.wait_ge(sem("act_stored1"), 16 * KEYS // 2)

        @block.gpsimd
        def _(pool):
            pool.memset(zeros[:, :], 0.0).then_inc(sem("zeros_set"), 1)
            pool.wait_ge(sem("zeros_set"), 1)

            def split_tile(s, n, nth, reused):
                pool.wait_ge(w_loaded[s], nth * 16)
                if reused:
                    pool.wait_ge(tile_done, n + 1 - RING)
                hi = whi[:, s, :, :].rearrange("p k n -> p (k n)")
                lo = wlo[:, s, :, :].rearrange("p k n -> p (k n)")
                pool.tensor_tensor(hi, w32[:, s, :], zeros[:, :].broadcast_to((P, 1024)), ALU.add)\
                    .then_inc(sem("w_upper"), 1)
                pool.wait_ge(sem("w_upper"), n + 1)
                pool.tensor_tensor(lo, w32[:, s, :], hi.bitcast(F32), ALU.subtract).then_inc(w_split, 1)

            for s in range(RING):
                split_tile(s, s, 1, False)

            def split_tiles(first, end):
                up, down = -(-first // RING), end // RING
                for n in range(first, up * RING):
                    split_tile(n % RING, n, n // RING + 1, True)
                with pool.Fori(up, down) as g:
                    for s in range(RING):
                        split_tile(s, g * RING + s, g + 1, True)
                for n in range(down * RING, end):
                    split_tile(n % RING, n, n // RING + 1, True)

            mixed = first_tile("pool") + RING
            split_tiles(RING, mixed)
            step = Steps(pool, "pool_step")
            pool.wait_ge(sem("affine_done"), 8 * 6 + 1)
            step(pool.memset(ppad_odd[:, :, 0:16], 0.0))
            step.settle()
            for i in range(0, 6, 2):
                k = MIX_ORDER[i]
                pool.wait_ge(sem("affine_done"), 8 * 6 + i + 1)
                mix_window(pool, step, k, ppad_odd, pool_y_odd, False)
                step(pool.tensor_tensor(yhi[:, k, :], pool_y_odd, zeros[:, :].broadcast_to((P, T)), ALU.add))
                step.settle()
                pool.tensor_tensor(ylo[:, k, :], pool_y_odd, yhi[:, k, :].bitcast(F32), ALU.subtract)\
                    .then_inc(sem("odd_split"), 1)
                pool.wait_ge(sem("odd_split"), i // 2 + 1)
            split_tiles(mixed, NTILES)

        @block.tensor
        def _(pe):
            def feature_product(dst, s, xh, xl, ks, w0=0, ready=None, last_sem=None):
                for j, k in enumerate(ks):
                    if ready is not None:
                        pe.wait_ge(ready[0], ready[1] + k + 1)
                    hi, lo = whi[:, s, w0 + j, :], wlo[:, s, w0 + j, :]
                    pe.matmul(dst, hi, xh(k), start=(j == 0), stop=False)
                    pe.matmul(dst, hi, xl(k), start=False, stop=False)
                    mm = pe.matmul(dst, lo, xh(k), start=False, stop=(j == len(ks) - 1))
                mm.then_inc(last_sem, 1)

            XH, XL = (lambda k: xhi[:, k, :]), (lambda k: xlo[:, k, :])
            YH, YL = (lambda k: yhi[:, k, :]), (lambda k: ylo[:, k, :])
            CH, CL = (lambda k: yhi[:, k, 0:CT]), (lambda k: ylo[:, k, 0:CT])

            def linear(n, o, XH=XH, XL=XL, cols=T, ready=None):
                pe.wait_ge(w_split, n + 1)
                wait_bank(pe, o)
                feature_product(bank(o % RING)[:, 0:cols], n % RING, XH, XL, range(KB), ready=ready,
                                last_sem=tile_done)

            def linear_group(n, outs, ready):
                pe.wait_ge(w_split, n + len(outs))
                for oo in outs:
                    wait_bank(pe, oo)
                for k in range(KB):
                    pe.wait_ge(ready[0], ready[1] + k + 1)
                    for m, oo in enumerate(outs):
                        dst, s = bank(oo % RING), (n + m) % RING
                        pe.matmul(dst, whi[:, s, k, :], XH(k), start=(k == 0), stop=False)
                        pe.matmul(dst, whi[:, s, k, :], XL(k), start=False, stop=False)
                        mm = pe.matmul(dst, wlo[:, s, k, :], XH(k), start=False, stop=(k == KB - 1))
                        if k == KB - 1:
                            mm.then_inc(tile_done, 1)

            def norm_sums(ni, cols=T, mean=False):
                pe.wait_ge(sem("summed"), 8 * (ni + 1))
                if ni:
                    pe.wait_ge(sem("stats_read"), ni)
                for c in range(cols // P):
                    t = slice(c * P, (c + 1) * P)
                    if mean:
                        pe.matmul(bank(4)[:, 4 + c:5 + c], work[:, 4, t], ones[:, 0:1], start=True, stop=True)
                    mm = pe.matmul(bank(4)[:, c:c + 1], work[:, 5, t], ones[:, 0:1], start=True, stop=True)
                mm.then_inc(sem("sums_ready"), 1)
                if mean:
                    spread_means(ni, cols)

            def spread_means(ni, cols):
                pe.wait_ge(sem("stats_read"), ni + 1)
                spread(bank(4), stats[ni % 2][:, 4:8], cols).then_inc(sem("mean_spread"), 1)

            def spread(dst, columns, cols):
                for c in range(cols // P):
                    mm = pe.matmul(dst[:, c * P:(c + 1) * P], columns[:, c:c + 1].broadcast_to((P, P)), ident,
                                   start=True, stop=True)
                return mm

            def norm_spread(ni, cols=T, to=5):
                pe.wait_ge(sem("root_ready"), ni + 1)
                spread(bank(to), stats[ni % 2][:, 0:4], cols).then_inc(sem("inverse_spread"), 1)

            cond = small[:, 0:16].rearrange("p (k two) -> p k two", two=2)
            pe.wait_ge(sem("consts_in"), 16)
            norm_sums(0, CT)
            pe.wait_ge(sem("cond_ready"), 1)

            def mod_product_of(dst, w, signal):
                w = w.rearrange("p (k n) -> p k n", k=KB)
                for k in range(KB):
                    mm = pe.matmul(dst, w[:, k, :], cond[:, k, :], start=(k == 0), stop=(k == KB - 1))
                mm.then_inc(signal, 1)

            for t in range(16):
                if t % 4 >= 2:
                    continue
                if t % 4 == 0:
                    pe.wait_ge(sem(f"mod_in{t // 4}"), 16)
                mod_product_of(bank(6)[:, 2 * t:2 * t + 2], mod_w[:, t % 12, :], sem("mod_used"))
                if t == 1:
                    norm_spread(0, CT, to=7)
                    norm_sums(1)
            norm_spread(1)

            n, o = SECTIONS["in"]
            NX, NC = (sem("split1"), 0), (sem("split0"), 0)

            def both(n, o, product_x, product_c):
                pe.wait_ge(w_split, n + 1)
                wait_bank(pe, o)
                product_c(bank(o % RING)[:, 0:CT], early_done)
                wait_bank(pe, o + 1)
                product_x(bank((o + 1) % RING), tile_done)

            pe.wait_ge(w_split, n + 1)
            feature_product(bank(o % RING)[:, 0:CT], n % RING, CH, CL, range(KB), ready=NC, last_sem=early_done)
            linear_group(n, [o + 1, o + 2, o + 3], NX)

            def rotate(i):
                wait_read(pe, SECTIONS["in"][1] + 1 + i)
                if i:
                    pe.wait_ge(sem("rotated"), i)
                pe.matmul(bank(6), const("perm"), work[:, i % 2, :], start=True, stop=True)\
                    .then_inc(sem("swapped"), 1)

            rotate(0)
            linear(n + 3, o + 4)
            rotate(1)
            linear(n + 4, o + 5)
            rotate(2)
            both(n + 5, o + 6, lambda d, m: feature_product(d, (n + 5) % RING, XH, XL, range(KB), last_sem=m),
                 lambda d, m: feature_product(d, (n + 5) % RING, CH, CL, range(KB), last_sem=m))
            rotate(3)
            rotate(4)

            def turn_values(src, tiles, dst):
                for t in range(tiles):
                    mm = pe.transpose(dst[:, t * P:(t + 1) * P], src[:, t * P:(t + 1) * P], ident)
                mm.then_inc(sem("values_turned"), 1)

            wait_read(pe, o + 6)
            turn_values(work[:, 1, :], CT // P, bank(7))
            wait_read(pe, o + 7)
            pe.wait_ge(sem("values_copied"), 1)
            turn_values(work[:, 0, :], TT, bank(7))

            def attn_scores(u):
                m, g, qt, lo, hi = unit(u)
                rows = slice(64 * g, 64 * g + 64)
                if u:
                    pe.wait_ge(sem("scores_read"), u)
                qs = q_rope[rows, m, qt * P:(qt + 1) * P]
                for j, kt in enumerate(range(lo, hi + 1)):
                    pe.matmul(wide(4, 640)[:, j * P:(j + 1) * P], qs, k_rope[rows, kt * P:(kt + 1) * P],
                              start=True, stop=True)
                nl = hi - lo + 1
                for j in range(2):
                    c = (nl + j) * P
                    mm = pe.matmul(wide(4, 640)[:, c:c + P], qs, k_ctx[rows, j * P:(j + 1) * P], start=True, stop=True)
                mm.then_inc(sem("scores_ready"), 1)

            def attn_turn(u):
                m, g, qt, lo, hi = unit(u)
                nk = hi - lo + 3
                pe.wait_ge(sem("probs_ready"), u + 1)
                if u:
                    pe.wait_ge(sem("turned_copied"), u)
                for j in range(nk):
                    mm = pe.transpose(wide(6, 640)[:, j * P:(j + 1) * P], probs[:, u % 2, j * P:(j + 1) * P], ident)
                mm.then_inc(sem("turned"), 1)

            def attn_values(u):
                m, g, qt, lo, hi = unit(u)
                rows = slice(64 * g, 64 * g + 64)
                pe.wait_ge(sem("turned_copied"), u + 1)
                o = attn_product(u)
                wait_bank(pe, o)
                for j, kt in enumerate(list(range(lo, hi + 1)) + [0, 1]):
                    vs = (v_tok[:, kt, 64 * g:64 * g + 64] if j < hi - lo + 1 else v_ctx[:, kt, 64 * g:64 * g + 64])
                    mm = pe.matmul(psum[rows, o % RING, 0:P], vs, probsT[:, j * P:(j + 1) * P],
                                   start=(j == 0), stop=(j == hi - lo + 2))
                mm.then_inc(early_done, 1)

            def attn_slot(i):
                if i < 32:
                    if i == 0:
                        pe.wait_ge(sem("rotated"), 5)
                        wait_read(pe, SECTIONS["in"][1])
                        pe.wait_ge(sem("values_copied"), 2)
                    attn_scores(i)
                if 1 <= i <= 32:
                    attn_turn(i - 1)
                if 2 <= i <= 33:
                    attn_values(i - 2)

            for i in range(12):
                linear(SECTIONS[f"conv{i}"][0], conv_out(i))
                attn_slot(i)
            n, o = SECTIONS["gates"]
            for i in range(16):
                linear(n + i, o + 2 * i)
                attn_slot(12 + i)
            for i in range(28, 34):
                attn_slot(i)
            n, o = SECTIONS["branch"]
            for u in range(28, 32):
                wait_read(pe, attn_product(u))
            pe.wait_ge(sem("conv_split"), 4)
            for m in range(KB):
                pe.wait_ge(w_split, n + m + 1)
                for j, done in ((0, early_done), (1, tile_done)):
                    wait_bank(pe, o + 2 * m + j)
                    feature_product(bank((o + 2 * m + j) % RING), (n + m) % RING, YH, YL, range(4 * j, 4 * j + 4),
                                    w0=4 * j, last_sem=done)
            n, o = SECTIONS["mix"]
            for m in range(KB):
                linear(n + m, o + m, ready=(sem("merge_split"), 0) if m == 0 else None)
            norm_sums(2)
            norm_spread(2)

            n, o = SECTIONS["pq"]

            def key_scores(m):
                wait_read(pe, SECTIONS["pq"][1] + m)
                if m == 0:
                    pe.wait_ge(sem("keys_in"), 16)
                if m:
                    pe.wait_ge(sem("key_scores_copied"), m)
                for t in range(TT):
                    mm = pe.matmul(bank(6)[:, t * P:(t + 1) * P], acc[:, m % 2, t * P:(t + 1) * P], sub_keys[:, m, :],
                                   start=True, stop=True)
                mm.then_inc(sem("key_scores"), 1)

            linear_group(n, range(o, o + 4), (sem("split2"), 0))
            for m in range(3):
                key_scores(m)
            for m in range(4, HP):
                linear(n + m, o + m)
                key_scores(m - 1)
            key_scores(HP - 1)

            n, o = SECTIONS["pu"]

            def expert_inputs(g, k, n0, o0):
                pe.wait_ge(w_split, g * RING + (n0 + k + 1))
                wait_bank(pe, o0 + k, g)
                feature_product(bank((o0 + k) % RING), (n0 + k) % RING, XH, XL, range(KB), last_sem=tile_done)

            with pe.Fori(0, 16) as g:
                for k in range(RING):
                    expert_inputs(g, k, n, o)
            for tt in range(TT):
                for j in range(3):
                    pe.wait_ge(sem("picks_ready"), tt + 1)
                    i = 3 * tt + j
                    if i >= 2:
                        pe.wait_ge(sem("picks_copied"), i - 1)
                    pe.transpose(bank(6 + i % 2)[:, 0:P], picks[:, tt, j, :], ident).then_inc(sem("picks_turned"), 1)

            def gate_turn(g, half, first):
                for k in range(RING):
                    t0 = 64 + 4 * half
                    nn, oo = n + t0 + k, o + t0 + k
                    pe.wait_ge(w_split, g * 8 + (nn + 1))
                    wait_bank(pe, oo, g * 2)
                    feature_product(bank(oo % RING), nn % RING, XH, XL, range(KB), last_sem=tile_done)
                    for q in range(2 * k, 2 * k + 2):
                        pe.wait_ge(sem("hot_ready"), g * 16 + (8 * half + q + 1))
                        if not (first and q < 2):
                            pe.wait_ge(sem("quad_copied"), g * 16 + (8 * half + q - 1))
                        for r in range(4):
                            slot = (4 * q + r) % 8
                            mm = pe.matmul(bank(6 + q % 2)[:, r * P:(r + 1) * P], hot[:, slot, 0, :],
                                           hot[:, slot, 1, :], start=True, stop=True)
                        mm.then_inc(sem("quad_done"), 1)

            gate_turn(0, 0, True)
            gate_turn(0, 1, False)
            with pe.Fori(1, 8) as g:
                gate_turn(g, 0, False)
                gate_turn(g, 1, False)

            n, o = SECTIONS["memk"]
            MH, ML = (lambda k: xhi[:, k, 0:CT]), (lambda k: xlo[:, k, 0:CT])
            for m in range(KB):
                linear(n + m, o + m, MH, ML, CT, ready=(sem("mem_split"), 0) if m == 0 else None)

            n, o = SECTIONS["pv"]

            def half_group_out(turn_tiles, turn_outs, n0, o0, half, ready, ready_count):
                for k in range(4):
                    if k == 0:
                        pe.wait_ge(ready, ready_count)
                    pe.wait_ge(w_split, turn_tiles + (n0 + k + 1))
                    for j, done in ((0, early_done), (1, tile_done)):
                        oo = o0 + 2 * k + j
                        wait_bank(pe, oo, turn_outs)
                        feature_product(bank(oo % RING), (n0 + k) % RING, YH, YL, range(4 * half, 4 * half + 4),
                                        w0=4 * j, last_sem=done)

            with pe.Fori(0, 16) as g:
                for half in range(2):
                    half_group_out(g * 8, g * 4, n + 4 * half, o + 8 * half, half, sem("gated_split"),
                                   g * 8 + 4 * (half + 1))

            n, o = SECTIONS["memv"]

            def turn_copied(m, o, src, tiles, turned):
                wait_read(pe, o + m)
                if m >= 2:
                    pe.wait_ge(sem("values_copied"), turned + m - 1)
                turn_values(src[:, m % 2, :], tiles, bank(6 + m % 2))

            for m in range(KB):
                linear(n + m, o + m, MH, ML, CT)
                if m:
                    turn_copied(m - 1, o, mem_raw, CT // P, 2)
                if m == 4:
                    norm_sums(3)
                if m == 5:
                    norm_spread(3)
            turn_copied(7, o, mem_raw, CT // P, 2)

            n, o = SECTIONS["lstm"]
            linear_group(n, range(o, o + 2), (sem("split3"), 0))
            pe.wait_ge(sem("values_copied"), 10)
            for m in range(2, 17):
                linear(n + m, o + m)
                if m > 9:
                    turn_copied(m - 10, o + 9, work, TT, 10)
            turn_copied(7, o + 9, work, TT, 10)
            pe.wait_ge(sem("values_copied"), 18)
            pe.wait_ge(sem("rows_ready"), 1)
            for t in range(TT):
                mm = pe.transpose(bank(7)[:, 4 * t:4 * t + 4], arow[:, t * P:(t + 1) * P], const("ident", 4)[:, 0:4])
            mm.then_inc(sem("decay_turned"), 1)
            n, o = SECTIONS["core"]
            def head_sums(h):
                pe.wait_ge(sem("head_squares"), 2 * h + 2)
                pe.wait_ge(sem("floor_read"), h + 1)
                for c in range(TT):
                    for j in range(2):
                        mm = pe.matmul(bank(7)[:, c:c + 1], work[:, j, c * P:(c + 1) * P], ones[:, 0:1],
                                       start=(j == 0), stop=(j == 1))
                mm.then_inc(sem("head_rms"), 1)

            def head_spread(h):
                pe.wait_ge(sem("head_root"), h + 1)
                spread(bank(5), stats[0][:, 0:4], T).then_inc(sem("head_inverse_spread"), 1)

            def lstm_scores(h, st):
                i = 4 * h + st
                if st >= 2:
                    pe.wait_ge(sem("lstm_weighted"), i - 1)
                elif h and st:
                    pe.wait_ge(sem("floor_read"), h)
                elif h >= 2:
                    pe.wait_ge(sem("lstm_split"), 2 * h - 2)
                elif h:
                    pe.wait_ge(sem("lstm_weighted"), 4)
                if i == 0:
                    pe.wait_ge(sem("qk_ready"), 8)
                c = slice(st * P, T)
                pe.matmul(bank(5 + st % 2)[:, c], lk[:, h, st * P:(st + 1) * P], lq[:, h, c],
                          start=True, stop=True).then_inc(sem("lstm_scores"), 1)

            for h in range(4):
                pick = const("ident", 4)[:, h:h + 1].broadcast_to((4, P))
                if h:
                    pe.wait_ge(sem("decay_arg"), 4 * h)
                pe.matmul(bank(4), pick, mrow, start=True, stop=True).then_inc(sem("max_spread"), 1)
                lstm_scores(h, 0)
                lstm_scores(h, 1)
                linear(n + 2 * h, o + 4 * h)
                if h:
                    head_sums(h - 1)
                lstm_scores(h, 2)
                lstm_scores(h, 3)
                linear(n + 2 * h + 1, o + 4 * h + 1)
                pe.wait_ge(sem("lstm_weighted"), 4 * h + 4)
                if h:
                    head_spread(h - 1)
                    pe.wait_ge(sem("head_rms_read"), h)
                else:
                    pe.wait_ge(sem("decay_copied"), 1)
                for st in range(TT):
                    c = slice(st * P, T)
                    mm = pe.matmul(bank(7)[:, c], ones, lp[:, st, c], start=(st == 0), stop=(st == TT - 1))
                mm.then_inc(sem("lstm_den"), 1)
                pe.matmul(bank(6), pick, frow, start=True, stop=True).then_inc(sem("floor_spread"), 1)
                for j in range(2):
                    oo = o + 4 * h + 2 + j
                    wait_bank(pe, oo)
                    for st in range(TT):
                        c = slice(st * P, T)
                        f = (2 * h + j) * P
                        mm = pe.matmul(bank(oo % RING)[:, c], lv[:, st, f:f + P], lp[:, st, c],
                                       start=(st == 0), stop=(st == TT - 1))
                    mm.then_inc(early_done, 1)
            n, o = SECTIONS["lout"]

            def lstm_out(m, ks):
                if ks[0] == 0:
                    pe.wait_ge(w_split, n + m + 1)
                    wait_bank(pe, o + m)
                pe.wait_ge(sem("lstm_split"), ks[-1] + 1)
                dst, s = bank((o + m) % RING), (n + m) % RING
                for k in ks:
                    pe.matmul(dst, whi[:, s, k, :], YH(k), start=(k == 0), stop=False)
                    pe.matmul(dst, whi[:, s, k, :], YL(k), start=False, stop=False)
                    mm = pe.matmul(dst, wlo[:, s, k, :], YH(k), start=False, stop=(k == KB - 1))
                if ks[-1] == KB - 1:
                    mm.then_inc(tile_done, 1)

            lstm_out(0, range(0, 6))
            lstm_out(1, range(0, 6))
            head_sums(3)
            lstm_out(2, range(0, 6))
            head_spread(3)
            lstm_out(3, range(0, 6))
            for m in range(4):
                lstm_out(m, range(6, 8))
            for m in range(4, KB):
                lstm_out(m, range(KB))
            norm_sums(4, mean=True)
            norm_spread(4)

            ni = 4
            for layer in range(2):
                if layer:
                    n, o = SECTIONS["pool"]
                    for m in range(KB):
                        if m % 4 == 0:
                            pe.wait_ge(w_split, n + m // 4 + 1)
                        wait_bank(pe, o + m)
                        if m % 2 == 0:
                            pe.wait_ge(sem("pool_split"), m // 2 + 1 if m < 6 else 5)
                            if m < 6:
                                pe.wait_ge(sem("odd_split"), m // 2 + 1)
                        feature_product(bank((o + m) % RING), (n + m // 4) % RING, YH, YL,
                                        range(2 * (m // 2), 2 * (m // 2) + 2), w0=2 * (m % 4),
                                        last_sem=tile_done if m % 4 == 3 else early_done)
                    norm_sums(7, mean=True)
                    norm_spread(7)
                    ni = 7
                n, o = SECTIONS[f"xq{layer}"]

                def x_scores(h):
                    i = 4 * layer + h
                    wait_read(pe, o + 2 * h + 1 + (0, 0, 2, 4)[h])
                    wait_read(pe, o + 2 * h + (0, 0, 2, 4)[h])
                    if i:
                        pe.wait_ge(sem("x_scores_read"), 4 * i)
                    for t in range(TT):
                        for j in range(2):
                            mm = pe.matmul(wide(4, 1024)[:, t * CT:(t + 1) * CT], xq[:, 2 * h + j, t * P:(t + 1) * P],
                                           mk[:, 2 * h + j, :], start=(j == 0), stop=(j == 1))
                        mm.then_inc(sem("x_scores"), 1)

                def x_turn(h):
                    i = 4 * layer + h
                    for t in range(TT):
                        pe.wait_ge(sem("x_probs"), 4 * i + t + 1)
                        if t == 0 and i:
                            pe.wait_ge(sem("x_turned_copied"), 2 * i)
                        for j in range(2):
                            mm = pe.transpose(bank(6 + j)[:, t * P:(t + 1) * P], xp[:, t % 4, j * P:(j + 1) * P],
                                              ident)
                        mm.then_inc(sem("x_turned"), 1)

                def x_values(h, o):
                    i = 4 * layer + h
                    pe.wait_ge(sem("x_turned_copied"), 2 * i + 2)
                    for j in range(2):
                        wait_bank(pe, o + j)
                        for mt in range(2):
                            f = (2 * h + j) * P
                            mm = pe.matmul(bank((o + j) % RING), mv[:, mt, f:f + P], xpT[:, mt, :],
                                           start=(mt == 0), stop=(mt == 1))
                        mm.then_inc(early_done, 1)

                linear_group(n, range(o, o + 4), (sem(f"split{ni}"), 0))
                for m in range(KB):
                    oo = o + m + (0 if m < 4 else 2 if m < 6 else 4)
                    if m >= 4:
                        linear(n + m, oo)
                    if m % 2:
                        h = m // 2
                        if h:
                            x_turn(h - 1)
                        x_scores(h)
                        if h:
                            x_values(h - 1, o + (4, 8, 12)[h - 1])
                x_turn(3)
                x_values(3, o + 14)
                n, o = SECTIONS[f"xo{layer}"]
                for m in range(KB):
                    if m == 0:
                        for j in range(4):
                            wait_read(pe, x_value_out(4 * layer + 3) - j)
                    linear(n + m, o + m, YH, YL)
                norm_sums(ni + 1, mean=True)
                norm_spread(ni + 1)
                n, o = SECTIONS[f"mlp{layer}"]
                hidden = sem("hidden_split")

                linear_group(n, range(o, o + 4), (sem(f"split{ni + 1}"), 0))
                def turn(g, half, last):
                    if not last:
                        for k in range(4):
                            nn, oo = n + 4 + 8 * half + k, o + 4 + 12 * half + k
                            pe.wait_ge(w_split, g * 16 + (nn + 1))
                            wait_bank(pe, oo, g * 6)
                            feature_product(bank(oo % RING), nn % RING, XH, XL, range(KB), last_sem=tile_done)
                    if last:
                        half_group_out(0, 0, n + 60, o + 88, half, hidden, 32 * layer + 32)
                    else:
                        half_group_out(g * 16, g * 6, n + 8 + 8 * half, o + 8 + 12 * half, half, hidden,
                                       g * 8 + (32 * layer + 4 * half + 4))

                with pe.Fori(0, 3) as g:
                    turn(g, 0, False)
                    turn(g, 1, False)
                turn(3, 0, False)
                turn(3, 1, True)
                norm_sums(ni + 2, mean=True)
                norm_spread(ni + 2)

        @block.scalar
        def _(act):
            step = Steps(act, "act_step")

            def squares(ni, src, cols=T, ready=None):
                for k in range(KB):
                    if ready is not None:
                        ready(k)
                    if k >= 2:
                        act.wait_ge(sem("summed"), 8 * ni + k - 1)
                    act.activation(work[:, k % 2, 0:cols], src(k), ACT.Square).then_inc(sem("squared"), 1)

            def root(ni, cols=T):
                act.wait_ge(sem("inverse_ready"), ni + 1)
                r = stats[ni % 2][:, 0:cols // P]
                act.activation(r, r, ACT.Sqrt).then_inc(sem("root_ready"), 1)

            def affine(ni, scale, bias, dst, cols=T, last=None, between=None, order=range(KB)):
                for i, k in enumerate(order):
                    act.wait_ge(sem("scaled"), 8 * ni + i + 1)
                    if i >= 2 and dst is None:
                        act.wait_ge(sem(f"split{ni}"), i - 1)
                    to = work[:, i % 2, 0:cols] if dst is None else dst(k)
                    src = work[:, 2 + i % 2, 0:cols]
                    b = 0.0 if bias is None else bias(k)
                    act.activation(to, src, ACT.Identity, scale=scale(k), bias=b)\
                        .then_inc(sem("affine_done") if last is None else last, 1)
                    if between is not None:
                        between(k)

            act.wait_ge(sem("vecs_in"), 16)
            act.activation(small[:, 0:16], vecr("c"), ACT.Silu).then_inc(sem("cond_ready"), 1)
            act.wait_ge(sem("ctx_in"), 16)
            act.wait_ge(sem("conds_in"), 16)
            act.activation(acc[:, :, CT:2 * CT], acc[:, :, CT:2 * CT], ACT.Silu).then_inc(sem("cond_ready"), 1)
            squares(0, lambda k: acc[:, k, 0:CT], CT)
            root(0, CT)
            act.wait_ge(sem("x_in"), 16)
            squares(1, lambda k: xres[:, k, :])
            root(1)
            act.wait_ge(sem("mod_ready"), 3)
            affine(0, lambda k: gain[:, 1, k:k + 1], lambda k: mod[:, k, 1:2], None, CT)
            affine(1, lambda k: gain[:, 0, k:k + 1], lambda k: mod[:, k, 0:1], None)

            n, o = SECTIONS["in"]

            def copy_product(dst, o, cols=T, func=ACT.Copy, **more):
                wait_product(act, o)
                free(act.activation(dst, bank(o % RING)[:, 0:cols], func, **more), o)

            def raw(i, o):
                if i == 0:
                    act.wait_ge(sem("split1"), 8)
                if i >= 2:
                    act.wait_ge(sem("rotated"), i - 1)
                copy_product(work[:, i % 2, :], o)

            def load_mod_pair(p):
                act.dma_start(mod_pairs[p % 4].rearrange("p (a n) -> p a n", a=2),
                              a["wmod"][16 + 2 * p:18 + 2 * p].rearrange("a p n -> p a n"))\
                    .then_inc(sem(f"mod_in{p % 4}"), 16)

            act.wait_ge(sem("mod_ready"), 3)
            act.wait_ge(sem("scaled"), 8)
            conds = a["conds"].rearrange("a (k n) -> a k n", n=CT)
            act.dma_start(cond_row, conds[:, 0:4, :].broadcast_to((P, 4, CT))).then_inc(sem("conds_in"), 16)
            for p in range(4):
                load_mod_pair(p)
            act.wait_ge(sem("conds_in"), 32)
            act.activation(cond_row, cond_row, ACT.Silu).then_inc(sem("cond_ready"), 1)
            copy_product(k_ctx, o, CT)
            for i in range(5):
                raw(i, o + 1 + i)
            act.wait_ge(sem("rotated"), 4)
            copy_product(work[:, 1, 0:CT], o + 6, CT)
            act.wait_ge(sem("rotated"), 5)
            copy_product(work[:, 0, :], o + 7)
            act.wait_ge(sem("values_turned"), 1)
            act.activation(v_ctx.rearrange("p t n -> p (t n)"), bank(7)[:, 0:CT], ACT.Copy)\
                .then_inc(sem("values_copied"), 1)
            act.wait_ge(sem("values_turned"), 2)
            act.activation(v_tok.rearrange("p t n -> p (t n)"), bank(7), ACT.Copy).then_inc(sem("values_copied"), 1)

            def attn_exp(u):
                m, g, qt, lo, hi = unit(u)
                w = (hi - lo + 3) * P
                act.wait_ge(sem("shift_ready"), u + 1)
                act.activation(probs[:, u % 2, 0:w], probs[:, u % 2, 0:w], ACT.Exp, scale=0.125,
                               bias=small[:, 20 + u % 2:21 + u % 2],
                               accum_out=small[:, 24 + u % 2:25 + u % 2]).then_inc(sem("attn_exp"), 1)
                head = m + 4 * g
                act.activation(small[:, 26 + u % 2:27 + u % 2], vec("sink", head), ACT.Exp,
                               bias=small[:, 20 + u % 2:21 + u % 2]).then_inc(sem("attn_exp"), 1)

            def attn_copy(u):
                m, g, qt, lo, hi = unit(u)
                act.wait_ge(sem("turned"), u + 1)
                if u:
                    wait_product(act, attn_product(u - 1))
                w = (hi - lo + 3) * P
                act.activation(probsT[:, 0:w], wide(6, 640)[:, 0:w], ACT.Copy).then_inc(sem("turned_copied"), 1)

            def attn_slot(i):
                if 1 <= i <= 32:
                    attn_copy(i - 1)
                if i < 32:
                    attn_exp(i)

            def reload_mod_pair(p):
                act.wait_ge(sem("mod_dot"), 16 + 2 * (p - 3))
                load_mod_pair(p)

            for p in range(4, 8):
                reload_mod_pair(p)
            for i in range(12):
                if 1 <= i <= 8:
                    reload_mod_pair(7 + i)
                if i % 3 == 0:
                    c = i // 3
                    if c >= 2:
                        act.wait_ge(sem("conv_in"), c - 1)
                    copy_product(cgate[:, c % 2, :], conv_out(i))
                attn_slot(i)
            n, o = SECTIONS["gates"]
            for i in range(16):
                dst = acc[:, i // 2, :] if i % 2 == 0 else gv[:, i // 2, :]
                copy_product(dst, o + 2 * i, func=ACT.Sigmoid)
                attn_slot(12 + i)
            for i in range(28, 34):
                attn_slot(i)

            squares(2, lambda k: xres[:, k, :], ready=lambda k: wait_read(act, SECTIONS["mix"][1] + k))
            root(2)
            act.wait_ge(sem("mod_ready"), 4)
            affine(2, lambda k: gain[:, 2, k:k + 1], lambda k: mod[:, 24 + k, 0:1], None)

            act.dma_start(sub_keys, a["keysT"]).then_inc(sem("keys_in"), 16)
            n, o = SECTIONS["pq"]
            for m in range(HP):
                if m >= 2:
                    act.wait_ge(sem("key_scores"), m - 1)
                copy_product(acc[:, m % 2, :], o + m)

            n, o = SECTIONS["pu"]
            act.wait_ge(sem("split2"), 8)

            def gelu_out(g, k, n0, o0, tile0, first, per_turn=RING):
                s = k % 2
                wait_product(act, o0 + k, g * per_turn)
                if not (first and k < 2):
                    act.wait_ge(sem(f"act_stored{s}"), g * (8 * per_turn) + 16 * ((tile0 + k) // 2))
                free(act.activation(work[:, s, :], bank((o0 + k) % RING), ACT.Gelu), o0 + k)
                wait_read(act, o0 + k, g * per_turn // RING)
                act.dma_start(act_dram[bass.ds(g * per_turn + (tile0 + k), 1)].rearrange("a p n -> (a p) n"),
                              work[:, s, :]).then_inc(sem(f"act_stored{s}"), 16)

            for k in range(RING):
                gelu_out(0, k, n, o, 0, True)
            with act.Fori(0, 12) as g:
                for k in range(RING):
                    gelu_out(g, k, n + 4, o + 4, 4, False)
            act.wait_ge(sem("best_ready"), TT)
            act.activation(best_e, best_e, ACT.Exp).then_inc(sem("best_exp"), 1)
            with act.Fori(0, 3) as g:
                for k in range(RING):
                    gelu_out(g, k, n + 52, o + 52, 52, False)

            act.wait_ge(sem("picks_ready"), TT)
            act.dma_start(memT, a["memT"].rearrange("(k p) t -> p k t", p=P)).then_inc(sem("mem_in"), 16)

            def gate_turn(g, half, first):
                for k in range(RING):
                    t0 = 64 + 4 * half
                    gelu_out(g, k, n + t0, o + t0, t0, False, 8)
                    for q in range(2 * k, 2 * k + 2):
                        act.wait_ge(sem("quad_done"), g * 16 + (8 * half + q + 1))
                        if q == 0 and not first:
                            act.wait_ge(sem(f"gates_stored{half}"), g * 16)
                        act.activation(stage[:, half, :, 4 * q:4 * q + 4],
                                       bank(6 + q % 2).rearrange("p (t j) -> p j t", t=4),
                                       ACT.Copy).then_inc(sem("quad_copied"), 1)
                act.wait_ge(sem("quad_copied"), g * 16 + (8 * half + 8))
                act.dma_start(gates_dram[bass.ds(g * 2 + half, 1)].rearrange("a i j t -> (a i) (j t)"),
                              stage[:, half, :, :].rearrange("p j t -> p (j t)"))\
                    .then_inc(sem(f"gates_stored{half}"), 16)

            gate_turn(0, 0, True)
            gate_turn(0, 1, True)
            with act.Fori(1, 8) as g:
                gate_turn(g, 0, False)
                gate_turn(g, 1, False)

            act.wait_ge(sem("gates_stored0"), 8 * TBS)
            act.wait_ge(sem("gates_stored1"), 8 * TBS)
            act.wait_ge(sem("act_stored0"), 16 * KEYS // 2)
            act.wait_ge(sem("act_stored1"), 16 * KEYS // 2)

            def load_half(j0, b):
                js = bass.ds(j0, 4)
                act.dma_start(ga_act[:, b, :, :], act_dram[js].rearrange("j p t -> p j t")).then_inc(
                    sem(f"act_back{b}"), 16)
                act.dma_start(ga_gate[:, b, :].rearrange("p (b n) -> p b n", b=TBS),
                              gates_dram[:, :, js, :].rearrange("b i j t -> i b (j t)")).then_inc(
                    sem(f"gate_back{b}"), 16)

            load_half(0, 0)
            load_half(4, 1)
            n, o = SECTIONS["memk"]
            for m in range(KB):
                copy_product(mk[:, m, :], o + m, CT)
            with act.Fori(1, 16) as g:
                for b in range(2):
                    act.wait_ge(sem("gated_split"), g * 8 + (4 * b - 4))
                    load_half(g * 8 + 4 * b, b)

            n, o = SECTIONS["memv"]

            def turn_back(m, dst, tiles, turned):
                act.wait_ge(sem("values_turned"), turned + m + 1)
                act.activation(dst[:, :, m * P:(m + 1) * P],
                               bank(6 + m % 2)[:, 0:tiles * P].rearrange("p (t n) -> p t n", t=tiles), ACT.Copy)\
                    .then_inc(sem("values_copied"), 1)

            def mem_copy(m):
                if m < KB:
                    if m >= 2:
                        act.wait_ge(sem("values_turned"), 2 + m - 1)
                    copy_product(mem_raw[:, m % 2, :], o + m, CT)
                if m:
                    turn_back(m - 1, mv, CT // P, 2)

            squares(3, lambda k: xres[:, k, :], ready=lambda k: act.wait_ge(sem("peer_added"), k + 1))
            for m in range(5):
                mem_copy(m)
            root(3)
            for m in range(5, 9):
                mem_copy(m)
            affine(3, lambda k: vec("final", k), None, lambda k: xres[:, k, :])

            n, o = SECTIONS["lstm"]

            def silu(m):
                act.wait_ge(sem("lconv_done"), m + 1)
                dst = lq[:, m, :] if m < 4 else lk[:, m - 4, :]
                act.activation(dst, work[:, 2 + m % 2, :], ACT.Silu).then_inc(sem("qk_ready"), 1)

            act.wait_ge(sem("lraw_zero"), 1)
            for m in range(8):
                if m >= 2:
                    act.wait_ge(sem("lconv_done"), m - 1)
                copy_product(lraw[:, m % 2, 3:3 + T], o + m)
                if m:
                    silu(m - 1)
            silu(7)
            wait_product(act, o + 8)
            act.wait_ge(sem("split3"), 8)
            gb = _VEC["gate_b"][0]
            step(act.activation(irow, psum[0:4, (o + 8) % RING, :], ACT.Identity, bias=vecs[0:4, gb:gb + 1]))
            free(act.activation(frow, psum[32:36, (o + 8) % RING, :], ACT.Identity, bias=vecs[32:36, gb:gb + 1]),
                 o + 8)
            wait_read(act, o + 8)
            step(act.activation(mrow, frow, ACT.Abs))
            step.settle()
            step(act.activation(mrow, mrow, ACT.Exp, scale=-1.0))
            step.settle()
            act.activation(mrow, mrow, ACT.Ln, bias=1.0).then_inc(sem("gate_rows"), 1)
            for m in range(9):
                if m < 8:
                    if m >= 2:
                        act.wait_ge(sem("values_turned"), 10 + m - 1)
                    copy_product(work[:, m % 2, :], o + 9 + m)
                if m:
                    turn_back(m - 1, lv, TT, 10)
            act.wait_ge(sem("floor_arg"), 1)
            act.activation(frow, frow, ACT.Exp, scale=-1.0).then_inc(sem("rows_ready"), 1)
            n, o = SECTIONS["core"]
            def head_root(h):
                act.wait_ge(sem("head_inverse"), h + 1)
                act.activation(stats[0][:, 0:4], stats[0][:, 0:4], ACT.Sqrt).then_inc(sem("head_root"), 1)

            for h in range(4):
                for st in range(TT):
                    i = 4 * h + st
                    act.wait_ge(sem("decay_arg"), i + 1)
                    c = slice(st * P, T)
                    act.activation(work[:, 2 + i % 2, c], work[:, 2 + i % 2, c], ACT.Exp).then_inc(sem("decay"), 1)
                if h:
                    head_root(h - 1)
                for j in range(2):
                    oo = o + 4 * h + j
                    wait_product(act, oo)
                    if h:
                        act.wait_ge(sem("lstm_split"), 2 * h + j - 1)
                    free(act.activation(lsig[:, j, :], bank(oo % RING), ACT.Sigmoid), oo)
                for j in range(2):
                    wait_read(act, o + 4 * h + 2 + j)
                    if h:
                        act.wait_ge(sem("head_rms"), h)
                    act.activation(work[:, j, :], acc[:, 2 * h + j, :], ACT.Square).then_inc(sem("head_squares"), 1)
            head_root(3)

            def post_norm(ni, j, ready, last=False):
                squares(ni, lambda k: acc[:, k, :], ready=ready)
                root(ni)
                affine(ni, lambda k: vec("ln_g", 8 * j + k), lambda k: vec("ln_b", 8 * j + k),
                       lambda k: xres[:, k, :], last=sem("norm_out") if last else None,
                       order=MIX_ORDER if ni == 6 else range(KB))

            def read_of(o):
                return lambda k: wait_read(act, o + k)

            post_norm(4, 0, read_of(SECTIONS["lout"][1]))
            ni = 4
            for layer in range(2):
                if layer:
                    o = SECTIONS["pool"][1]

                    def scale_pooled(k):
                        wait_product(act, o + k)
                        free(act.activation(acc[:, k, :], bank((o + k) % RING), ACT.Copy, scale=vec("pscale", k)),
                             o + k)

                    def pooled(k):
                        if k + 1 < KB:
                            scale_pooled(k + 1)
                        act.wait_ge(sem("pool_added"), k + 1)

                    scale_pooled(0)
                    post_norm(7, 3, pooled)
                    ni = 7
                n, o = SECTIONS[f"xq{layer}"]

                def x_exp(h):
                    for t in range(TT):
                        i = 4 * (4 * layer + h) + t
                        act.wait_ge(sem("x_shift"), i + 1)
                        act.activation(xp[:, t, :], xp[:, t, :], ACT.Exp, scale=0.0625,
                                       bias=small[:, 32 + t:33 + t],
                                       accum_out=small[:, 36 + t:37 + t]).then_inc(sem("x_exp"), 1)

                def x_copy(h):
                    i = 4 * layer + h
                    for j in range(2):
                        if j == 0:
                            act.wait_ge(sem("x_turned"), 4 * i + 4)
                            if i:
                                wait_product(act, x_value_out(i - 1))
                        act.activation(xpT[:, j, :], bank(6 + j), ACT.Copy).then_inc(sem("x_turned_copied"), 1)

                for m in range(KB):
                    oo = o + m + (0 if m < 4 else 2 if m < 6 else 4)
                    copy_product(xq[:, m, :], oo)
                    if m % 2:
                        h = m // 2
                        if h:
                            x_copy(h - 1)
                        x_exp(h)
                x_copy(3)
                post_norm(ni + 1, 3 * layer + 1, read_of(SECTIONS[f"xo{layer}"][1]))
                act.wait_ge(sem("affine_done"), 8 * (ni + 2))
                act.wait_ge(sem("scaled"), 8 * (ni + 2))
                for k in range(KB):
                    act.activation(acc[:, k, :], xres[:, k, :], ACT.Identity, scale=ALPHA,
                                   bias=vec("b2", 8 * layer + k)).then_inc(sem("mlp_start"), 1)
                n, o = SECTIONS[f"mlp{layer}"]
                b1at = _VEC["b1"][0] + 32 * layer

                def relu(oo, first, f, turn=0):
                    wait_product(act, oo, turn * 16)
                    if not first:
                        act.wait_ge(sem("hidden_split"), turn * 8 + (32 * layer + f - 1))
                    free(act.activation(work[:, f % 2, :], bank(oo % RING), ACT.Relu,
                                        bias=vecs[:, bass.ds(turn * 8 + (b1at + f), 1)]), oo)

                for k in range(4):
                    relu(o + k, layer == 0 and k < 2, k)
                with act.Fori(0, 3) as g:
                    for half in range(2):
                        for k in range(4):
                            relu(o + 4 + 12 * half + k, False, 4 + 4 * half + k, g)
                for k in range(4):
                    relu(o + 76 + k, False, 28 + k)
                post_norm(ni + 2, 3 * layer + 2, read_of(o + 88), last=(layer == 1))

        @block.vector
        def _(dve):
            step = Steps(dve, "dve_step")

            def split(src, hi, lo, signal):
                step(dve.tensor_copy(hi, src))
                step.settle()
                dve.tensor_tensor(lo, src, hi.bitcast(F32), ALU.subtract).then_inc(signal, 1)

            def add_square(ni, k, cols=T):
                dve.wait_ge(sem("squared"), 8 * ni + k + 1)
                if k:
                    dve.wait_ge(sem("summed"), 8 * ni + k)
                    ins = dve.tensor_tensor(work[:, 5, 0:cols], work[:, 5, 0:cols], work[:, k % 2, 0:cols], ALU.add)
                else:
                    ins = dve.tensor_copy(work[:, 5, 0:cols], work[:, k % 2, 0:cols])
                ins.then_inc(sem("summed"), 1)

            def add_value(ni, k, src):
                step.settle()
                if k:
                    step(dve.tensor_tensor(work[:, 4, :], work[:, 4, :], src, ALU.add))
                else:
                    step(dve.tensor_copy(work[:, 4, :], src))

            def statistics(ni, eps, cols=T, mean=False, width=D):
                dve.wait_ge(sem("sums_ready"), ni + 1)
                nt = cols // P
                st = stats[ni % 2]
                v, mu, mu2 = st[:, 0:nt], st[:, 4:4 + nt], st[:, 8:8 + nt]
                if mean:
                    dve.tensor_scalar(st[:, 0:8], bank(4)[:, 0:8], 1.0 / width, None, ALU.mult)\
                        .then_inc(sem("stats_read"), 1)
                    dve.wait_ge(sem("stats_read"), ni + 1)
                    step(dve.tensor_tensor(mu2, mu, mu, ALU.mult))
                    step.settle()
                    step(dve.tensor_tensor(v, v, mu2, ALU.subtract))
                    step.settle()
                    step(dve.tensor_scalar(v, v, 0.0, eps, ALU.max, ALU.add))
                else:
                    dve.tensor_scalar(v, bank(4)[:, 0:nt], 1.0 / width, eps, ALU.mult, ALU.add)\
                        .then_inc(sem("stats_read"), 1)
                    dve.wait_ge(sem("stats_read"), ni + 1)
                step.settle()
                dve.reciprocal(v, v).then_inc(sem("inverse_ready"), 1)

            def normalise(ni, src, cols=T, mean=False, at=5):
                def centre(k):
                    step(dve.tensor_tensor(src(k), src(k), bank(4), ALU.subtract))

                if mean:
                    dve.wait_ge(sem("mean_spread"), ni - 3)
                    for k in range(3):
                        centre(k)
                dve.wait_ge(sem("inverse_spread"), ni + 1)
                step.settle()

                def scale(k):
                    if mean and k >= 3:
                        centre(k)
                        step.settle()
                    if k >= 2:
                        dve.wait_ge(sem("norm_out") if ni == 9 else sem("affine_done"),
                                    (k - 1) if ni == 9 else 8 * ni + k - 1)
                    dve.tensor_tensor(work[:, 2 + k % 2, 0:cols], src(k), bank(at)[:, 0:cols], ALU.mult)\
                        .then_inc(sem("scaled"), 1)
                return scale

            def norm_out(ni, scale, out_tile, hi, lo):
                scale(0)
                for k in range(KB):
                    if k + 1 < KB:
                        scale(k + 1)
                    dve.wait_ge(sem("affine_done"), 8 * ni + k + 1)
                    split(out_tile(k), hi(k), lo(k), sem(f"split{ni}"))

            dve.wait_ge(sem("vecs_in"), 16)
            dve.wait_ge(sem("consts_in"), 16)
            step(dve.tensor_scalar(sink8, vecr("sink"), 8.0, None, ALU.mult))
            for k in range(KB):
                add_square(0, k, CT)
            statistics(0, EPS, CT)
            for k in range(KB):
                add_square(1, k)

            dots = 0

            def mod_dot(t, w, col):
                nonlocal dots
                scratch = work[:, 6:8, :].rearrange("p a n -> p (a n)").rearrange("p (k n) -> p k n", n=CT)
                if dots:
                    dve.wait_ge(sem("mod_dot"), dots)
                w = w.rearrange("p (k n) -> p k n", n=CT)
                dve.scalar_tensor_tensor(scratch, w, 1.0, cond_rows[col] if t < 16 else cond_row, ALU.mult, ALU.mult,
                                         accum_out=mod[:, t, col:col + 1]).then_inc(sem("mod_dot"), 1)
                dots += 1

            dve.wait_ge(sem("cond_ready"), 2)
            for g in range(4):
                dve.wait_ge(sem(f"mod_in{g}"), 16)
                for t in (4 * g + 2, 4 * g + 3):
                    for col in range(2):
                        mod_dot(t, mod_w[:, t % 12, :], col)
                if g == 1:
                    statistics(1, EPS)
            dve.wait_ge(sem("mod_dot"), 16)
            dve.wait_ge(sem("mod_used"), 8)
            step(dve.memset(zpad[:, :, 0:1], 0.0))
            step(dve.memset(zpad[:, :, T + 1:T + 2], 0.0))

            def gain_of(j, t0, col, nv):
                dve.scalar_tensor_tensor(gain[:, j, :], mod[:, t0:t0 + 8, col], 1.0, vecr(nv), ALU.add, ALU.mult)\
                    .then_inc(sem("mod_ready"), 1)

            def by_kind(t, kind):
                return t.rearrange("p (g kind a) two -> p g kind (a two)", kind=2, a=2)[:, :, kind, :]

            first = mod[:, 0:16, :]
            products = bank(6)[:, 0:32].rearrange("p (t two) -> p t two", two=2)
            step(dve.tensor_copy(by_kind(first, 0), by_kind(products, 0)))
            step.settle()
            dve.tensor_tensor(first, first, vecr("b_mod")[:, 0:16].unsqueeze(2).broadcast_to((P, 16, 2)), ALU.add)\
                .then_inc(sem("mod_ready"), 1)
            dve.wait_ge(sem("mod_ready"), 1)
            gain_of(0, 8, 0, "n1")
            gain_of(1, 8, 1, "n1")
            norm_out(0, normalise(0, lambda k: acc[:, k, 0:CT], CT, at=7), lambda k: work[:, k % 2, 0:CT],
                     lambda k: yhi[:, k, 0:CT], lambda k: ylo[:, k, 0:CT])
            norm_out(1, normalise(1, lambda k: xres[:, k, :]), lambda k: work[:, k % 2, :],
                     lambda k: xhi[:, k, :], lambda k: xlo[:, k, :])

            def mod_pair_dot(p, j):
                dve.wait_ge(sem(f"mod_in{p % 4}"), 32 + 16 * (p // 4))
                mod_dot(16 + 2 * p + j, mod_pairs[p % 4][:, 1024 * j:1024 * j + 1024], 0)

            def mod_pair_dots(p):
                mod_pair_dot(p, 0)
                mod_pair_dot(p, 1)

            dve.wait_ge(sem("cond_ready"), 3)
            n, o = SECTIONS["in"]
            for i in range(5):
                dst = k_rope if i == 0 else q_rope[:, i - 1, :]
                wait_read(dve, o + 1 + i)
                step(dve.tensor_tensor(work[:, 2, :], work[:, i % 2, :], const("cos"), ALU.mult))
                dve.wait_ge(sem("swapped"), i + 1)
                step(dve.tensor_tensor(work[:, 3, :], bank(6), const("sin"), ALU.mult))
                step.settle()
                dve.tensor_tensor(dst, work[:, 2, :], work[:, 3, :], ALU.add).then_inc(sem("rotated"), 1)
                dve.wait_ge(sem("rotated"), i + 1)
                if i:
                    mod_pair_dots(i - 1)

            def attn_softmax_in(u):
                m, g, qt, lo, hi = unit(u)
                wl = (hi - lo + 1) * P
                w = wl + CT
                s = probs[:, u % 2, :]
                dve.wait_ge(sem("scores_ready"), u + 1)
                if u >= 2:
                    dve.wait_ge(sem("turned"), u - 1)
                b0 = _CONST["band"][0] + (lo - qt + 1) * P
                step(dve.tensor_tensor(s[:, 0:wl], wide(4, 640)[:, 0:wl], consts[:, b0:b0 + wl], ALU.add))
                dve.tensor_copy(s[:, wl:w], wide(4, 640)[:, wl:w]).then_inc(sem("scores_read"), 1)
                step.settle()
                dve.wait_ge(sem("scores_read"), u + 1)
                mx = small[:, 22 + u % 2:23 + u % 2]
                step(dve.tensor_reduce(mx, s[:, 0:w], AX.X, ALU.max))
                step.settle()
                head = m + 4 * g
                dve.tensor_scalar(small[:, 20 + u % 2:21 + u % 2], mx, sink8[:, head:head + 1], -0.125, ALU.max,
                                  ALU.mult).then_inc(sem("shift_ready"), 1)

            def attn_softmax_out(u):
                m, g, qt, lo, hi = unit(u)
                w = (hi - lo + 3) * P
                dve.wait_ge(sem("attn_exp"), 2 * u + 2)
                den = small[:, 28 + u % 2:29 + u % 2]
                step(dve.tensor_tensor(den, small[:, 24 + u % 2:25 + u % 2], small[:, 26 + u % 2:27 + u % 2], ALU.add))
                step.settle()
                step(dve.reciprocal(den, den))
                step.settle()
                dve.tensor_scalar(probs[:, u % 2, 0:w], probs[:, u % 2, 0:w], den, None, ALU.mult)\
                    .then_inc(sem("probs_ready"), 1)

            def attn_split(u):
                m, g, qt, lo, hi = unit(u)
                rows = slice(64 * g, 64 * g + 64)
                c = slice(qt * P, (qt + 1) * P)
                o = attn_product(u)
                wait_product(dve, o)
                split(psum[rows, o % RING, 0:P], yhi[rows, m, c], ylo[rows, m, c], bank_free[o % RING])

            def attn_slot(i):
                if i < 32:
                    attn_softmax_in(i)
                    if i < 12:
                        mod_pair_dot(4 + i, 0)
                    attn_softmax_out(i)
                    if i < 12:
                        mod_pair_dot(4 + i, 1)
                if 2 <= i <= 33:
                    attn_split(i - 2)

            for i in range(12):
                c = i // 3
                if i % 3 == 1:
                    wait_read(dve, conv_out(i - 1))
                    o = conv_out(i)
                    wait_product(dve, o)
                    free(dve.tensor_tensor(zpad[:, c % 2, 1:T + 1], bank(o % RING), cgate[:, c % 2, :],
                                           ALU.mult), o)
                    wait_read(dve, o)
                    y = work[:, 2 + c % 2, :]
                    z = zpad[:, c % 2, :]
                    dve.tensor_scalar(y, z[:, 0:T], vec("conv", c), None, ALU.mult).then_inc(sem("conv_in"), 1)
                    dve.wait_ge(sem("conv_in"), c + 1)
                    for tap in (1, 2):
                        step(dve.scalar_tensor_tensor(y, z[:, tap:tap + T], vec("conv", 4 * tap + c), y, ALU.mult,
                                                      ALU.add))
                        step.settle()
                if i % 3 == 2:
                    o = conv_out(i)
                    wait_product(dve, o)
                    y = work[:, 2 + c % 2, :]
                    free(dve.tensor_tensor(y, bank(o % RING), y, ALU.mult), o)
                    wait_read(dve, o)
                    split(y, yhi[:, 4 + c, :], ylo[:, 4 + c, :], sem("conv_split"))
                attn_slot(i)
            dve.wait_ge(sem("mod_dot"), 16 + 32)
            later = mod[:, 16:48, 0:1]
            step(dve.tensor_tensor(later, later, vecr("b_mod")[:, 16:48].unsqueeze(2), ALU.add))
            step.settle()
            gain_of(2, 32, 0, "n2")
            for i in range(12, 34):
                attn_slot(i)

            n, o = SECTIONS["branch"]
            for m in range(KB):
                for j, t in ((0, acc[:, m, :]), (1, gv[:, m, :])):
                    wait_read(dve, SECTIONS["gates"][1] + 4 * m + 2 * j)
                    wait_product(dve, o + 2 * m + j)
                    free(dve.tensor_tensor(t, bank((o + 2 * m + j) % RING), t, ALU.mult), o + 2 * m + j)
                    wait_read(dve, o + 2 * m + j)
                step(dve.tensor_tensor(acc[:, m, :], acc[:, m, :], gv[:, m, :], ALU.add))
                step.settle()
                split(acc[:, m, :], xhi[:, m, :], xlo[:, m, :], sem("merge_split"))

            n, o = SECTIONS["mix"]
            for k in range(KB):
                wait_product(dve, o + k)
                free(dve.scalar_tensor_tensor(xres[:, k, :], bank((o + k) % RING), mod[:, 16 + k, 0:1], xres[:, k, :],
                                              ALU.mult, ALU.add), o + k)
                if k:
                    add_square(2, k - 1)
            add_square(2, KB - 1)
            statistics(2, EPS)
            norm_out(2, normalise(2, lambda k: xres[:, k, :]), lambda k: work[:, k % 2, :],
                     lambda k: xhi[:, k, :], lambda k: xlo[:, k, :])

            for m in range(HP):
                dve.wait_ge(sem("key_scores"), m + 1)
                dve.tensor_copy(scores_all[:, :, m, :], bank(6).rearrange("p (t n) -> p t n", t=TT))\
                    .then_inc(sem("key_scores_copied"), 1)
            dve.wait_ge(sem("key_scores_copied"), HP)

            def top16(values, indices, rows, src):
                for half in range(2):
                    c = slice(8 * half, 8 * half + 8)
                    for r in range(rows):
                        step(dve.max(values[:, r, c], src[:, r, :]))
                    step.settle()
                    for r in range(rows):
                        step(dve.max_index(indices[:, r, c], values[:, r, c], src[:, r, :]))
                    step.settle()
                    if half == 0:
                        for r in range(rows):
                            step(dve.match_replace(src[:, r, :], values[:, r, c], src[:, r, :], LOWEST))
                        step.settle()

            heads = HP // 2
            v = top_v.rearrange("p (h s r) -> p h s r", h=heads, s=2)
            f = top_f.rearrange("p (h s r) -> p h s r", h=heads, s=2)
            b = best.rearrange("p (h k) -> p h k", h=heads)
            e_all = best_e.rearrange("p (t h k) -> p t h k", t=TT, h=heads)
            look3 = look.rearrange("p (n r) -> p n r", r=TOPK)
            look4 = look.rearrange("p (h k r) -> p h k r", h=heads, k=TOPK)
            for tt in range(TT):
                top16(top_v.rearrange("p (h r) -> p h r", h=HP), top_i.bitcast(U32).rearrange("p (h r) -> p h r", h=HP),
                      HP, scores_all[:, tt, :, :])
                step(dve.tensor_copy(top_f, top_i.bitcast(U32)))
                step(dve.tensor_tensor(cand.rearrange("p (h a b) -> p h a b", h=heads, a=TOPK),
                                       v[:, :, 0, :].unsqueeze(3).broadcast_to((P, heads, TOPK, TOPK)),
                                       v[:, :, 1, :].unsqueeze(2).broadcast_to((P, heads, TOPK, TOPK)), ALU.add))
                step.settle()
                top16(b, best_pos.bitcast(U32).rearrange("p (h k) -> p h k", h=heads), heads,
                      cand.rearrange("p (h n) -> p h n", h=heads))
                step(dve.tensor_scalar(best_row.bitcast(U32), best_pos.bitcast(U32), 4, None,
                                       ALU.logical_shift_right))
                step.settle()
                step(dve.tensor_scalar(best_pos.bitcast(U32), best_pos.bitcast(U32), 15, None, ALU.bitwise_and))
                step(dve.tensor_copy(top_i[:, 0:P], best_row.bitcast(U32)))
                step.settle()
                step(dve.tensor_copy(top_i[:, P:2 * P], best_pos.bitcast(U32)))
                step.settle()
                for s in range(2):
                    step(dve.tensor_tensor(look3, top_i[:, s * P:(s + 1) * P].unsqueeze(2).broadcast_to((P, P, TOPK)),
                                           const("iota")[:, 0:TOPK].unsqueeze(1).broadcast_to((P, P, TOPK)),
                                           ALU.is_equal))
                    step.settle()
                    step(dve.tensor_tensor(look4, look4,
                                           f[:, :, s, :].unsqueeze(2).broadcast_to((P, heads, TOPK, TOPK)),
                                           ALU.mult))
                    step.settle()
                    step(dve.tensor_reduce(picks[:, tt, s, :], look3, AX.X, ALU.add))
                    step.settle()
                dve.tensor_tensor(e_all[:, tt, :, :], b, b[:, :, 0:1].broadcast_to((P, heads, TOPK)),
                                  ALU.subtract).then_inc(sem("best_ready"), 1)
                dve.wait_ge(sem("best_ready"), tt + 1)
            dve.wait_ge(sem("best_exp"), 1)
            for tt in range(TT):
                step(dve.tensor_reduce(best_sum, e_all[:, tt, :, :], AX.X, ALU.add))
                step.settle()
                step(dve.reciprocal(best_sum, best_sum))
                step.settle()
                dve.tensor_tensor(picks[:, tt, 2, :].rearrange("p (h k) -> p h k", h=heads), e_all[:, tt, :, :],
                                  best_sum.unsqueeze(2).broadcast_to((P, heads, TOPK)), ALU.mult)\
                    .then_inc(sem("picks_ready"), 1)
                dve.wait_ge(sem("picks_ready"), tt + 1)

            for i in range(3 * TT):
                dve.wait_ge(sem("picks_turned"), i + 1)
                dve.tensor_copy(picksT[:, i % 3, (i // 3) * P:(i // 3 + 1) * P], bank(6 + i % 2)[:, 0:P])\
                    .then_inc(sem("picks_copied"), 1)
            dve.wait_ge(sem("picks_copied"), 3 * TT)

            def hot_rows(g, half, first):
                for q in range(8):
                    if not (first and q < 2):
                        dve.wait_ge(sem("quad_done"), g * 16 + (8 * half + q - 1))
                    for r in range(4):
                        slot = (4 * q + r) % 8
                        tok = bass.ds(g * (2 * TB) + (TB * half + 4 * q + r), 1)
                        step(dve.tensor_scalar(hot[:, slot, 0, :], const("iota"), picksT[:, 0, tok], None,
                                               ALU.is_equal))
                        ins = dve.tensor_scalar(hot[:, slot, 1, :], const("iota"), picksT[:, 1, tok],
                                                picksT[:, 2, tok], ALU.is_equal, ALU.mult)
                        if r < 3:
                            step(ins)
                        else:
                            ins.then_inc(sem("hot_ready"), 1)

            hot_rows(0, 0, True)
            hot_rows(0, 1, False)
            per = 7 * 16
            with dve.Fori(1, 8) as g:
                hot_rows(g, 0, False)
                hot_rows(g, 1, False)
            step.n += 6 * per
            dve.wait_ge(sem("quad_done"), 128)
            dve.wait_ge(sem("mem_in"), 16)
            wait_product(dve, SECTIONS["pu"][1] + 127)
            for k in range(KB):
                split(memT[:, k, :], xhi[:, k, 0:CT], xlo[:, k, 0:CT], sem("mem_split"))
            dve.wait_ge(sem("mem_split"), KB)

            def gated(g, b, j):
                if j == 0:
                    dve.wait_ge(sem(f"act_back{b}"), g * 16 + 16)
                    dve.wait_ge(sem(f"gate_back{b}"), g * 16 + 16)
                t = ga_act[:, b, j, :]
                gt = ga_gate[:, b, :].rearrange("p (b j t) -> p b j t", b=TBS, j=4)[:, :, j, :]
                step(dve.tensor_tensor(t.rearrange("p (b t) -> p b t", b=TBS), t.rearrange("p (b t) -> p b t", b=TBS),
                                       gt, ALU.mult))
                step.settle()
                split(t, yhi[:, 4 * b + j, :], ylo[:, 4 * b + j, :], sem("gated_split"))

            def collect(oo, shift, k, first=False):
                wait_product(dve, oo, shift)
                if first:
                    ins = dve.tensor_copy(acc[:, k, :], bank(oo % RING))
                else:
                    ins = dve.tensor_tensor(acc[:, k, :], acc[:, k, :], bank(oo % RING), ALU.add)
                free(ins, oo)

            n, o = SECTIONS["pv"]
            for b in range(2):
                for j in range(4):
                    gated(0, b, j)
            for half in range(2):
                for k in range(KB):
                    collect(o + 8 * half + k, 0, k, first=(half == 0))
                for j in range(4):
                    gated(1, half, j)
            per = 2 * 4 * 2
            base = step.n
            with dve.Fori(1, 15) as g:
                step.turn = g * per - per
                for half in range(2):
                    for k in range(KB):
                        collect(o + 8 * half + k, g * 8, k)
                    for j in range(4):
                        gated(g + 1, half, j)
            assert step.n == base + per
            step.turn = 0
            step.n = base + 14 * per
            dve.wait_ge(sem("gated_split"), 128)
            for k in range(2 * KB):
                if k >= KB:
                    wait_read(dve, o + 240 + k - KB)
                collect(o + 240 + k, 0, k % KB)
            for k in range(KB):
                wait_read(dve, o + 248 + k)
                dve.scalar_tensor_tensor(xres[:, k, :], acc[:, k, :], mod[:, 40 + k, 0:1], xres[:, k, :], ALU.mult,
                                         ALU.add).then_inc(sem("peer_added"), 1)
                if k:
                    add_square(3, k - 1)
            add_square(3, KB - 1)
            statistics(3, EPS)
            wait_product(dve, SECTIONS["memv"][1] + 7)
            norm_out(3, normalise(3, lambda k: xres[:, k, :]), lambda k: xres[:, k, :],
                     lambda k: xhi[:, k, :], lambda k: xlo[:, k, :])

            dve.memset(lraw[:, :, 0:3], 0.0).then_inc(sem("lraw_zero"), 1)
            dve.wait_ge(sem("lraw_zero"), 1)
            for m in range(8):
                wait_read(dve, SECTIONS["lstm"][1] + m)
                if m >= 2:
                    dve.wait_ge(sem("qk_ready"), m - 1)
                y = work[:, 2 + m % 2, :]
                step(dve.tensor_scalar(y, lraw[:, m % 2, 0:T], vec("mconv", m), None, ALU.mult))
                step.settle()
                for tap in (1, 2, 3):
                    ins = dve.scalar_tensor_tensor(y, lraw[:, m % 2, tap:tap + T], vec("mconv", 8 * tap + m), y,
                                                   ALU.mult, ALU.add)
                    if tap < 3:
                        step(ins)
                        step.settle()
                    else:
                        ins.then_inc(sem("lconv_done"), 1)
            dve.wait_ge(sem("gate_rows"), 1)
            step(dve.tensor_scalar(arow, frow, 0.0, None, ALU.min))
            step.settle()
            step(dve.tensor_tensor(arow, arow, mrow, ALU.subtract))
            step.settle()
            step(dve.tensor_tensor_scan(frow, const("ones", 4)[:, 0:1].broadcast_to((4, T)), arow, 0.0, ALU.mult,
                                        ALU.add))
            step.settle()
            step(dve.tensor_tensor(arow, irow, frow, ALU.subtract))
            step.settle()
            step(dve.tensor_tensor_scan(mrow, arow, arow, 0.0, ALU.max, ALU.max))
            step.settle()
            step(dve.tensor_tensor(frow, frow, mrow, ALU.add))
            step.settle()
            dve.tensor_scalar(mrow, mrow, -1.0, None, ALU.mult).then_inc(sem("floor_arg"), 1)
            dve.wait_ge(sem("decay_turned"), 1)
            dve.tensor_copy(acol, bank(7)[:, 0:16]).then_inc(sem("decay_copied"), 1)
            dve.wait_ge(sem("decay_copied"), 1)
            n, o = SECTIONS["core"]
            def head_stats(h):
                st = stats[0][:, 0:4]
                dve.wait_ge(sem("head_rms"), h + 1)
                dve.tensor_scalar(st, bank(7)[:, 0:4], 1.0 / 256, LN_EPS, ALU.mult, ALU.add)\
                    .then_inc(sem("head_rms_read"), 1)
                dve.wait_ge(sem("head_rms_read"), h + 1)
                dve.reciprocal(st, st).then_inc(sem("head_inverse"), 1)

            def head_out(h):
                dve.wait_ge(sem("head_inverse_spread"), h + 1)
                for j in range(2):
                    t = acc[:, 2 * h + j, :]
                    step(dve.tensor_tensor(t, t, bank(5), ALU.mult))
                    step.settle()
                    wait_read(dve, o + 4 * h + j)
                    step(dve.scalar_tensor_tensor(t, t, vec("mnorm", 2 * h + j), lsig[:, j, :], ALU.mult, ALU.mult))
                    step.settle()
                    split(t, yhi[:, 2 * h + j, :], ylo[:, 2 * h + j, :], sem("lstm_split"))

            for h in range(4):
                dve.wait_ge(sem("max_spread"), h + 1)
                dve.wait_ge(sem("qk_ready"), 8)

                def decay_arg(st):
                    i = 4 * h + st
                    c = slice(st * P, T)
                    step.settle()
                    dve.tensor_scalar(work[:, 2 + i % 2, c], bank(4)[:, c], acol[:, 4 * st + h:4 * st + h + 1], 0.0,
                                      ALU.add, ALU.min).then_inc(sem("decay_arg"), 1)
                decay_arg(0)
                for st in range(TT):
                    i = 4 * h + st
                    if st + 1 < TT:
                        if i >= 1:
                            dve.wait_ge(sem("lstm_weighted"), i)
                        decay_arg(st + 1)
                    c = slice(st * P, T)
                    dve.wait_ge(sem("decay"), i + 1)
                    dve.wait_ge(sem("lstm_scores"), i + 1)
                    step(dve.scalar_tensor_tensor(lp[:, st, c], bank(5 + i % 2)[:, c], 128 ** -0.5,
                                                  work[:, 2 + i % 2, c], ALU.mult, ALU.mult))
                    step.settle()
                    d = slice(st * P, (st + 1) * P)
                    dve.tensor_tensor(lp[:, st, d], lp[:, st, d], const("utri"), ALU.mult)\
                        .then_inc(sem("lstm_weighted"), 1)
                dve.wait_ge(sem("lstm_weighted"), 4 * h + 4)
                if h:
                    head_stats(h - 1)
                    head_out(h - 1)
                dve.wait_ge(sem("lstm_den"), h + 1)
                den = work[:, 2, :]
                step(dve.tensor_copy(den, bank(7)))
                step.settle()
                step(dve.scalar_tensor_tensor(den, den, -1.0, den, ALU.mult, ALU.max))
                dve.wait_ge(sem("floor_spread"), h + 1)
                step.settle()
                dve.tensor_tensor(den, den, bank(6), ALU.max).then_inc(sem("floor_read"), 1)
                dve.wait_ge(sem("floor_read"), h + 1)
                step(dve.reciprocal(den, den))
                step.settle()
                for j in range(2):
                    oo = o + 4 * h + 2 + j
                    wait_product(dve, oo)
                    free(dve.tensor_tensor(acc[:, 2 * h + j, :], bank(oo % RING), den, ALU.mult), oo)
                    wait_read(dve, oo)
            head_stats(3)
            head_out(3)

            def residual_products(ni, o):
                for k in range(KB):
                    wait_product(dve, o + k)
                    free(dve.scalar_tensor_tensor(acc[:, k, :], xres[:, k, :], ALPHA, bank((o + k) % RING), ALU.mult,
                                                  ALU.add), o + k)
                    wait_read(dve, o + k)
                    add_value(ni, k, acc[:, k, :])
                    if k:
                        add_square(ni, k - 1)
                add_square(ni, KB - 1)
                step.settle()

            def pool_mixer(scale):
                dve.memset(ppad[:, :, 0:16], 0.0).then_inc(sem("ppad_zero"), 1)
                dve.wait_ge(sem("ppad_zero"), 1)
                scale(0)
                scale(1)
                for n, i in enumerate((1, 3, 5, 6, 7)):
                    k = MIX_ORDER[i]
                    dve.wait_ge(sem("affine_done"), 8 * 6 + i + 1)
                    y = pool_y[:, n % 2, :]
                    mix_window(dve, step, k, ppad, y, True)
                    split(y, yhi[:, k, :], ylo[:, k, :], sem("pool_split"))
                    dve.wait_ge(sem("pool_split"), n + 1)
                    if n < 3:
                        scale(2 * n + 2)
                        scale(2 * n + 3)

            def post_norm(ni, last=False):
                statistics(ni, LN_EPS, mean=True)
                scale = normalise(ni, lambda k: acc[:, MIX_ORDER[k] if ni == 6 else k, :], mean=True)
                if ni == 6:
                    pool_mixer(scale)
                elif last:
                    for k in range(KB):
                        scale(k)
                else:
                    norm_out(ni, scale, lambda k: xres[:, k, :], lambda k: xhi[:, k, :], lambda k: xlo[:, k, :])

            dve.wait_ge(sem("lstm_split"), 8)
            residual_products(4, SECTIONS["lout"][1])
            post_norm(4)
            ni = 4
            for layer in range(2):
                if layer:
                    o = SECTIONS["pool"][1]
                    for k in range(KB):
                        wait_read(dve, o + k)
                        dve.scalar_tensor_tensor(acc[:, k, :], xres[:, k, :], ALPHA, acc[:, k, :], ALU.mult,
                                                 ALU.add).then_inc(sem("pool_added"), 1)
                        dve.wait_ge(sem("pool_added"), k + 1)
                        add_value(7, k, acc[:, k, :])
                        if k:
                            add_square(7, k - 1)
                    add_square(7, KB - 1)
                    step.settle()
                    post_norm(7)
                    ni = 7
                n, o = SECTIONS[f"xq{layer}"]

                def x_softmax_in(h):
                    for t in range(TT):
                        i = 4 * (4 * layer + h) + t
                        dve.wait_ge(sem("x_scores"), i + 2 - t % 2)
                        if i >= 4:
                            dve.wait_ge(sem("x_turned"), i - 3)
                        s = wide(4, 1024)[:, t * CT:(t + 1) * CT]
                        mx = small[:, 40 + t:41 + t]
                        step(dve.tensor_reduce(mx, s, AX.X, ALU.max))
                        dve.tensor_copy(xp[:, t, :], s).then_inc(sem("x_scores_read"), 1)
                        dve.wait_ge(sem("x_scores_read"), i + 1)
                        step.settle()
                        dve.tensor_scalar(small[:, 32 + t:33 + t], mx, -0.0625, None, ALU.mult)\
                            .then_inc(sem("x_shift"), 1)

                def x_softmax_out(h):
                    for t in range(TT):
                        i = 4 * (4 * layer + h) + t
                        dve.wait_ge(sem("x_exp"), i + 1)
                        r = small[:, 36 + t:37 + t]
                        step(dve.reciprocal(r, r))
                        step.settle()
                        dve.tensor_scalar(xp[:, t, :], xp[:, t, :], r, None, ALU.mult).then_inc(sem("x_probs"), 1)

                def x_split(h):
                    for j in range(2):
                        oo = x_value_out(4 * layer + h) - 1 + j
                        wait_product(dve, oo)
                        step(dve.tensor_copy(yhi[:, 2 * h + j, :], bank(oo % RING)))
                        step.settle()
                        free(dve.tensor_tensor(ylo[:, 2 * h + j, :], bank(oo % RING), yhi[:, 2 * h + j, :].bitcast(F32),
                                               ALU.subtract), oo)

                for h in range(4):
                    x_softmax_in(h)
                    x_softmax_out(h)
                    if h:
                        x_split(h - 1)
                x_split(3)
                residual_products(ni + 1, SECTIONS[f"xo{layer}"][1])
                post_norm(ni + 1)
                n, o = SECTIONS[f"mlp{layer}"]

                def hidden(oo, j, f, first=False, turn=0):
                    wait_read(dve, oo, turn * 6)
                    if not first:
                        dve.wait_ge(sem("hidden_split"), turn * 8 + (32 * layer + f - 1))
                    t, q = work[:, j % 2, :], work[:, 2 + j % 2, :]
                    step(dve.tensor_tensor(q, t, t, ALU.mult))
                    step.settle()
                    split(q, yhi[:, j, :], ylo[:, j, :], sem("hidden_split"))

                dve.wait_ge(sem("mlp_start"), 8 * layer + 8)
                for j in range(4):
                    hidden(o + j, j, j, layer == 0 and j < 2)

                def turn(g, half):
                    for j in range(4):
                        hidden(o + 4 + 12 * half + j, 4 * (1 - half) + j, 4 + 4 * half + j, turn=g)
                    for k in range(KB):
                        oo = o + 8 + 12 * half + k
                        wait_product(dve, oo, g * 16 if DONE[oo][0] == "tile" else g * 8)
                        free(dve.tensor_tensor(acc[:, k, :], acc[:, k, :], bank(oo % RING), ALU.add), oo)

                per = 2 * (4 * 2)
                base = step.n
                with dve.Fori(0, 3) as g:
                    step.turn = g * per
                    turn(g, 0)
                    turn(g, 1)
                assert step.n == base + per
                step.turn = 0
                step.n = base + 3 * per
                turn(3, 0)
                for k in range(8):
                    oo = o + 88 + k
                    wait_product(dve, oo)
                    wait_read(dve, oo - 8)
                    free(dve.tensor_tensor(acc[:, k, :], acc[:, k, :], bank(oo % RING), ALU.add), oo)
                    wait_read(dve, oo)
                    add_value(ni + 2, k, acc[:, k, :])
                    if k:
                        add_square(ni + 2, k - 1)
                add_square(ni + 2, KB - 1)
                step.settle()
                post_norm(ni + 2, last=(layer == 1))


def shape_constants():
    parts = {"ident": np.eye(P), "ones": np.ones((P, P)), "iota": np.tile(np.arange(P), (P, 1))}
    perm = np.zeros((P, P))
    for f in range(P):
        if f % 32 < 16:
            perm[f + 16, f] = -1.0
        else:
            perm[f - 16, f] = 1.0
    parts["perm"] = perm
    r = np.arange(P)
    parts["utri"] = (r[:, None] <= r[None, :]).astype(np.float32)
    before = np.where(r[None, :] >= r[:, None], 0.0, NEG)
    after = np.where(r[None, :] <= r[:, None], 0.0, NEG)
    parts["band"] = np.concatenate([before, np.zeros((P, P)), after], axis=1)
    t = np.arange(T)
    freq = (np.float32(ROPE_BASE) ** (-np.arange(PAIRS, dtype=np.float32) / np.float32(PAIRS))).astype(np.float32)
    angle = np.zeros((P, T), np.float32)
    for f in range(P):
        place = (t // GRID_W if f % 64 < 32 else t % GRID_W).astype(np.float32)
        angle[f] = place * freq[f % 16]
    parts["cos"], parts["sin"] = np.cos(angle), np.sin(angle)
    parts["cnt"] = np.tile(np.concatenate([1.0 / np.minimum(np.arange(16) + 1, w) for w in WINDOWS]), (P, 1))
    return np.concatenate([np.asarray(parts[name], np.float32) for name in _CONST], axis=1)


def columns(v):
    return np.ascontiguousarray(np.asarray(v).reshape(-1, P).T)


def row_tiles(w):
    k, m = w.shape
    return w.reshape(k // P, P, m // P, P).transpose(2, 1, 0, 3).reshape(m // P, P, k)


def half_groups(w):
    k = w.shape[0]
    return w.reshape(k // 512, 4, P, 4, 2, P).transpose(0, 3, 2, 4, 1, 5).reshape(k // 128, P, 1024)


def layout(x):
    a = {}
    z = np.zeros
    f32 = np.float32
    w_in = x["w_in"][0]
    heads = w_in[:, 0:512].reshape(D, 2, 4, 64).transpose(0, 2, 1, 3).reshape(D, 512)
    q, rest = row_tiles(heads), row_tiles(w_in[:, 512:])
    k, v, gb, gc, u, ga, gv = rest[0:1], rest[1:2], rest[2:6], rest[6:10], rest[10:14], rest[14:22], rest[22:30]
    conv = np.stack([gc, u, gb], axis=1).reshape(12, P, 1024)
    gates = np.stack([ga, gv], axis=1).reshape(16, P, 1024)
    attn_out = x["w_attn_out"][0].reshape(2, 4, 64, D).transpose(1, 0, 2, 3).reshape(512, D)
    branch = np.concatenate([row_tiles(attn_out), row_tiles(x["w_conv_out"][0])], axis=2)
    peer_u = x["peer_u"][0].reshape(P, KEYS, KB, P).transpose(1, 3, 2, 0).reshape(KEYS, P, 1024)
    peer_v = half_groups(x["peer_v"][0].reshape(P, KEYS, D).transpose(1, 0, 2).reshape(P * KEYS, D))
    w_l = x["mlstm_w_in_2"][0]
    pad = z((D, 28), f32)
    gate_cols = np.concatenate([w_l[:, 3072:3076], pad, w_l[:, 3076:3080], z((D, 92), f32)], axis=1)
    l_tiles = row_tiles(w_l[:, 0:3072])

    def mlp(layer):
        w1, w2 = row_tiles(x["mlp_w1_2"][layer]), half_groups(x["mlp_w2_2"][layer])
        parts = [w1[0:4]]
        for g in range(7):
            parts += [w1[4 * g + 4:4 * g + 8], w2[4 * g:4 * g + 4]]
        return parts + [w2[28:32]]

    pool = x["pool_w_2"][0].reshape(4, 2, P, 2, P).transpose(0, 3, 2, 1, 4)
    pool = pool.reshape(2, 4, P, 256).transpose(0, 2, 1, 3).reshape(2, P, 1024)
    mem = row_tiles(x["mem_w_kv_2"])
    stream = [k, q, v, conv, gates, branch, row_tiles(x["w_mix_out"][0]), row_tiles(x["peer_w_q"][0]), peer_u,
              mem[0:8], peer_v, mem[8:16], l_tiles[0:8], row_tiles(gate_cols), l_tiles[8:16], l_tiles[16:24],
              row_tiles(x["mlstm_w_out_2"][0])]
    for layer in range(2):
        if layer:
            stream.append(pool)
        stream += [row_tiles(x["xattn_wq_2"][layer]), row_tiles(x["xattn_wo_2"][layer])] + mlp(layer)
    a["stream"] = np.concatenate(stream, axis=0)
    assert a["stream"].shape[0] == NTILES
    w_mod = x["w_mod"][0]
    by_row = w_mod.T.reshape(48, P, D)
    first = np.stack([row_tiles(w_mod)[0:16].reshape(4, 2, 2, P, D)[:, 0], by_row[0:16].reshape(4, 2, 2, P, D)[:, 1]],
                     axis=1)
    a["wmod"] = np.concatenate([first.reshape(16, P, D), by_row[16:48]], axis=0)
    a["conds"] = np.concatenate([x["c"][0].reshape(1, D), x["c_ctx"].reshape(1, D)], axis=1)
    a["xT"] = x["x"][0].T
    a["ctxT"] = x["ctx"][0].T
    a["memT"] = x["mem_2"][0].T
    a["keysT"] = x["peer_sub_keys"][0].reshape(HP, KEYS, P).transpose(2, 0, 1)
    gate_b = z((P, 1), f32)
    gate_b[0:4, 0] = x["mlstm_gate_b_2"][0, 0:4]
    gate_b[32:36, 0] = x["mlstm_gate_b_2"][0, 4:8]
    vec = {
        "b_mod": columns(x["b_mod"][0]), "n1": columns(x["norm1_g"][0]), "n2": columns(x["norm2_g"][0]),
        "final": columns(x["final_g"]), "conv": columns(x["conv_w"][0]), "mconv": columns(x["mlstm_conv_w_2"][0]),
        "mnorm": columns(x["mlstm_norm_g_2"][0]), "gate_b": gate_b, "pscale": columns(x["pool_scale_2"][0]),
        "b1": columns(x["mlp_b1_2"]), "b2": columns(x["mlp_b2_2"]), "ln_g": columns(x["ln_g_2"]),
        "ln_b": columns(x["ln_b_2"]), "sink": np.broadcast_to(x["attn_sink"], (P, 8)),
        "c": np.stack([columns(x["c"][0]), columns(x["c_ctx"])], axis=2).reshape(P, 16),
    }
    a["vecs"] = np.concatenate([vec[name] for name in _VEC], axis=1)
    a["consts"] = shape_constants()
    return {name: np.ascontiguousarray(v) for name, v in a.items()}


def kernel(**inputs):
    import concourse.bacc as bacc
    from concourse.bass_utils import run_bass_kernel_spmd

    arrays = layout({name: np.asarray(v) for name, v in inputs.items()})
    nc = bacc.Bacc("TRN2", target_bir_lowering=False, num_devices=1, dynamic_dma_scratch_size=1024)
    aps = {name: nc.dram_tensor(f"in_{name}", v.shape, mybir.dt.from_np(v.dtype), kind="ExternalInput").ap()
           for name, v in arrays.items()}
    out = nc.dram_tensor("outT", (D, T), F32, kind="ExternalOutput").ap()
    build(nc, aps, out)
    r = run_bass_kernel_spmd(nc, [{f"in_{name}": v for name, v in arrays.items()}], core_ids=[0])
    return np.ascontiguousarray(r.results[0]["outT"].T)[None]
```
